# Optimizing a Trainium2 kernel written in Bass

```python
import math
import jax, jax.numpy as jnp
from jax import lax
import numpy as np

D_MODEL = 1024
BATCH = 1
SEQ = 128
DEPTH = 2
DEC_BATCH = 1
DEC_SEQ = 128
PAST_LEN = 128

GRID_W = 64
EPS = 1e-6
MIN_GATE = 1e-30
ROPE_BASE = 10000.0
Q_BLOCK = 128
H_DA = 8
DA_QK = 32
DA_V = 64
H_RET = 4
RET_DK = 64
RET_DV = 64
RET_CHUNK = 64
H_HG = 4
HG_DK = 64
HG_DV = 64
HG_CHUNK = 16
D_DA_QK = H_DA * 2 * DA_QK
D_DA_V = H_DA * DA_V
D_RET_QK = H_RET * RET_DK
D_RET_V = H_RET * RET_DV
D_HG_K = H_HG * HG_DK
D_HG_V = H_HG * HG_DV
IN_SPLITS = (D_DA_QK, D_DA_QK, D_DA_V,
             D_RET_QK, D_RET_QK, D_RET_V, D_RET_V,
             D_HG_K, D_HG_K, D_HG_K, D_HG_V, D_HG_V)
D_IN = 2 * D_DA_QK + D_DA_V + 2 * D_RET_QK + 2 * D_RET_V + 3 * D_HG_K + 2 * D_HG_V
D_MIX = D_DA_V + D_RET_V + D_HG_V
N_EXPERTS = 16
N_GROUPS = 4
EXPERTS_PER_GROUP = 4
TOP_K = 2
D_EXPERT = 512
MASKED_SCORE = -2.0

kernel_name = "hybrid_diffusion_prefix_step"

def rmsnorm(x, w):
    xf = x.astype(jnp.float32)
    y = xf * lax.rsqrt(jnp.mean(xf * xf, axis=-1, keepdims=True) + EPS)
    return (y * w.astype(jnp.float32)).astype(x.dtype)

def _split_columns(h):
    parts, start = [], 0
    for size in IN_SPLITS:
        parts.append(h[..., start:start + size])
        start += size
    return parts

def rope_tables(n_tokens):
    rows = n_tokens // GRID_W
    pos_r = jnp.repeat(jnp.arange(rows, dtype=jnp.float32), GRID_W)
    pos_c = jnp.tile(jnp.arange(GRID_W, dtype=jnp.float32), rows)
    n_freq = DA_QK // 4
    inv = ROPE_BASE ** (-jnp.arange(n_freq, dtype=jnp.float32) / n_freq)
    ang = jnp.concatenate([pos_r[:, None] * inv, pos_c[:, None] * inv], axis=-1)
    return jnp.cos(ang), jnp.sin(ang)

def apply_rope(x, cos, sin):
    xp = x.reshape(*x.shape[:-1], DA_QK // 2, 2)
    x1, x2 = xp[..., 0], xp[..., 1]
    c = cos[None, :, None, None, :].astype(x.dtype)
    s = sin[None, :, None, None, :].astype(x.dtype)
    return jnp.stack([x1 * c - x2 * s, x1 * s + x2 * c], axis=-1).reshape(x.shape)

def diff_attention(q, k, v, lam):
    B, Lq = q.shape[0], q.shape[1]
    nb = Lq // Q_BLOCK
    qb = q.reshape(B, nb, Q_BLOCK, *q.shape[2:]).swapaxes(0, 1)
    scale = DA_QK ** -0.5

    def block(qblk):
        s = jnp.einsum('bqhrd,bkhrd->brhqk', qblk, k, preferred_element_type=jnp.float32) * scale
        p = jax.nn.softmax(s, axis=-1)
        w = (p[:, 0] - lam * p[:, 1]).astype(v.dtype)
        return jnp.einsum('bhqk,bkhd->bqhd', w, v)

    out = lax.map(block, qb)
    return out.swapaxes(0, 1).reshape(B, Lq, *v.shape[2:])

def chunk_recurrence(q, k, v, log_a, s0, chunk):
    f32 = jnp.float32
    B, H, L, _ = q.shape
    n = L // chunk
    rs = lambda t: t.astype(f32).reshape(B, H, n, chunk, t.shape[-1])
    q, k, v, la = rs(q), rs(k), rs(v), rs(log_a)
    b = jnp.cumsum(la, axis=-2)
    b_end = b[..., -1:, :]
    mask = jnp.tril(jnp.ones((chunk, chunk), dtype=bool))[:, :, None]
    diff = b[..., :, None, :] - b[..., None, :, :]
    decay = jnp.where(mask, jnp.exp(jnp.minimum(diff, 0.0)), 0.0)
    if la.shape[-1] == 1:
        scores = jnp.einsum('bhncd,bhnsd->bhncs', q, k) * decay[..., 0]
    else:
        scores = jnp.einsum('bhncd,bhnsd,bhncsd->bhncs', q, k, decay)
    o_intra = jnp.einsum('bhncs,bhnse->bhnce', scores, v)
    kv = jnp.einsum('bhncd,bhnce->bhnde', k * jnp.exp(b_end - b), v)
    a_chunk = jnp.exp(b_end[..., 0, :])

    def step(S, inp):
        a_c, kv_c = inp
        return a_c[..., :, None] * S + kv_c, S

    s_fin, s_prev = lax.scan(step, s0.astype(f32),
                             (jnp.moveaxis(a_chunk, 2, 0), jnp.moveaxis(kv, 2, 0)))
    s_prev = jnp.moveaxis(s_prev, 0, 2)
    o_inter = jnp.einsum('bhncd,bhnde->bhnce', q * jnp.exp(b), s_prev)
    return (o_intra + o_inter).reshape(B, H, L, v.shape[-1]), s_fin

def bidir_recurrence(q, k_f, k_b, v, la_f, la_b, s0_f, s0_b, chunk):
    flip = lambda t: jnp.flip(t, axis=2)
    o_f, s_f = chunk_recurrence(q, k_f, v, la_f, s0_f, chunk)
    o_b, s_b = chunk_recurrence(flip(q), flip(k_b), flip(v), flip(la_b), s0_b, chunk)
    return o_f + flip(o_b), s_f, s_b

def token_mixers(hn, l, p, ctx):
    f32 = jnp.float32
    B, L, _ = hn.shape
    proj = jnp.einsum('bld,de->ble', hn, p['w_in'][l])
    (da_q, da_k, da_v, r_q, r_k, r_v, r_g, g_q, g_ff, g_fb, g_i, g_g) = _split_columns(proj)

    lam_init = 0.8 - 0.6 * math.exp(-0.3 * l)
    lp = p['da_lambda'][l].astype(f32)
    lam = jnp.exp(jnp.sum(lp[0] * lp[1])) - jnp.exp(jnp.sum(lp[2] * lp[3])) + lam_init
    q = rmsnorm(da_q.reshape(B, L, H_DA, 2, DA_QK), p['da_qnorm'][l])
    k = rmsnorm(da_k.reshape(B, L, H_DA, 2, DA_QK), p['da_knorm'][l])
    v = da_v.reshape(B, L, H_DA, DA_V)
    if ctx is None:
        o_da = diff_attention(q, k, v, lam)
        s_ret0 = jnp.zeros((B, 2, H_RET, RET_DK, RET_DV), f32)
        s_hg0 = jnp.zeros((B, 2, H_HG, HG_DK, HG_DV), f32)
    else:
        ctx_k, ctx_v, s_ret0, s_hg0 = ctx
        cos, sin = rope_tables(L)
        q = apply_rope(q, cos, sin)
        k_lat = apply_rope(k, cos, sin)
        o_da = diff_attention(q, jnp.concatenate([k_lat, ctx_k.astype(k_lat.dtype)], axis=1),
                              jnp.concatenate([v, ctx_v.astype(v.dtype)], axis=1), lam)
    o_da = rmsnorm(o_da, p['da_subln'][l]) * (1.0 - lam_init)

    to_heads = lambda t, h, d: t.reshape(B, L, h, d).transpose(0, 2, 1, 3)

    rq = to_heads(r_q, H_RET, RET_DK)
    rk = to_heads(r_k, H_RET, RET_DK) * (RET_DK ** -0.5)
    rv = to_heads(r_v, H_RET, RET_DV)
    log_gamma = -jnp.exp(p['ret_decay'][l].astype(f32))
    la = lambda g: jnp.broadcast_to(g[None, :, None, None], (B, H_RET, L, 1))
    o_ret, sr_f, sr_b = bidir_recurrence(rq, rk, rk, rv, la(log_gamma[0]), la(log_gamma[1]),
                                         s_ret0[:, 0], s_ret0[:, 1], RET_CHUNK)
    o_ret = o_ret.transpose(0, 2, 1, 3).astype(hn.dtype)
    o_ret = rmsnorm(o_ret, p['ret_norm'][l]) * jax.nn.silu(r_g.reshape(B, L, H_RET, RET_DV))

    p_lb = jax.nn.softmax(p['hg_lb'].astype(f32), axis=0)
    lb = (jnp.cumsum(p_lb, axis=0) - p_lb[0])[l].reshape(H_HG, 1, HG_DK)
    hq = to_heads(jax.nn.silu(g_q), H_HG, HG_DK)
    zf = to_heads(g_ff, H_HG, HG_DK).astype(f32)
    zb = to_heads(g_fb, H_HG, HG_DK).astype(f32)
    log_f = lambda z: jnp.log(jnp.maximum(lb + (1.0 - lb) * jax.nn.sigmoid(z), MIN_GATE))
    one_minus_f = lambda z: (1.0 - lb) * jax.nn.sigmoid(-z)
    hv = to_heads(g_i, H_HG, HG_DV)
    o_hg, sh_f, sh_b = bidir_recurrence(hq, one_minus_f(zf), one_minus_f(zb), hv, log_f(zf), log_f(zb),
                                        s_hg0[:, 0], s_hg0[:, 1], HG_CHUNK)
    o_hg = o_hg.transpose(0, 2, 1, 3).astype(hn.dtype)
    o_hg = rmsnorm(o_hg, p['hg_norm'][l]) * jax.nn.silu(g_g.reshape(B, L, H_HG, HG_DV))

    mixed = jnp.concatenate([o_da.reshape(B, L, D_DA_V), o_ret.reshape(B, L, D_RET_V),
                             o_hg.reshape(B, L, D_HG_V)], axis=-1)
    out = jnp.einsum('blm,md->bld', mixed, p['w_out'][l])
    if ctx is None:
        return out, (k, v, jnp.stack([sr_f, sr_b], axis=1), jnp.stack([sh_f, sh_b], axis=1))
    return out, None

def moe(h, l, p):
    f32 = jnp.float32
    B, L, _ = h.shape
    scores = jax.nn.sigmoid(jnp.einsum('bld,de->ble', h, p['w_router'], preferred_element_type=f32))
    sel = scores + p['router_bias'].astype(f32)
    group_score = jnp.sum(lax.top_k(sel.reshape(B, L, N_GROUPS, EXPERTS_PER_GROUP), TOP_K)[0], axis=-1)
    best_group = jnp.argmax(group_score, axis=-1)
    in_group = best_group[..., None] == jnp.arange(N_GROUPS)
    masked = jnp.where(jnp.repeat(in_group, EXPERTS_PER_GROUP, axis=-1), sel, MASKED_SCORE)
    _, idx = lax.top_k(masked, TOP_K)
    w = jnp.take_along_axis(scores, idx, axis=-1)
    w = w / jnp.sum(w, axis=-1, keepdims=True)
    gate = jnp.sum(jax.nn.one_hot(idx, N_EXPERTS, dtype=f32) * w[..., None], axis=-2)
    hg = jnp.einsum('bld,edf->blef', h, p['w_gate'][l])
    hu = jnp.einsum('bld,edf->blef', h, p['w_up'][l])
    act = jax.nn.silu(hg) * hu
    return jnp.einsum('blef,ble,efd->bld', act, gate.astype(act.dtype), p['w_down'][l])

def layer(x, cond, l, p, ctx):
    mod = jnp.einsum('...d,de->...e', jax.nn.silu(cond), p['w_ada'][l]) + p['b_ada'][l]
    mod = mod.reshape(-1, 1, 6 * D_MODEL)
    sh1, sc1, g1, sh2, sc2, g2 = jnp.split(mod, 6, axis=-1)
    hn = rmsnorm(x, p['norm_mix'][l]) * (1.0 + sc1) + sh1
    mix, ctx_tensors = token_mixers(hn, l, p, ctx)
    x = x + g1 * mix
    hn = rmsnorm(x, p['norm_ffn'][l]) * (1.0 + sc2) + sh2
    x = x + g2 * moe(hn, l, p)
    return x, ctx_tensors

def setup_inputs(seed: int = 0) -> dict:
    key = jax.random.key(seed)
    ks = jax.random.split(key, 32)
    nrm = lambda k, shape, s=1.0: s * jax.random.normal(k, shape, jnp.float32)
    ret_base = -(5.0 + jnp.arange(H_RET, dtype=jnp.float32)) * math.log(2.0)
    return {
        "x_prompt": nrm(ks[0], (BATCH, SEQ, D_MODEL)),
        "x_sample": nrm(ks[1], (DEC_BATCH, DEC_SEQ, D_MODEL)),
        "cache_k": nrm(ks[2], (DEC_BATCH, DEPTH, PAST_LEN, H_DA, 2, DA_QK)),
        "cache_v": nrm(ks[3], (DEC_BATCH, DEPTH, PAST_LEN, H_DA, DA_V)),
        "state_ret": nrm(ks[4], (DEC_BATCH, DEPTH, 2, H_RET, RET_DK, RET_DV), 0.5),
        "state_hgrn": nrm(ks[5], (DEC_BATCH, DEPTH, 2, H_HG, HG_DK, HG_DV), 0.5),
        "c": nrm(ks[6], (DEC_BATCH, D_MODEL)),
        "c_ctx": nrm(ks[7], (D_MODEL,)),
        "w_in": nrm(ks[8], (DEPTH, D_MODEL, D_IN), D_MODEL ** -0.5),
        "w_out": nrm(ks[9], (DEPTH, D_MIX, D_MODEL), D_MIX ** -0.5),
        "w_ada": nrm(ks[10], (DEPTH, D_MODEL, 6 * D_MODEL), 0.5 * D_MODEL ** -0.5),
        "b_ada": nrm(ks[11], (DEPTH, 6 * D_MODEL), 0.01),
        "norm_mix": 1.0 + nrm(ks[12], (DEPTH, D_MODEL), 0.01),
        "norm_ffn": 1.0 + nrm(ks[13], (DEPTH, D_MODEL), 0.01),
        "da_qnorm": 1.0 + nrm(ks[14], (DEPTH, DA_QK), 0.01),
        "da_knorm": 1.0 + nrm(ks[15], (DEPTH, DA_QK), 0.01),
        "da_lambda": nrm(ks[16], (DEPTH, 4, DA_QK), 0.1),
        "da_subln": 1.0 + nrm(ks[17], (DEPTH, DA_V), 0.01),
        "ret_decay": ret_base + nrm(ks[18], (DEPTH, 2, H_RET), 0.1),
        "ret_norm": 1.0 + nrm(ks[19], (DEPTH, RET_DV), 0.01),
        "hg_lb": nrm(ks[20], (DEPTH, D_HG_K), 0.1),
        "hg_norm": 1.0 + nrm(ks[21], (DEPTH, HG_DV), 0.01),
        "w_router": nrm(ks[22], (D_MODEL, N_EXPERTS), D_MODEL ** -0.5),
        "router_bias": nrm(ks[23], (N_EXPERTS,), 0.01),
        "w_gate": nrm(ks[24], (DEPTH, N_EXPERTS, D_MODEL, D_EXPERT), D_MODEL ** -0.5),
        "w_up": nrm(ks[25], (DEPTH, N_EXPERTS, D_MODEL, D_EXPERT), D_MODEL ** -0.5),
        "w_down": nrm(ks[26], (DEPTH, N_EXPERTS, D_EXPERT, D_MODEL), D_EXPERT ** -0.5),
    }

def reference(x_prompt, x_sample, cache_k, cache_v, state_ret, state_hgrn, c, c_ctx,
              w_in, w_out, w_ada, b_ada, norm_mix, norm_ffn, da_qnorm, da_knorm, da_lambda,
              da_subln, ret_decay, ret_norm, hg_lb, hg_norm, w_router, router_bias,
              w_gate, w_up, w_down):
    p = dict(w_in=w_in, w_out=w_out, w_ada=w_ada, b_ada=b_ada, norm_mix=norm_mix,
             norm_ffn=norm_ffn, da_qnorm=da_qnorm, da_knorm=da_knorm, da_lambda=da_lambda,
             da_subln=da_subln, ret_decay=ret_decay, ret_norm=ret_norm, hg_lb=hg_lb,
             hg_norm=hg_norm, w_router=w_router, router_bias=router_bias,
             w_gate=w_gate, w_up=w_up, w_down=w_down)

    x = x_prompt
    ks_, vs_, srs_, shs_ = [], [], [], []
    for l in range(DEPTH):
        x, (k_l, v_l, sr_l, sh_l) = layer(x, c_ctx, l, p, None)
        ks_.append(k_l)
        vs_.append(v_l)
        srs_.append(sr_l)
        shs_.append(sh_l)
    y_prompt = x
    new_cache_k = jnp.stack(ks_, axis=1)
    new_cache_v = jnp.stack(vs_, axis=1)
    new_state_ret = jnp.stack(srs_, axis=1)
    new_state_hgrn = jnp.stack(shs_, axis=1)

    x = x_sample
    for l in range(DEPTH):
        x, _ = layer(x, c, l, p, (cache_k[:, l], cache_v[:, l], state_ret[:, l], state_hgrn[:, l]))
    y_sample = x

    return (y_prompt, y_sample, new_cache_k, new_cache_v, new_state_ret, new_state_hgrn)


_drawn_inputs = setup_inputs


def setup_inputs(seed=0):
    import zlib

    import numpy as np

    out = dict(_drawn_inputs(seed))
    spreads = {}
    factors = {'state_hgrn': 4.72,
     'norm_mix': 2.701,
     'da_qnorm': 4.52,
     'da_knorm': 14.134,
     'da_subln': 32.592,
     'ret_norm': 31.296,
     'hg_norm': 26.56,
     'cache_k': 8.0,
     'norm_ffn': 4.935,
     'router_bias': 3.422}
    for name, (base, spread) in spreads.items():
        noise = np.random.default_rng([zlib.crc32(name.encode()), seed]).standard_normal(out[name].shape)
        drawn = base * np.exp(spread * noise) if base else spread * noise
        out[name] = __import__('jax').numpy.asarray(drawn.astype(out[name].dtype))
    for name, factor in factors.items():
        out[name] = (out[name] * factor).astype(out[name].dtype)
    return out
```

```python
import math
from contextlib import ExitStack

import numpy as np
import concourse.bass as bass
from concourse import mybir
from concourse.alu_op_type import AluOpType as ALU

P = 128
D = 1024
KC = D // P
L = 2
NG = 2
D_IN = 3840
NH, DQ, DV = 8, 32, 64
HR, DR = 4, 64
NE, DE = 16, 512
KE = DE // P
EPS = 1e-6
C_DAQ, C_DAK, C_DAV = 0, 512, 1024
C_RQ, C_RK, C_RV, C_RG = 1536, 1792, 2048, 2304
C_GQ, C_GFF, C_GFB, C_GI, C_GG = 2560, 2816, 3072, 3328, 3584
LEVELS = (64, 32, 16, 8, 4, 2, 1)
NLV = len(LEVELS)
RING = 6
KH = KC // 2
BLK = 512
N_IN = (D_IN + BLK - 1) // BLK
LN_LOW = 2.0 ** -60
GRID_W = 64


def host_constants():
    t = np.arange(P)
    c = {}
    c["ident"] = np.eye(P)
    masks = []
    for b in LEVELS:
        pair = (t[:, None] // (2 * b)) == (t[None, :] // (2 * b))
        fwd = pair & (t[:, None] // b % 2 == 0) & (t[None, :] // b % 2 == 1)
        masks += [fwd, fwd.T]
    c["masks"] = np.stack(masks, 1).reshape(P, -1)
    steps = []
    for b in LEVELS:
        fwd, bwd = np.zeros((P, P)), np.zeros((P, P))
        for i in t:
            base = i - i % (2 * b)
            mid, end = base + b, base + 2 * b
            if i >= mid:
                fwd[mid:i + 1, i] = 1
                bwd[mid:i, i] = 1
            else:
                fwd[i + 1:mid, i] = 1
                bwd[i:mid, i] = 1
        steps += [fwd, bwd]
    u, i = t[:, None], t[None, :]
    steps += [u <= i, u >= i]
    steps += [u > i, u < i]
    c["steps"] = np.stack(steps, 1).reshape(P, -1)
    c["dist"] = np.stack([np.maximum(i - u, 0), np.maximum(u - i, 0)], 1).reshape(P, -1)
    c["inpos"] = np.where(u < 64, i + 1, P - i) * np.ones((P, P))
    c["endpos"] = np.stack([P - 1 - t, t], 1)
    c["quarter"] = (t[:, None] // DQ == np.arange(4)[None, :])
    c["pick"] = np.stack([((u % 32 == g) | (u == NG)) * np.ones((P, P)) for g in range(NG)], 1).reshape(P, -1)
    c["pick2"] = (t[:, None] % 32 == np.arange(NG)[None, :]) | (t[:, None] == NG)
    rows = P // GRID_W
    inv = 10000.0 ** (-np.arange(DQ // 4) / (DQ // 4))
    ang = np.concatenate([np.repeat(np.arange(rows), GRID_W)[:, None] * inv, np.tile(np.arange(GRID_W), rows)[:, None] * inv], -1)
    c["cos"] = np.repeat(np.cos(ang), 2, axis=1)
    sn = np.sin(ang)
    c["sin"] = np.stack([-sn, sn], -1).reshape(P, DQ)
    c["rank4"] = np.tile(np.arange(4, 0, -1)[None], (P, 1))
    c["rank16"] = np.tile(np.arange(NE, 0, -1)[None], (P, 1))
    li = [0.8 - 0.6 * math.exp(-0.3 * l) for l in range(L)]
    c["lami"] = np.tile(np.array([[a, 1.0 - a] for a in li]).reshape(1, -1), (P, 1))
    return {k: np.ascontiguousarray(v, dtype=np.float32) for k, v in c.items()}


class Ledger:

    def __init__(self, known):
        self.totals, self.labels = known or ({}, {})
        self.count, self.found, self.where = {}, {}, "start"

    def made(self, sem, label=None, n=1):
        key = (sem, self.where)
        self.count[key] = self.count.get(key, 0) + n
        if label is not None:
            self.found[label] = (sem, self.where, self.count[key])
        return self.where, self.count[key]

    def value(self, sem, where, n, layer, turn):
        t = {w: self.totals.get((sem, w), 0) for w in ("start", "layer", "turn", "after")}
        if where == "start":
            return n
        v = n + t["start"]
        per_layer = t["layer"] + TURNS * t["turn"] + t["after"]
        if per_layer:
            v = layer * per_layer + v
        if where == "turn":
            v = v + t["layer"]
            if t["turn"]:
                v = turn * t["turn"] + v
        if where == "after":
            v = v + t["layer"] + TURNS * t["turn"]
        return v


TURNS = NE


class Counts:

    def __init__(self, led, sem):
        self.led, self.sem, self.l, self.t = led, sem, 0, 0
        self.last = None

    def value(self, sem, where, n):
        return self.led.value(sem, where, n, self.l, self.t)

    def of(self, *label):
        if label not in self.led.labels:
            self.led.found.setdefault("missing", set()).add(label)
        return self.sem(self.led.labels.get(label, ("none",))[0])

    def at(self, *label):
        sem, where, n = self.led.labels.get(label, ("none", "start", 1))
        return self.value(sem, where, n)

    def makes(self, *label):
        self.last = (label[0], *self.led.made(label[0], label))
        return self.sem(label[0])

    def last_value(self):
        return self.value(*self.last)

    def claim(self, b):
        where, n = self.led.made(f"bank{b}_claim")
        t = self.led.totals
        for w in ("layer", "turn", "after"):
            t[(f"bank{b}_free", w)] = t.get((f"bank{b}_full", w), 0)
        return self.value(f"bank{b}_free", where, n - 1)

    def fills(self, b, *label):
        self.led.made(f"bank{b}_full", label)
        return self.sem(f"bank{b}_full")

    def freed(self, read, *label):
        sem, where, n = self.led.labels.get(read, ("bank0_full", "start", 1))
        sem = sem.replace("_full", "_free")
        if label:
            self.led.found[label] = (sem, where, n)
        self.last = (sem, where, n)
        return self.sem(sem)

    def bank(self, *read):
        return int(self.led.labels.get(read, ("bank0_full",))[0][4])

    def loads(self, s):
        where, n = self.led.made(f"slot{s}_turn")
        t = self.led.totals
        for w in ("start", "layer", "turn", "after"):
            t[(f"slot{s}_loaded", w)] = 16 * t.get((f"slot{s}_turn", w), 0)
        return self.value(f"slot{s}_loaded", where, 16 * n)


def build(nc, io, known):
    f32 = mybir.dt.float32
    AF = mybir.ActivationFunctionType
    AX = mybir.AxisListType.X
    led = Ledger(known)
    ap = io["ap"]
    v = nc.vector
    with ExitStack() as ctx:
        sems = {}

        def S(name):
            if name not in sems:
                sems[name] = ctx.enter_context(nc.semaphore(name))
            return sems[name]

        def sb(name, *shape):
            return ctx.enter_context(nc.sbuf_tensor(name, [P, *shape], f32))

        ps = ctx.enter_context(nc.psum_tensor("ps", [P, 8, BLK], f32))

        ring = sb("ring", RING, KH, BLK)
        x = sb("x", NG, D)
        proj = sb("proj", NG, D_IN)
        xs = sb("xs", NG, D)
        hnT = sb("hnT", KC, NG * P)
        gateR = sb("gateR", 2, D)
        modT = sb("modT", 4, KC, NG)
        C = {n: sb("c_" + n, a.shape[1]) for n, a in io["consts"].items()}
        condT, silT, sile = sb("condT", NG, KC), sb("silT", KC, 32), sb("sile", NG, KC)
        lbt, lb, oml = sb("lbt", L, 256), sb("lb", 256), sb("oml", 256)
        epsc = sb("epsc", 1)
        nrmT = sb("nrmT", 2, KC)
        wqk, lamp = sb("wqk", 2, DQ), sb("lamp", 4, DQ)
        subln, rnorm, hnorm = sb("subln", DV), sb("rnorm", DR), sb("hnorm", DR)
        rdec, rdecH = sb("rdec", 2 * HR), sb("rdecH", HR)
        ctxk, ctxv = sb("ctxk", BLK), sb("ctxv", BLK)
        s0r, s0h = sb("s0r", HR, DR), sb("s0h", HR, DR)
        wrt, rbias = sb("wrt", KC, NE), sb("rbias", NE)
        lam, lams = sb("lam", 8), sb("lams", 2)
        decT, decin, decend = sb("decT", HR, P), sb("decin", HR, P), sb("decend", HR, 2)
        stat = sb("stat", NG, 64)
        sq, t1, t2, t3, t4 = sb("sq", D), sb("t1", D), sb("t2", BLK), sb("t3", BLK), sb("t4", BLK)
        oT = sq[:, BLK:D].rearrange("p (m t) -> p m t", t=P)
        qw, kT = sb("qw", 4, 4 * P), sb("kT", 4, 2, P)
        qTm = qw[:].rearrange("p j (m t) -> p j m t", m=4)
        wT = qw[:].rearrange("p (hh u) (v t) -> p hh (u v) t", hh=2, t=P).rearrange("p hh (hd part) t -> p hh hd part t", part=2)
        rqT, rkT, rqi = (qw[:, i].rearrange("p (h t) -> p h t", h=HR) for i in range(3))
        hqT, hkT, hqi = rqT, rkT, rqi
        rA = qw[:, 3].rearrange("p (h t) -> p h t", h=HR)
        la = qw[:, 3].rearrange("p (r h d) -> p r h d", r=2, h=HR)
        kf = kT[:].rearrange("p m r t -> p (m r t)")
        rq2, rk2 = (kf[:, i * BLK:(i + 1) * BLK].rearrange("p (h r d) -> p h r d", h=HR, r=2) for i in range(2))
        hq2, hk = rq2, rk2
        eP = sb("eP", 2, 8, 2 * P)
        ef = eP[:].rearrange("p a b c -> p (a b c)")
        A = ef[:, 0:4 * BLK].rearrange("p (z r h t) -> p z r h t", z=2, r=2, h=HR)
        lbin = ef[:, 0:BLK].rearrange("p (l n) -> p l n", l=L)
        gbuf1 = ef[:, 0:NG * D].rearrange("p (g n) -> p g n", g=NG)
        wP = hnT[:].rearrange("p k t -> p (k t)").rearrange("p (hh hd t) -> p hh hd t", hh=2, hd=4)
        rkd = sb("rkd", HR, 2, DR)
        hkd = rkd
        qlv, klv = sb("qlv", 2, HR, P), sb("klv", 2, HR, P)
        ex = sb("ex", 2, HR, P)
        stout = sb("stout", 2, HR, DR)
        gt = sb("gt", NG, NE)
        rt = sb("rt", 14, NG, NE)
        pf = proj[:].rearrange("p g n -> p (g n)")
        modR = pf[:, 0:4 * D]
        ge, gs, act, actT = (pf[:, i * 2 * BLK:(i + 1) * 2 * BLK].rearrange("p (g f) -> p g f", g=NG) for i in range(4))
        gbuf2 = pf[:, 4 * D:6 * D].rearrange("p (g n) -> p g n", g=NG)
        zero = t2

        w_in = ap["w_in"].rearrange("l (p k) n -> p l k n", k=KC)
        w_ada = ap["w_ada"].rearrange("l (p k) n -> p l k n", k=KC)
        w_out = ap["w_out"].rearrange("l (p k) n -> p l k n", k=KC)
        w_gate = ap["w_gate"].rearrange("l e (p k) f -> p (l e) k f", k=KC)
        w_up = ap["w_up"].rearrange("l e (p k) f -> p (l e) k f", k=KC)
        w_down = ap["w_down"].rearrange("l e (p k) d -> p (l e) (k d)", k=KE)

        block = ctx.enter_context(nc.Block())

        def one(i):
            return bass.ds(i, 1)

        @block.sync
        def _(sp):
            c = Counts(led, S)
            led.where = "start"
            n_loads = [0]
            for s in range(RING):
                sp.sem_inc(c.makes(f"slot{s}_used"), 1)

            def load(dst_cols, src):
                s = n_loads[0] % RING
                n_loads[0] += 1
                where, n = led.made(f"slot{s}_load")
                t = led.totals
                for w in ("layer", "turn", "after"):
                    t[(f"slot{s}_used", w)] = t.get((f"slot{s}_load", w), 0)
                sp.wait_ge(S(f"slot{s}_used"), c.value(f"slot{s}_used", where, n - 1))
                sp.dma_start(dst_cols(s), src).then_inc(S(f"slot{s}_loaded"), 16)

            with sp.Fori(0, L) as l:
                c.l = l
                led.where = "layer"
                for i in range(12):
                    for r in range(2):
                        load(lambda s: ring[:, s:s + 1], w_ada[:, one(l), KH * r:KH * (r + 1), i * BLK:(i + 1) * BLK])
                for i in range(N_IN):
                    n = min(BLK, D_IN - i * BLK)
                    for r in range(2):
                        load(lambda s: ring[:, s:s + 1, :, 0:n], w_in[:, one(l), KH * r:KH * (r + 1), i * BLK:i * BLK + n])
                for i in range(4):
                    for r in range(2):
                        load(lambda s: ring[:, s:s + 1, :, 0:256], w_out[:, one(l), KH * r:KH * (r + 1), i * 256:(i + 1) * 256])
                with sp.Fori(0, TURNS) as t:
                    c.t = t
                    led.where = "turn"
                    e = l * NE + t
                    for w in (w_gate, w_up):
                        for r in range(2):
                            load(lambda s: ring[:, s:s + 1], w[:, one(e), KH * r:KH * (r + 1)])
                    for r in range(2):
                        load(lambda s: ring[:, s:s + 1].rearrange("p s k n -> p s (k n)"), w_down[:, one(e), 2 * D * r:2 * D * (r + 1)])
                led.where = "after"

        @block.tensor
        def _(pe):
            c = Counts(led, S)
            led.where = "start"
            n_slots, n_tr, owed = [0], [0], []

            def mm(*a, **k):
                ins = nc.tensor.matmul(*a, **k)
                return ins

            def pay(ins):
                if owed:
                    ins.then_inc(S(f"slot{owed.pop(0)}_used"), 1)
                return ins

            def slot():
                s = n_slots[0] % RING
                n_slots[0] += 1
                pe.wait_ge(S(f"slot{s}_loaded"), c.loads(s))
                return s

            def sweep(out, lhs, rhs, n, free_group=False):
                for k in range(n):
                    last = mm(out, lhs(k), rhs(k), start=(k == 0), stop=(k == n - 1), skip_group_check=free_group)
                    if k < n - 1:
                        pay(last)
                return last

            def bank_of_transposes(label, sources, b=None):
                if b is None:
                    b = n_tr[0] % 2
                    n_tr[0] += 1
                pe.wait_ge(S(f"bank{b}_free"), c.claim(b))
                for i, src in enumerate(sources):
                    last = nc.tensor.transpose(ps[:, b, i * P:(i + 1) * P], src, C["ident"][:])
                    if i < len(sources) - 1:
                        pay(last)
                last.then_inc(c.fills(b, *label), 1)

            def by_feature(stage, rows):
                for g in range(NG):
                    pe.wait_ge(c.of(rows, g), c.at(rows, g))
                    xv = xs[:, g].rearrange("p (q k) -> p k q", k=KC)
                    for h in range(2):
                        bank_of_transposes((stage + "T", g, h), [xv[:, 4 * h + k, :] for k in range(4)])
                for g in range(NG):
                    for h in range(2):
                        pe.wait_ge(c.of(stage + "S", g, h), c.at(stage + "S", g, h))

            for b in range(8):
                pe.sem_inc(c.makes(f"bank{b}_free"), 1)
            pe.wait_ge(c.of("start_dma"), c.at("start_dma"))
            pe.wait_ge(c.of("silT"), c.at("silT"))
            with pe.Fori(0, L) as l:
                c.l = l
                led.where = "layer"
                for i in range(12):
                    b = 4 + i % 4
                    pe.wait_ge(S(f"bank{b}_free"), c.claim(b))
                    for r in range(2):
                        s = slot()
                        for j in range(4):
                            last = mm(ps[32 * j:32 * j + 32, b, :], silT[:, KH * r + j, :], ring[:, s, j, :], start=(r == 0), stop=(r == 1))
                            if not (r and j == 3):
                                pay(last)
                        owed.append(s)
                    last.then_inc(c.fills(b, "mod", i), 1)
                pe.wait_ge(c.of("bias"), c.at("bias"))
                pe.wait_ge(S(f"bank{0}_free"), c.claim(0))
                for a in range(4):
                    mv = modR[:, a * D:(a + 1) * D].rearrange("p (q k) -> p k q", k=KC)
                    for k in range(KC):
                        at = (a * KC + k) * NG
                        last = mm(ps[:, 0, at:at + NG], mv[:, k, :], C["pick2"][:], start=True, stop=True)
                        if k < 7:
                            pay(last)
                last.then_inc(c.fills(0, "modT"), 1)

                def spread_gate(a):
                    for g in range(NG):
                        for h in range(2):
                            b = 2 * g + h
                            pe.wait_ge(S(f"bank{b}_free"), c.claim(b))
                            last = mm(ps[:, b, :], C["pick"][:, g * P:(g + 1) * P], gateR[:, a, h * BLK:(h + 1) * BLK], start=True, stop=True)
                            last.then_inc(c.fills(b, "gateP", a, g, h), 1)

                by_feature("hn1", "xn1")
                nb = 0
                for i in range(N_IN):
                    ss = [slot(), slot()]
                    n = min(BLK, D_IN - i * BLK)
                    for g in range(NG):
                        b = 2 + nb % 6
                        nb += 1
                        pe.wait_ge(S(f"bank{b}_free"), c.claim(b))
                        last = sweep(ps[:, b, 0:n], lambda k: hnT[:, k, g * P:(g + 1) * P], lambda k: ring[:, ss[k // KH], k % KH, 0:n], KC)
                        last.then_inc(c.fills(b, "projP", i, g), 1)
                    owed.extend(ss)

                pe.wait_ge(c.of("params"), c.at("params"))
                for g in range(NG):
                    nk = 1 + g
                    pe.wait_ge(c.of("qkn", g), c.at("qkn", g))
                    bank_of_transposes(("daqT", g), [proj[:, g, C_DAQ + m * P:C_DAQ + (m + 1) * P] for m in range(4)])
                    bank_of_transposes(("dakT", g), [proj[:, g, C_DAK + m * P:C_DAK + (m + 1) * P] for m in range(4)])
                    if g:
                        bank_of_transposes(("ctxkT", g), [ctxk[:, m * P:(m + 1) * P] for m in range(4)])
                    pe.wait_ge(c.of("qTm", g), c.at("qTm", g))
                    pe.wait_ge(c.of("kT", g), c.at("kT", g))
                    if g:
                        pe.wait_ge(c.of("kTc", g), c.at("kTc", g))
                    for hh in range(2):
                        for j in range(4):
                            pe.wait_ge(S(f"bank{4 + j}_free"), c.claim(4 + j))
                            for mi in range(2):
                                m = 2 * hh + mi
                                last = mm(ps[:, 4 + j, mi * nk * P:(mi + 1) * nk * P], qTm[:, j, m, :], kT[:, m, 0:nk, :].rearrange("p a t -> p (a t)"), start=True, stop=True)
                            last.then_inc(c.fills(4 + j, "score", g, hh, j), 1)
                    for hh in range(2):
                        pe.wait_ge(c.of("wP", g, hh), c.at("wP", g, hh))
                        for part in range(nk):
                            bank_of_transposes(("wPT", g, hh, part), [wP[:, hh, hd, part * P:(part + 1) * P] for hd in range(4)])
                        if hh == 0:
                            pe.wait_ge(S(f"bank{2}_free"), c.claim(2))
                        for part in range(nk):
                            pe.wait_ge(c.of("wT", g, hh, part), c.at("wT", g, hh, part))
                        for hd in range(4):
                            h = 4 * hh + hd
                            dst = ps[64 * (h % 2):64 * (h % 2) + 64, 2, (h // 2) * P:(h // 2 + 1) * P]
                            for part in range(nk):
                                val = ctxv[:, h * DV:(h + 1) * DV] if part else proj[:, g, C_DAV + h * DV:C_DAV + (h + 1) * DV]
                                last = mm(dst, val, wT[:, hh, hd, part, :], start=(part == 0), stop=(part == nk - 1), skip_group_check=True)
                    last.then_inc(c.fills(2, "daoT", g), 1)
                    pe.wait_ge(c.of("daoTs", g), c.at("daoTs", g))
                    bank_of_transposes(("dao", g), [oT[:, m, :] for m in range(4)], 3)

                    pe.wait_ge(c.of("rk2", g), c.at("rk2", g))
                    bank_of_transposes(("rqT", g), [rq2[:, h].rearrange("p r d -> p (r d)") for h in range(HR)])
                    bank_of_transposes(("rkT", g), [rk2[:, h].rearrange("p r d -> p (r d)") for h in range(HR)])
                    pe.wait_ge(c.of("rqTs", g), c.at("rqTs", g))
                    pe.wait_ge(c.of("rkTs", g), c.at("rkTs", g))
                    pe.wait_ge(S(f"bank{2}_free"), c.claim(2))
                    for h in range(HR):
                        last = mm(ps[:, 2, h * P:(h + 1) * P], rkT[:, h, :], rqT[:, h, :], start=True, stop=True)
                    last.then_inc(c.fills(2, "rS", g), 1)
                    pe.wait_ge(c.of("rA", g), c.at("rA", g))
                    if g:
                        pe.wait_ge(c.of("rqi", g), c.at("rqi", g))
                    pe.wait_ge(S(f"bank{3}_free"), c.claim(3))
                    for h in range(HR):
                        dst = ps[64 * (h % 2):64 * (h % 2) + 64, 3, (h // 2) * P:(h // 2 + 1) * P]
                        last = mm(dst, proj[:, g, C_RV + h * DR:C_RV + (h + 1) * DR], rA[:, h, :], start=True, stop=not g, skip_group_check=True)
                        if g:
                            last = mm(dst, s0r[:, h, :], rqi[:, h, :], start=False, stop=True, skip_group_check=True)
                    last.then_inc(c.fills(3, "roT", g), 1)
                    pe.wait_ge(c.of("roTs", g), c.at("roTs", g))
                    bank_of_transposes(("ro", g), [oT[:, m, :] for m in range(2)], 2)
                    if not g:
                        pe.wait_ge(c.of("rkd", g), c.at("rkd", g))
                        pe.wait_ge(S(f"bank{3}_free"), c.claim(3))
                        for h in range(HR):
                            last = mm(ps[:, 3, h * DR:(h + 1) * DR], rkd[:, h].rearrange("p r d -> p (r d)"), proj[:, g, C_RV + h * DR:C_RV + (h + 1) * DR], start=True, stop=True)
                        last.then_inc(c.fills(3, "rstate", g), 1)

                    pe.wait_ge(c.of("hk", g), c.at("hk", g))
                    pe.wait_ge(c.of("hq2", g), c.at("hq2", g))
                    bank_of_transposes(("hqT", g), [hq2[:, h].rearrange("p r d -> p (r d)") for h in range(HR)])
                    bank_of_transposes(("hkT", g), [hk[:, h].rearrange("p r d -> p (r d)") for h in range(HR)])
                    pe.wait_ge(c.of("la", g), c.at("la", g))
                    def decays(lv):
                        b = 4 + lv % 2
                        pe.wait_ge(S(f"bank{b}_free"), c.claim(b))
                        for h in range(HR):
                            for d in range(2):
                                last = mm(ps[64 * d:64 * d + 64, b, h * P:(h + 1) * P], la[:, d, h, :], C["steps"][:, (2 * lv + d) * P:(2 * lv + d + 1) * P], start=True, stop=True)
                        last.then_inc(c.fills(b, "level", g, lv), 1)
                    decays(0)
                    decays(1)
                    if not g:
                        pe.wait_ge(S(f"bank{6}_free"), c.claim(6))
                        for d in range(2):
                            at = (2 * (NLV + 1) + d) * P
                            last = mm(ps[:, 6, d * 256:(d + 1) * 256], C["steps"][:, at:at + P], la[:, d].rearrange("p h d -> p (h d)"), start=True, stop=True)
                        last.then_inc(c.fills(6, "toend", g), 1)
                    pe.wait_ge(c.of("hqTs", g), c.at("hqTs", g))
                    pe.wait_ge(c.of("hkTs", g), c.at("hkTs", g))
                    def scores(lv):
                        if lv >= 0:
                            pe.wait_ge(c.of("klv", g, lv), c.at("klv", g, lv))
                            pe.wait_ge(c.of("qlv", g, lv), c.at("qlv", g, lv))
                        for r in range(2 if lv >= 0 else 1):
                            pe.wait_ge(S(f"bank{2 + r}_free"), c.claim(2 + r))
                            q = slice(64 * r, 64 * r + 64)
                            for h in range(HR):
                                k_, q_ = (klv[q, lv % 2, h, :], qlv[q, lv % 2, h, :]) if lv >= 0 else (hkT[:, h, :], hqT[:, h, :])
                                last = mm(ps[:, 2 + r, h * P:(h + 1) * P], k_, q_, start=True, stop=True)
                            last.then_inc(c.fills(2 + r, "hS", g, lv, r), 1)

                    def head(h):
                        return ps[64 * (h % 2):64 * (h % 2) + 64, 7, (h // 2) * P:(h // 2 + 1) * P]

                    def values(lv):
                        for r in range(2 if lv >= 0 else 1):
                            pe.wait_ge(c.of("hA", g, lv, r), c.at("hA", g, lv, r))
                            for h in range(HR):
                                end = not g and lv == NLV - 1 and r == 1
                                last = mm(head(h), proj[:, g, C_GI + h * DR:C_GI + (h + 1) * DR], A[:, lv % 2, r, h, :], start=(lv < 0 and h < 2), stop=end, skip_group_check=True)
                        if lv < NLV - 1:
                            last.then_inc(c.makes("hV", g, lv), 1)
                        return last

                    scores(-1)
                    scores(0)
                    decays(2)
                    pe.wait_ge(S(f"bank{7}_free"), c.claim(7))
                    for lv in range(-1, NLV):
                        last = values(lv)
                        if lv + 2 < NLV:
                            scores(lv + 2)
                        if lv + 4 < NLV + g:
                            decays(lv + 4)
                    if g:
                        pe.wait_ge(c.of("hqi", g), c.at("hqi", g))
                        for h in range(HR):
                            last = mm(head(h), s0h[:, h, :], hqi[:, h, :], start=False, stop=True, skip_group_check=True)
                    last.then_inc(c.fills(7, "hoT", g), 1)
                    pe.wait_ge(c.of("hoTs", g), c.at("hoTs", g))
                    bank_of_transposes(("ho", g), [oT[:, m, :] for m in range(2)], 2)
                    if not g:
                        pe.wait_ge(c.of("hkd", g), c.at("hkd", g))
                        pe.wait_ge(S(f"bank{3}_free"), c.claim(3))
                        for h in range(HR):
                            last = mm(ps[:, 3, h * DR:(h + 1) * DR], hkd[:, h].rearrange("p r d -> p (r d)"), proj[:, g, C_GI + h * DR:C_GI + (h + 1) * DR], start=True, stop=True)
                        last.then_inc(c.fills(3, "hstate", g), 1)

                by_feature("mix", "mixed")
                spread_gate(0)
                for n in range(4):
                    ss = [slot(), slot()]
                    for g in range(NG):
                        b = 4 + 2 * (n % 2) + g
                        pe.wait_ge(S(f"bank{b}_free"), c.claim(b))
                        last = sweep(ps[:, b, 0:256], lambda k: hnT[:, k, g * P:(g + 1) * P], lambda k: ring[:, ss[k // KH], k % KH, 0:256], KC)
                        last.then_inc(c.fills(b, "out", n, g), 1)
                    owed.extend(ss)

                by_feature("hn2", "xn2")
                pe.wait_ge(S(f"bank{2}_free"), c.claim(2))
                for g in range(NG):
                    last = sweep(ps[:, 2, g * NE:(g + 1) * NE], lambda k: hnT[:, k, g * P:(g + 1) * P], lambda k: wrt[:, k, :], KC)
                last.then_inc(c.fills(2, "router"), 1)

                pe.wait_ge(c.of("zeroed"), c.at("zeroed"))
                for b in range(4, 8):
                    pe.wait_ge(S(f"bank{b}_free"), c.claim(b))
                    mm(ps[:, b, :], zero[:, 0:P], zero[:, 0:BLK], start=True, stop=False, skip_group_check=True)
                with pe.Fori(0, TURNS) as t:
                    c.t = t
                    led.where = "turn"
                    gate_up = [[slot(), slot()], [slot(), slot()]]
                    for g in range(NG):
                        for i, ss in enumerate(gate_up):
                            b = 2 * g + i
                            pe.wait_ge(S(f"bank{b}_free"), c.claim(b))
                            last = sweep(ps[:, b, :], lambda k: hnT[:, k, g * P:(g + 1) * P], lambda k: ring[:, ss[k // KH], k % KH, :], KC)
                            last.then_inc(c.fills(b, "gu", g, i), 1)
                            if g:
                                owed.extend(ss)
                    sd = [slot(), slot()]
                    down = lambda k, h: ring[:, sd[k // 2]].rearrange("p k n -> p (k n)")[:, (k % 2) * D + h * BLK:(k % 2) * D + (h + 1) * BLK]
                    for g in range(NG):
                        pe.wait_ge(c.of("act", g), c.at("act", g))
                        bank_of_transposes(("actT", g), [act[:, g].rearrange("p (q k) -> p k q", k=KE)[:, k, :] for k in range(KE)], 2 * g)
                        pe.wait_ge(c.of("actTs", g), c.at("actTs", g))
                        for k in range(KE):
                            for h in range(2):
                                last = mm(ps[:, 4 + 2 * g + h, :], actT[:, g, k * P:(k + 1) * P], down(k, h), start=False, stop=False, skip_group_check=True)
                                if g and h and k % 2:
                                    last.then_inc(S(f"slot{sd[k // 2]}_used"), 1)
                                else:
                                    pay(last)
                led.where = "after"
                for b in range(4, 8):
                    last = mm(ps[:, b, :], zero[:, 0:P], zero[:, 0:BLK], start=False, stop=True, skip_group_check=True)
                    last.then_inc(c.fills(b, "y", b - 4), 1)
                spread_gate(1)
            assert not owed

        @block.vector
        def _(dve):
            c = Counts(led, S)
            led.where = "start"
            tt, ts, stt = v.tensor_tensor, v.tensor_scalar, v.scalar_tensor_tensor

            def st(ins, *label):
                ins.then_inc(c.makes(*(label or ("dve_step",))), 1)
                dve.wait_ge(S(c.last[0]), c.last_value())

            def red(out, in_, op=ALU.add):
                return v.tensor_reduce(out=out, in_=in_, axis=AX, op=op)

            def cols(a, g, n, h=HR):
                return proj[:, g, a:a + n].rearrange("p (h d) -> p h d", h=h)

            st(v.memset(epsc[:], EPS))
            st(v.memset(silT[:].rearrange("p k n -> p (k n)"), 0.0))
            led.found[("eps",)] = ("dve_step", "start", 1)
            dve.wait_ge(c.of("start_dma"), c.at("start_dma"))
            dve.wait_ge(c.of("sile"), c.at("sile"))
            st(ts(t1[:, 0:16], sile[:].rearrange("p g k -> p (g k)"), 1.0, None, ALU.add))
            st(v.reciprocal(t1[:, 16:32], t1[:, 0:16]))
            st(tt(silT[:, :, 0:NG].rearrange("p k g -> p g k"), condT[:], t1[:, 16:32].rearrange("p (g k) -> p g k", k=KC), ALU.mult), "silT", 0)
            led.found[("silT",)] = led.found[("silT", 0)]
            st(tt(t1[:, 0:256], lbin[:, 0], lbin[:, 1], ALU.max))
            for l_ in range(L):
                st(tt(lbt[:, l_], lbin[:, l_], t1[:, 0:256], ALU.subtract), "lbd", l_)
            dve.wait_ge(c.of("lbe"), c.at("lbe"))
            st(tt(t1[:, 0:256], lbin[:, 0], lbin[:, 1], ALU.add))
            st(v.reciprocal(t1[:, 256:512], t1[:, 0:256]))
            for l_ in range(L):
                st(tt(lbin[:, l_], lbin[:, l_], t1[:, 256:512], ALU.mult))
            st(tt(t1[:, 0:256], lbin[:, 0], lbin[:, 1], ALU.add))
            st(tt(lbt[:, 0], lbin[:, 0], lbin[:, 0], ALU.subtract))
            st(tt(lbt[:, 1], t1[:, 0:256], lbin[:, 0], ALU.subtract))

            with dve.Fori(0, L) as l:
                c.l = l
                led.where = "layer"
                dve.wait_ge(c.of("params"), c.at("params"))
                st(v.tensor_copy(lb[:], lbt[:, one(l)].rearrange("p l n -> p (l n)")))
                st(ts(oml[:], lb[:], -1.0, 1.0, ALU.mult, ALU.add))
                st(v.tensor_copy(lams[:], C["lami"][:, bass.ds(l * 2, 2)]))
                st(tt(t1[:, 0:32], lamp[:, 0], lamp[:, 1], ALU.mult))
                st(tt(t1[:, 32:64], lamp[:, 2], lamp[:, 3], ALU.mult))
                st(red(lam[:, 0:2], t1[:, 0:64].rearrange("p (a b) -> p a b", a=2)), "lamsum", 0)
                dve.wait_ge(c.of("lamexp"), c.at("lamexp"))
                st(tt(lam[:, 4:5], lam[:, 2:3], lam[:, 3:4], ALU.subtract))
                st(tt(lam[:, 5:6], lam[:, 4:5], lams[:, 0:1], ALU.add))
                st(ts(lam[:, 6:7], lam[:, 5:6], -1.0, None, ALU.mult))
                st(ts(subln[:], subln[:], lams[:, 1:2], None, ALU.mult))
                dve.wait_ge(c.of("rdec"), c.at("rdec"))
                st(ts(rdec[:], rdec[:], -1.0, None, ALU.mult))
                st(ts(rdecH[:], rdecH[:], -1.0, None, ALU.mult), "rdecn", 0)
                dve.wait_ge(c.of("decT"), c.at("decT"))
                tb = t1[:, 0:BLK].rearrange("p (h t) -> p h t", h=HR)
                for d, half in enumerate((decT[:], tb)):
                    st(tt(half, half, C["steps"][:, (2 * NLV + d) * P:(2 * NLV + d + 1) * P].rearrange("p (o t) -> p o t", o=1).broadcast_to([P, HR, P]), ALU.mult))
                st(tt(decT[:], decT[:], tb, ALU.add), "decS", 0)

                dve.wait_ge(c.of("modT"), c.at("modT"))
                v.tensor_copy(modT[:].rearrange("p a k g -> p (a k g)"), ps[:, 0, 0:64]).then_inc(c.freed(("modT",)), 1)
                dve.wait_ge(S(c.last[0]), c.last_value())
                for a in range(2):
                    st(stt(out=modT[:, 2 * a + 1], in0=modT[:, 2 * a + 1], scalar=1.0, in1=nrmT[:, a].rearrange("p (k o) -> p k o", o=1).broadcast_to([P, KC, NG]), op0=ALU.add, op1=ALU.mult), "modS", a)

                def normed(stage):
                    for g in range(NG):
                        dve.wait_ge(c.of(stage + "r", g), c.at(stage + "r", g))
                        st(ts(xs[:, g], x[:, g], stat[:, g, 2:3], None, ALU.mult), stage, g)

                def shifted(stage, a):
                    for h in range(2):
                        dve.wait_ge(c.of(stage + "T", 0, h), c.at(stage + "T", 0, h))
                        b = c.bank(stage + "T", 0, h)
                        for k in range(4):
                            kc = 4 * h + k
                            ins = ts(hnT[:, kc, 0:P], ps[:, b, k * P:(k + 1) * P], modT[:, 2 * a + 1, kc, 0:1], modT[:, 2 * a, kc, 0:1], ALU.mult, ALU.add)
                        ins.then_inc(c.freed((stage + "T", 0, h), stage + "S", 0, h), 1)
                        dve.wait_ge(S(c.last[0]), c.last_value())

                normed("xn1")
                shifted("hn1", 0)
                nb = 0
                for i in range(N_IN):
                    n = min(BLK, D_IN - i * BLK)
                    dve.wait_ge(c.of("projP", i, 0), c.at("projP", i, 0))
                    b = 2 + nb % 6
                    nb += 2
                    v.tensor_copy(proj[:, 0, i * BLK:i * BLK + n], ps[:, b, 0:n]).then_inc(c.freed(("projP", i, 0), "projS", i, 0), 1)
                    dve.wait_ge(S(c.last[0]), c.last_value())

                def group_norm(read, b, n, w, g, base, src_label):
                    m = n * 64
                    dve.wait_ge(c.of(src_label + "q", g), c.at(src_label + "q", g))
                    st(red(stat[:, g, 16:16 + n], sq[:, 0:m].rearrange("p (h d) -> p h d", h=n)), src_label + "m", g)
                    dve.wait_ge(c.of(src_label + "r", g), c.at(src_label + "r", g))
                    out = xs[:, g, base:base + m].rearrange("p (h d) -> p h d", h=n)
                    tt(out, ps[:, b, 0:m].rearrange("p (h d) -> p h d", h=n), stat[:, g, 16:16 + n].rearrange("p (h o) -> p h o", o=1).broadcast_to([P, n, 64]), ALU.mult).then_inc(c.freed(read), 1)
                    dve.wait_ge(S(c.last[0]), c.last_value())
                    ins = tt(out, out, w[:].rearrange("p (o d) -> p o d", o=1).broadcast_to([P, n, 64]), ALU.mult)
                    return ins, out

                def swish(src, e_label, g, out, label):
                    dve.wait_ge(c.of(e_label, g), c.at(e_label, g))
                    st(ts(t4[:, 0:256], t4[:, 0:256], 1.0, None, ALU.add))
                    st(v.reciprocal(t4[:, 0:256], t4[:, 0:256]))
                    st(out(t4[:, 0:256].rearrange("p (h d) -> p h d", h=HR)), *label)

                for g in range(NG):
                    nk = 1 + g
                    for i in range(3):
                        dve.wait_ge(c.of("projS", i, g), c.at("projS", i, g))
                    both = proj[:, g, 0:D].rearrange("p (a d) -> p a d", d=DQ)
                    st(tt(sq[:], proj[:, g, 0:D], proj[:, g, 0:D], ALU.mult))
                    st(red(stat[:, g, 32:64], sq[:].rearrange("p (a d) -> p a d", d=DQ)), "qkm", g)
                    dve.wait_ge(c.of("qkr", g), c.at("qkr", g))
                    st(tt(both, both, stat[:, g, 32:64].rearrange("p (a o) -> p a o", o=1).broadcast_to([P, 32, DQ]), ALU.mult))
                    for r in range(2):
                        lab = ("qkn", g) if (not g and r) else ()
                        st(tt(both[:, 2 * NH * r:2 * NH * (r + 1)], both[:, 2 * NH * r:2 * NH * (r + 1)], wqk[:, r].rearrange("p (o d) -> p o d", o=1).broadcast_to([P, 2 * NH, DQ]), ALU.mult), *lab)
                    if g:
                        pairs = both.rearrange("p a (i z) -> p a i z", z=2)
                        cs = C["cos"][:].rearrange("p (o d) -> p o d", o=1).broadcast_to([P, 32, DQ])
                        sn = C["sin"][:].rearrange("p (o i z) -> p o i z", o=1, z=2).broadcast_to([P, 32, DQ // 2, 2])
                        rot = t1[:].rearrange("p (a i z) -> p a i z", i=DQ // 2, z=2)
                        for z in range(2):
                            st(tt(rot[:, :, :, z], pairs[:, :, :, 1 - z], sn[:, :, :, z], ALU.mult))
                        st(tt(both, both, cs, ALU.mult))
                        st(tt(both, both, t1[:].rearrange("p (a d) -> p a d", d=DQ), ALU.add), "qkn", g)
                    dve.wait_ge(c.of("daqT", g), c.at("daqT", g))
                    b = c.bank("daqT", g)
                    for j in range(4):
                        ins = ts(qTm[:, j], ps[:, b].rearrange("p (m t) -> p m t", m=4), C["quarter"][:, j:j + 1], None, ALU.mult)
                    ins.then_inc(c.freed(("daqT", g), "qTm", g), 1)
                    dve.wait_ge(S(c.last[0]), c.last_value())
                    sm = stat[:, g]
                    for hh in range(2):
                        for j in range(4):
                            dve.wait_ge(c.of("score", g, hh, j), c.at("score", g, hh, j))
                        mx = rt[:, 2 * hh, 0, 0:8].rearrange("p (m j) -> p j m", j=4)
                        st(red(mx, ps[:, 4:8, 0:2 * nk * P].rearrange("p j (m t) -> p j m t", m=2), ALU.max))
                        st(ts(rt[:, 2 * hh, 0, 8:16], rt[:, 2 * hh, 0, 0:8], -DQ ** -0.5, None, ALU.mult), "nmax", g, hh)
                    for hh in range(2):
                        dve.wait_ge(c.of("expd", g, hh), c.at("expd", g, hh))
                        rs = rt[:, 2 * hh + 1, 0]
                        st(v.reciprocal(rs[:, 8:16], rs[:, 0:8]))
                        rr = rs[:, 8:16].rearrange("p (a r) -> p r a", r=2)
                        st(ts(rr[:, 1], rr[:, 1], lam[:, 6:7], None, ALU.mult))
                        for hd in range(4):
                            i0 = 2 * hd
                            st(ts(t2[:, 0:nk * P], eP[:, hh, i0, 0:nk * P], rs[:, 8 + i0:9 + i0], None, ALU.mult))
                            lab = ("wP", g, hh) if hd == 3 else ()
                            st(stt(out=wP[:, hh, hd, 0:nk * P], in0=eP[:, hh, i0 + 1, 0:nk * P], scalar=rs[:, 9 + i0:10 + i0], in1=t2[:, 0:nk * P], op0=ALU.mult, op1=ALU.add), *lab)
                    for i in range(3, 5):
                        dve.wait_ge(c.of("projS", i, g), c.at("projS", i, g))
                    st(v.tensor_copy(rq2, cols(C_RQ, g, 256).rearrange("p h (o d) -> p h o d", o=1).broadcast_to([P, HR, 2, DR])))
                    st(ts(rk2, cols(C_RK, g, 256).rearrange("p h (o d) -> p h o d", o=1).broadcast_to([P, HR, 2, DR]), DR ** -0.5, None, ALU.mult), "rk2", g)
                    if not g:
                        dve.wait_ge(c.of("decend"), c.at("decend"))
                        st(tt(rkd[:], rk2, decend[:].rearrange("p h (r o) -> p h r o", o=1).broadcast_to([P, HR, 2, DR]), ALU.mult), "rkd", g)
                    dve.wait_ge(c.of("rkT", g), c.at("rkT", g))
                    b = c.bank("rkT", g)
                    ts(qw[:, 1], ps[:, b], 0.5, None, ALU.mult).then_inc(c.freed(("rkT", g), "rkTs", g), 1)
                    dve.wait_ge(S(c.last[0]), c.last_value())
                    ins, _ = group_norm(("dao", g), 3, NH, subln, g, 0, "dao")
                    st(ins)
                    if g:
                        dve.wait_ge(c.of("rqTs", g), c.at("rqTs", g))
                        dve.wait_ge(c.of("decin"), c.at("decin"))
                        st(tt(rqi, rqT, decin[:], ALU.mult), "rqi", g)
                    dve.wait_ge(c.of("rS", g), c.at("rS", g))
                    tt(rA, ps[:, 2].rearrange("p (h t) -> p h t", h=HR), decT[:], ALU.mult).then_inc(c.freed(("rS", g), "rA", g), 1)
                    dve.wait_ge(S(c.last[0]), c.last_value())
                    ins, out = group_norm(("ro", g), 2, HR, rnorm, g, 512, "ro")
                    st(ins)
                    swish(None, "rge", g, lambda r: tt(t4[:, 256:512].rearrange("p (h d) -> p h d", h=HR), cols(C_RG, g, 256), r, ALU.mult), ())
                    st(tt(out, out, t4[:, 256:512].rearrange("p (h d) -> p h d", h=HR), ALU.mult), "rgdone", g)

                    for i in range(5, N_IN):
                        dve.wait_ge(c.of("projS", i, g), c.at("projS", i, g))
                    if g:
                        dve.wait_ge(c.of("toend", 0), c.at("toend", 0))
                    zz = proj[:, g, C_GFF:C_GFF + BLK]
                    st(ts(t2[:], zz, -80.0, None, ALU.max), "zc", g)
                    dve.wait_ge(c.of("ze", g), c.at("ze", g))
                    st(ts(t3[:], t2[:], 1.0, None, ALU.add))
                    st(v.reciprocal(t3[:], t3[:]))
                    st(tt(t2[:], t2[:], t3[:], ALU.mult))
                    omlv = oml[:].rearrange("p (o h d) -> p o h d", o=1, h=HR).broadcast_to([P, 2, HR, DR])
                    lbv = lb[:].rearrange("p (o h d) -> p o h d", o=1, h=HR).broadcast_to([P, 2, HR, DR])
                    dhd = lambda a: a.rearrange("p (r h d) -> p r h d", r=2, h=HR)
                    st(tt(hk.rearrange("p h r d -> p r h d"), dhd(t2[:]), omlv, ALU.mult), "hk", g)
                    st(tt(dhd(t3[:]), dhd(t3[:]), omlv, ALU.mult))
                    st(tt(dhd(t3[:]), dhd(t3[:]), lbv, ALU.add))
                    st(ts(t3[:], t3[:], 1e-30, None, ALU.max))
                    st(ts(t2[:], t3[:], LN_LOW, 1.0 / LN_LOW, ALU.is_lt, ALU.mult))
                    st(stt(out=t3[:], in0=t2[:], scalar=1.0, in1=t3[:], op0=ALU.max, op1=ALU.mult), "gatef", g)
                    dve.wait_ge(c.of("gln", g), c.at("gln", g))
                    st(stt(out=qw[:, 3], in0=t2[:], scalar=LN_LOW * math.log(LN_LOW), in1=t3[:], op0=ALU.mult, op1=ALU.add), "la", g)
                    swish(None, "gqe", g, lambda r: tt(hq2, cols(C_GQ, g, 256).rearrange("p h (o d) -> p h o d", o=1).broadcast_to([P, HR, 2, DR]), r.rearrange("p h (o d) -> p h o d", o=1).broadcast_to([P, HR, 2, DR]), ALU.mult), ("hq2", g))
                    dve.wait_ge(c.of("hkT", g), c.at("hkT", g))
                    b = c.bank("hkT", g)
                    v.tensor_copy(qw[:, 1], ps[:, b]).then_inc(c.freed(("hkT", g), "hkTs", g), 1)
                    dve.wait_ge(S(c.last[0]), c.last_value())
                    dve.wait_ge(c.of("hqTs", g), c.at("hqTs", g))

                    def masked(lv):
                        if lv >= 1:
                            dve.wait_ge(c.of("hV", g, lv - 2), c.at("hV", g, lv - 2))
                        for r in range(2 if lv >= 0 else 1):
                            m = C["ident"][:] if lv < 0 else C["masks"][:, (2 * lv + r) * P:(2 * lv + r + 1) * P]
                            dve.wait_ge(c.of("hS", g, lv, r), c.at("hS", g, lv, r))
                            src = ps[:, 2 + r].rearrange("p (h t) -> p h t", h=HR)
                            tt(A[:, lv % 2, r], src, m.rearrange("p (o t) -> p o t", o=1).broadcast_to([P, HR, P]), ALU.mult).then_inc(c.freed(("hS", g, lv, r), "hA", g, lv, r), 1)
                            dve.wait_ge(S(c.last[0]), c.last_value())

                    def scaled_queries(lv):
                        dve.wait_ge(c.of("ex", g, lv), c.at("ex", g, lv))
                        st(tt(qlv[:, lv % 2], hqT, ex[:, lv % 2], ALU.mult), "qlv", g, lv)

                    scaled_queries(0)
                    for lv in range(-1, NLV):
                        if 0 <= lv < NLV - 1:
                            scaled_queries(lv + 1)
                        masked(lv)
                    if g:
                        dve.wait_ge(c.of("ex", g, NLV), c.at("ex", g, NLV))
                        st(tt(hqi, hqT, ex[:, NLV % 2], ALU.mult), "hqi", g)
                    else:
                        dve.wait_ge(c.of("exend", g), c.at("exend", g))
                        st(tt(hkd[:].rearrange("p h r d -> p r h d"), hk.rearrange("p h r d -> p r h d"), dhd(t3[:]), ALU.mult), "hkd", g)
                    ins, out = group_norm(("ho", g), 2, HR, hnorm, g, 768, "ho")
                    st(ins)
                    swish(None, "gge", g, lambda r: tt(t4[:, 256:512].rearrange("p (h d) -> p h d", h=HR), cols(C_GG, g, 256), r, ALU.mult), ())
                    st(tt(out, out, t4[:, 256:512].rearrange("p (h d) -> p h d", h=HR), ALU.mult), "mixed", g)

                for g in range(1):
                    for h in range(2):
                        dve.wait_ge(c.of("mixT", g, h), c.at("mixT", g, h))
                        b = c.bank("mixT", g, h)
                        v.tensor_copy(hnT[:, 4 * h:4 * h + 4, g * P:(g + 1) * P], ps[:, b].rearrange("p (k t) -> p k t", k=4)).then_inc(c.freed(("mixT", g, h), "mixS", g, h), 1)
                        dve.wait_ge(S(c.last[0]), c.last_value())
                for n in range(4):
                    for g in range(NG):
                        sl = slice(n * 256, (n + 1) * 256)
                        dve.wait_ge(c.of("gateS", 0, g, n // 2), c.at("gateS", 0, g, n // 2))
                        dve.wait_ge(c.of("out", n, g), c.at("out", n, g))
                        tt(t1[:, 0:256], ps[:, 4 + 2 * (n % 2) + g, 0:256], gbuf1[:, g, sl], ALU.mult).then_inc(c.freed(("out", n, g)), 1)
                        dve.wait_ge(S(c.last[0]), c.last_value())
                        lab = ("x1", g) if n == 3 else ()
                        st(tt(x[:, g, sl], x[:, g, sl], t1[:, 0:256], ALU.add), *lab)
                normed("xn2")
                shifted("hn2", 1)

                st(v.memset(zero[:], 0.0), "zeroed", 0)
                led.found[("zeroed",)] = led.found[("zeroed", 0)]

                G4 = lambda a: a.rearrange("p g (q e) -> p g q e", e=4)
                dve.wait_ge(c.of("rexp"), c.at("rexp"))
                sc, sel = rt[:, 1], rt[:, 2]
                st(ts(rt[:, 3], rt[:, 0], 1.0, None, ALU.add))
                st(v.reciprocal(sc, rt[:, 3]))
                st(tt(sel, sc, rbias[:].rearrange("p (o e) -> p o e", o=1).broadcast_to([P, NG, NE]), ALU.add))
                s4 = sel.rearrange("p g (q a z) -> p g q a z", a=2, z=2)
                hi = rt[:, 3, :, 0:8].rearrange("p g (q a) -> p g q a", a=2)
                lo = rt[:, 4, :, 0:8].rearrange("p g (q a) -> p g q a", a=2)
                st(tt(hi, s4[:, :, :, :, 0], s4[:, :, :, :, 1], ALU.max))
                st(tt(lo, s4[:, :, :, :, 0], s4[:, :, :, :, 1], ALU.min))
                st(tt(rt[:, 5, :, 0:4], hi[:, :, :, 0], hi[:, :, :, 1], ALU.max))
                st(tt(rt[:, 5, :, 4:8], hi[:, :, :, 0], hi[:, :, :, 1], ALU.min))
                st(tt(rt[:, 5, :, 8:12], lo[:, :, :, 0], lo[:, :, :, 1], ALU.max))
                st(tt(rt[:, 5, :, 4:8], rt[:, 5, :, 4:8], rt[:, 5, :, 8:12], ALU.max))
                st(tt(rt[:, 5, :, 0:4], rt[:, 5, :, 0:4], rt[:, 5, :, 4:8], ALU.add))

                def first_best(vals, rank, n, pick, tmp):
                    m = stat[:, 0, 0:NG]
                    bc = lambda a: a.rearrange("p (g o) -> p g o", o=1).broadcast_to([P, NG, n])
                    st(red(m, vals, ALU.max))
                    st(tt(tmp, vals, bc(m), ALU.is_equal))
                    st(tt(tmp, tmp, C[rank][:].rearrange("p (o e) -> p o e", o=1).broadcast_to([P, NG, n]), ALU.mult))
                    st(red(m, tmp, ALU.max))
                    st(tt(pick, tmp, bc(m), ALU.is_equal))

                first_best(rt[:, 5, :, 0:4], "rank4", 4, rt[:, 6, :, 0:4], rt[:, 7, :, 0:4])
                grp = rt[:, 6, :, 0:4].rearrange("p g (q o) -> p g q o", o=1).broadcast_to([P, NG, 4, 4])
                st(ts(rt[:, 8, :, 0:4], rt[:, 6, :, 0:4], 2.0, -2.0, ALU.mult, ALU.add))
                st(tt(G4(rt[:, 9]), G4(sel), grp, ALU.mult))
                st(tt(G4(rt[:, 9]), G4(rt[:, 9]), rt[:, 8, :, 0:4].rearrange("p g (q o) -> p g q o", o=1).broadcast_to([P, NG, 4, 4]), ALU.add))
                first_best(rt[:, 9], "rank16", NE, rt[:, 10], rt[:, 11])
                st(stt(out=rt[:, 9], in0=rt[:, 10], scalar=-1e30, in1=rt[:, 9], op0=ALU.mult, op1=ALU.add))
                first_best(rt[:, 9], "rank16", NE, rt[:, 12], rt[:, 11])
                st(tt(rt[:, 10], rt[:, 10], rt[:, 12], ALU.add))
                st(tt(rt[:, 10], rt[:, 10], sc, ALU.mult))
                st(red(stat[:, 0, 0:NG], rt[:, 10]))
                st(v.reciprocal(stat[:, 0, 2:4], stat[:, 0, 0:NG]))
                tt(gt[:], rt[:, 10], stat[:, 0, 2:4].rearrange("p (g o) -> p g o", o=1).broadcast_to([P, NG, NE]), ALU.mult).then_inc(c.makes("gt"), 1)

                with dve.Fori(0, TURNS) as t:
                    c.t = t
                    led.where = "turn"
                    for g in range(NG):
                        dve.wait_ge(c.of("gexp", g), c.at("gexp", g))
                        st(ts(ge[:, g], ge[:, g], 1.0, None, ALU.add))
                        st(v.reciprocal(ge[:, g], ge[:, g]))
                        tt(gs[:, g], ps[:, 2 * g], ge[:, g], ALU.mult).then_inc(c.freed(("gu", g, 0)), 1)
                        dve.wait_ge(S(c.last[0]), c.last_value())
                        dve.wait_ge(c.of("gt"), c.at("gt"))
                        dve.wait_ge(c.of("gu", g, 1), c.at("gu", g, 1))
                        stt(out=act[:, g], in0=ps[:, 2 * g + 1], scalar=gt[:, g, one(t)], in1=gs[:, g], op0=ALU.mult, op1=ALU.mult).then_inc(c.freed(("gu", g, 1), "act", g), 1)
                        dve.wait_ge(S(c.last[0]), c.last_value())
                led.where = "after"
                for g in range(NG):
                    for h in range(2):
                        sl = slice(h * BLK, (h + 1) * BLK)
                        dve.wait_ge(c.of("gateS", 1, g, h), c.at("gateS", 1, g, h))
                        dve.wait_ge(c.of("y", 2 * g + h), c.at("y", 2 * g + h))
                        tt(t1[:, 0:BLK], ps[:, 4 + 2 * g + h], gbuf2[:, g, sl], ALU.mult).then_inc(c.freed(("y", 2 * g + h)), 1)
                        dve.wait_ge(S(c.last[0]), c.last_value())
                        lab = ("x2", g) if h else ()
                        st(tt(x[:, g, sl], x[:, g, sl], t1[:, 0:BLK], ALU.add), *lab)

        @block.scalar
        def _(acte):
            c = Counts(led, S)
            led.where = "start"

            def st(ins, *label):
                ins.then_inc(c.makes(*(label or ("act_step",))), 1)
                acte.wait_ge(S(c.last[0]), c.last_value())

            act_ = nc.scalar.activation

            def ex_(out, in_, scale=1.0, **k):
                return act_(out, in_, AF.Exp, scale=scale, **k)

            def rstd(g, cols_, n, label):
                a = stat[:, g, cols_]
                st(act_(a, a, AF.Ln, bias=epsc[:, 0:1], scale=1.0 / n))
                st(ex_(a, a, -0.5), *label)

            def evac(read, out, *label, fn=None):
                acte.wait_ge(c.of(*read), c.at(*read))
                b = c.bank(*read)
                src = ps[:, b]
                (nc.scalar.copy(out, src) if fn is None else fn(src)).then_inc(c.freed(read, *label), 1)
                acte.wait_ge(S(c.last[0]), c.last_value())

            for name in ("stored", "bias", "mixed", "x2"):
                acte.sem_inc(c.makes(name), 1)
            acte.wait_ge(c.of("start_dma"), c.at("start_dma"))
            acte.wait_ge(c.of("eps"), c.at("eps"))
            st(ex_(sile[:].rearrange("p g k -> p (g k)"), condT[:].rearrange("p g k -> p (g k)"), -1.0), "sile", 0)
            led.found[("sile",)] = led.found[("sile", 0)]
            acte.wait_ge(c.of("lbd", L - 1), c.at("lbd", L - 1))
            for l_ in range(L):
                st(ex_(lbin[:, l_], lbt[:, l_]), "lbe", l_)
            led.found[("lbe",)] = led.found[("lbe", L - 1)]
            with acte.Fori(0, L) as l:
                c.l = l
                led.where = "layer"

                def squares(stage):
                    for g in range(NG):
                        if stage == "xn1":
                            acte.wait_ge(S("x2"), c.value("x2", "layer", 0))
                        else:
                            acte.wait_ge(c.of("x1", g), c.at("x1", g))
                        st(act_(sq[:], x[:, g], AF.Square, accum_out=stat[:, g, 2:3]))
                        rstd(g, slice(2, 3), D, (stage + "r", g))

                acte.wait_ge(S("mixed"), c.value("mixed", "layer", 0))
                row = lambda name: ap[name][one(l)].rearrange("l n -> (l n)")
                rb = lambda name, a, n: ap[name][one(l), a:a + n].broadcast_to([P, n])
                bT = lambda r: r.rearrange("l (p k) -> p (l k)", k=KC)
                loads = [(nrmT[:, 0], bT(ap["norm_mix"][one(l)])), (nrmT[:, 1], bT(ap["norm_ffn"][one(l)]))]
                loads += [(wqk[:, 0], rb("da_qnorm", 0, DQ)), (wqk[:, 1], rb("da_knorm", 0, DQ)),
                          (lamp[:].rearrange("p a d -> p (a d)"), ap["da_lambda"].rearrange("l a d -> l (a d)")[one(l)].broadcast_to([P, 4 * DQ])),
                          (subln[:], rb("da_subln", 0, DV)), (rnorm[:], rb("ret_norm", 0, DR)), (hnorm[:], rb("hg_norm", 0, DR)),
                          (ctxk[:], ap["cache_k"][0].rearrange("l t h r d -> t l (h r d)")[:, one(l)].rearrange("t l n -> t (l n)")),
                          (ctxv[:], ap["cache_v"][0].rearrange("l t h d -> t l (h d)")[:, one(l)].rearrange("t l n -> t (l n)"))]
                dec = ap["ret_decay"].rearrange("l r h -> l (r h)")
                loads += [(rdec[:], dec[one(l)].broadcast_to([P, 2 * HR]))]
                for d in range(2):
                    q = slice(64 * d, 64 * d + 64)
                    loads += [(rdecH[q], dec[one(l), d * HR:(d + 1) * HR].broadcast_to([64, HR])),
                              (s0r[q], ap["state_ret"][0].rearrange("l r h d e -> r d l h e")[d, :, one(l)].rearrange("d l h e -> d (l h) e")),
                              (s0h[q], ap["state_hgrn"][0].rearrange("l r h d e -> r d l h e")[d, :, one(l)].rearrange("d l h e -> d (l h) e"))]
                for dst, src in loads:
                    acte.dma_start(dst, src).then_inc(S("params"), 16)
                led.made("params", ("params",), 16 * len(loads))

                def store(dst, src):
                    acte.dma_start(dst, src).then_inc(S("stored"), 16)
                    led.made("stored", ("stored",), 16)

                acte.wait_ge(c.of("params"), c.at("params"))
                acte.wait_ge(c.of("lamsum", 0), c.at("lamsum", 0))
                st(ex_(lam[:, 2:4], lam[:, 0:2]), "lamexp", 0)
                led.found[("lamexp",)] = led.found[("lamexp", 0)]
                st(ex_(rdec[:], rdec[:]))
                st(ex_(rdecH[:], rdecH[:]), "rdec", 0)
                led.found[("rdec",)] = led.found[("rdec", 0)]
                acte.wait_ge(c.of("rdecn", 0), c.at("rdecn", 0))
                acte.wait_ge(S("x2"), c.value("x2", "layer", 0))
                for d in range(2):
                    for h in range(HR):
                        lab = ("decT", 0) if (d and h == HR - 1) else ()
                        st(ex_(t1[:, h * P:(h + 1) * P] if d else decT[:, h], C["dist"][:, d * P:(d + 1) * P], rdec[:, d * HR + h:d * HR + h + 1]), *lab)
                led.found[("decT",)] = led.found[("decT", 0)]
                for h in range(HR):
                    st(ex_(decin[:, h], C["inpos"][:], rdecH[:, h:h + 1]), "decin", h)
                led.found[("decin",)] = led.found[("decin", HR - 1)]
                for d in range(2):
                    st(ex_(decend[:, :, d], rdec[:, d * HR:(d + 1) * HR], C["endpos"][:, d:d + 1]), "decend", d)
                led.found[("decend",)] = led.found[("decend", 1)]
                squares("xn1")
                acte.wait_ge(S("stored"), c.value("stored", "layer", 0))
                acte.wait_ge(S("bias"), c.value("bias", "layer", 0))
                for i in range(12):
                    vec, h = divmod(i, 2)
                    to = gateR[:, vec // 3] if vec % 3 == 2 else modR[:, (vec - vec // 3) * D:(vec - vec // 3 + 1) * D]
                    evac(("mod", i), to[:, h * BLK:(h + 1) * BLK], "modR", i)
                for i in range(12):
                    acte.wait_ge(c.of("modR", i), c.at("modR", i))
                rows = [(modR[NG:NG + 1, a * D:(a + 1) * D], vec) for a, vec in enumerate((0, 1, 3, 4))] + [(gateR[NG:NG + 1, a], vec) for a, vec in enumerate((2, 5))]
                for dst, vec in rows:
                    acte.dma_start(dst, ap["b_ada"][one(l), vec * D:(vec + 1) * D]).then_inc(S("bias"), 16)
                led.made("bias", ("bias",), 16 * len(rows))


                def shifted(stage, a):
                    acte.wait_ge(c.of("modS", 1), c.at("modS", 1))
                    for h in range(2):
                        acte.wait_ge(c.of(stage + "T", 1, h), c.at(stage + "T", 1, h))
                        b = c.bank(stage + "T", 1, h)
                        for k in range(4):
                            kc = 4 * h + k
                            ins = act_(hnT[:, kc, P:2 * P], ps[:, b, k * P:(k + 1) * P], AF.Identity, bias=modT[:, 2 * a, kc, 1:2], scale=modT[:, 2 * a + 1, kc, 1:2])
                        ins.then_inc(c.freed((stage + "T", 1, h), stage + "S", 1, h), 1)
                        acte.wait_ge(S(c.last[0]), c.last_value())

                shifted("hn1", 0)
                for i in range(N_IN):
                    n = min(BLK, D_IN - i * BLK)
                    evac(("projP", i, 1), None, "projS", i, 1, fn=lambda src: nc.scalar.copy(proj[:, 1, i * BLK:i * BLK + n], src[:, 0:n]))

                def square_of(read, n, label, g):
                    acte.wait_ge(c.of(*read), c.at(*read))
                    b = c.bank(*read)
                    st(act_(sq[:, 0:n], ps[:, b, 0:n], AF.Square), label + "q", g)
                    acte.wait_ge(c.of(label + "m", g), c.at(label + "m", g))
                    rstd(g, slice(16, 16 + n // 64), 64, (label + "r", g))

                for g in range(NG):
                    nk = 1 + g
                    acte.wait_ge(c.of("qkm", g), c.at("qkm", g))
                    rstd(g, slice(32, 64), DQ, ("qkr", g))
                    if not g:
                        acte.wait_ge(c.of("qkn", 0), c.at("qkn", 0))
                        acte.wait_ge(c.of("projS", 2, 0), c.at("projS", 2, 0))
                        store(ap["o_k"][0].rearrange("l t h r d -> t l (h r d)")[:, one(l)].rearrange("t l n -> t (l n)"), proj[:, 0, C_DAK:C_DAK + BLK])
                        store(ap["o_v"][0].rearrange("l t h d -> t l (h d)")[:, one(l)].rearrange("t l n -> t (l n)"), proj[:, 0, C_DAV:C_DAV + BLK])
                    evac(("dakT", g), None, "kT", g, fn=lambda src: nc.scalar.copy(kT[:, :, 0, :], src.rearrange("p (m t) -> p m t", m=4)))
                    if g:
                        evac(("ctxkT", g), None, "kTc", g, fn=lambda src: nc.scalar.copy(kT[:, :, 1, :], src.rearrange("p (m t) -> p m t", m=4)))
                    for hh in range(2):
                        acte.wait_ge(c.of("nmax", g, hh), c.at("nmax", g, hh))
                        for j in range(4):
                            for mi in range(2):
                                i = mi * 4 + j
                                ins = ex_(eP[:, hh, i, 0:nk * P], ps[:, 4 + j, mi * nk * P:(mi + 1) * nk * P], DQ ** -0.5, bias=rt[:, 2 * hh, 0, 8 + i:9 + i], accum_out=rt[:, 2 * hh + 1, 0, i:i + 1])
                            if j < 3:
                                ins.then_inc(c.freed(("score", g, hh, j)), 1)
                                acte.wait_ge(S(c.last[0]), c.last_value())
                            else:
                                ins.then_inc(c.freed(("score", g, hh, j), "expd", g, hh), 1)
                                acte.wait_ge(S(c.last[0]), c.last_value())
                    for hh in range(2):
                        for part in range(nk):
                            evac(("wPT", g, hh, part), None, "wT", g, hh, part, fn=lambda src: nc.scalar.copy(wT[:, hh, :, part, :], src.rearrange("p (m t) -> p m t", m=4)))
                    evac(("daoT", g), sq[:, BLK:D], "daoTs", g)
                    square_of(("dao", g), 512, "dao", g)
                    evac(("rqT", g), qw[:, 0], "rqTs", g)
                    evac(("roT", g), None, "roTs", g, fn=lambda src: nc.scalar.copy(sq[:, BLK:BLK + 256], src[:, 0:256]))
                    square_of(("ro", g), 256, "ro", g)
                    st(ex_(t4[:, 0:256], proj[:, g, C_RG:C_RG + 256], -1.0), "rge", g)
                    if not g:
                        evac(("rstate", g), None, "rstateS", fn=lambda src: nc.scalar.copy(stout[:, 0].rearrange("p h e -> p (h e)"), src[:, 0:256]))
                        for d in range(2):
                            store(ap["o_ret"][0].rearrange("l r h d e -> r d l h e")[d, :, one(l)].rearrange("d l h e -> d (l h) e"), stout[64 * d:64 * d + 64, 0])
                    acte.wait_ge(c.of("zc", g), c.at("zc", g))
                    st(ex_(t2[:], t2[:], -1.0), "ze", g)
                    acte.wait_ge(c.of("gatef", g), c.at("gatef", g))
                    st(act_(t3[:], t3[:], AF.Ln), "gln", g)
                    acte.wait_ge(c.of("rgdone", g), c.at("rgdone", g))
                    st(ex_(t4[:, 0:256], proj[:, g, C_GQ:C_GQ + 256], -1.0), "gqe", g)
                    evac(("hqT", g), qw[:, 0], "hqTs", g)
                    for lv in range(NLV + g):
                        if lv >= 2:
                            acte.wait_ge(c.of("qlv", g, lv - 2), c.at("qlv", g, lv - 2))
                            acte.wait_ge(c.of("klv", g, lv - 2), c.at("klv", g, lv - 2))
                        evac(("level", g, lv), None, "ex", g, lv, fn=lambda src: ex_(ex[:, lv % 2].rearrange("p h t -> p (h t)"), src))
                    if not g:
                        evac(("toend", g), None, "exend", g, fn=lambda src: ex_(t3[:], src))
                    evac(("hoT", g), None, "hoTs", g, fn=lambda src: nc.scalar.copy(sq[:, BLK:BLK + 256], src[:, 0:256]))
                    square_of(("ho", g), 256, "ho", g)
                    st(ex_(t4[:, 0:256], proj[:, g, C_GG:C_GG + 256], -1.0), "gge", g)
                    if not g:
                        evac(("hstate", g), None, "hstateS", fn=lambda src: nc.scalar.copy(stout[:, 1].rearrange("p h e -> p (h e)"), src[:, 0:256]))
                        for d in range(2):
                            store(ap["o_hg"][0].rearrange("l r h d e -> r d l h e")[d, :, one(l)].rearrange("d l h e -> d (l h) e"), stout[64 * d:64 * d + 64, 1])
                for h in range(2):
                    evac(("mixT", 1, h), None, "mixS", 1, h, fn=lambda src: nc.scalar.copy(hnT[:, 4 * h:4 * h + 4, P:2 * P], src.rearrange("p (k t) -> p k t", k=4)))
                for g in range(NG):
                    for h in range(2):
                        evac(("gateP", 0, g, h), gbuf1[:, g, h * BLK:(h + 1) * BLK], "gateS", 0, g, h)
                squares("xn2")
                shifted("hn2", 1)
                evac(("router",), None, "rexp", fn=lambda src: ex_(rt[:, 0].rearrange("p g e -> p (g e)"), src[:, 0:NG * NE], -1.0))
                acte.wait_ge(c.of("stored"), c.at("stored"))
                with acte.Fori(0, TURNS) as t:
                    c.t = t
                    led.where = "turn"
                    for g in range(NG):
                        acte.wait_ge(c.of("gu", g, 0), c.at("gu", g, 0))
                        st(ex_(ge[:, g], ps[:, 2 * g], -1.0), "gexp", g)
                    for g in range(NG):
                        evac(("actT", g), actT[:, g], "actTs", g)
                led.where = "after"
                for g in range(NG):
                    for h in range(2):
                        evac(("gateP", 1, g, h), gbuf2[:, g, h * BLK:(h + 1) * BLK], "gateS", 1, g, h)
            led.where = "end"
            acte.wait_ge(S("x2"), 1 + NG * L)
            acte.dma_start(ap["o_yp"][0], x[:, 0]).then_inc(S("stored"), 16)
            acte.dma_start(ap["o_ys"][0], x[:, 1]).then_inc(S("stored"), 16)
            acte.wait_ge(S("stored"), 1 + L * led.totals.get(("stored", "layer"), 0) + 32)

        @block.gpsimd
        def _(pool):
            c = Counts(led, S)
            led.where = "start"
            g_ = nc.gpsimd
            bc = lambda a: a.rearrange("(o n) -> o n", o=1).broadcast_to([P, a.shape[0]])
            starts = [(x[:, 0], ap["x_prompt"][0]), (x[:, 1], ap["x_sample"][0])]
            starts += [(C[n][:], io["cap"][n]) for n in io["consts"]]
            starts += [(condT[:, 0], ap["c_ctx"].rearrange("(p k) -> p k", k=KC)),
                       (condT[:, 1], ap["c"][0].rearrange("(p k) -> p k", k=KC)),
                       (wrt[:], ap["w_router"].rearrange("(p k) e -> p k e", k=KC)),
                       (rbias[:], bc(ap["router_bias"]))]
            starts += [(lbin[:, l_], bc(ap["hg_lb"][l_])) for l_ in range(L)]
            for dst, src in starts:
                pool.dma_start(dst, src).then_inc(S("start_dma"), 16)
            led.made("start_dma", ("start_dma",), 16 * len(starts))
            with pool.Fori(0, L) as l:
                c.l = l
                led.where = "layer"
                def scaled_keys(g):
                    for lv in range(NLV):
                        pool.wait_ge(c.of("hkTs", g), c.at("hkTs", g))
                        pool.wait_ge(c.of("ex", g, lv), c.at("ex", g, lv))
                        if lv >= 2:
                            pool.wait_ge(c.of("hS", g, lv - 2, 1), c.at("hS", g, lv - 2, 1))
                        g_.tensor_tensor(klv[:, lv % 2], hkT, ex[:, lv % 2], ALU.mult).then_inc(c.makes("klv", g, lv), 1)
                        pool.wait_ge(S(c.last[0]), c.last_value())

                scaled_keys(0)
                scaled_keys(1)
                led.where = "after"
    return dict(led.count), dict(led.found)


_INS = ["x_prompt", "x_sample", "cache_k", "cache_v", "state_ret", "state_hgrn", "c", "c_ctx", "w_in", "w_out", "w_ada", "b_ada",
        "norm_mix", "norm_ffn", "da_qnorm", "da_knorm", "da_lambda", "da_subln", "ret_decay", "ret_norm", "hg_lb", "hg_norm",
        "w_router", "router_bias", "w_gate", "w_up", "w_down"]
_OUTS = [("o_yp", (1, P, D)), ("o_ys", (1, P, D)), ("o_k", (1, L, P, NH, 2, DQ)), ("o_v", (1, L, P, NH, DV)),
         ("o_ret", (1, L, 2, HR, DR, DR)), ("o_hg", (1, L, 2, HR, DR, DR))]


def kernel(**inputs):
    import concourse.bacc as bacc
    from concourse.bass_utils import run_bass_kernel_spmd

    arrays = {"in_" + n: np.ascontiguousarray(inputs[n]) for n in _INS}
    consts = host_constants()
    arrays.update({"const_" + n: a for n, a in consts.items()})
    known = None
    for _ in range(3):
        nc = bacc.Bacc("TRN2", target_bir_lowering=False, num_devices=1)
        dram = {n: nc.dram_tensor(n, a.shape, mybir.dt.from_np(a.dtype), kind="ExternalInput").ap() for n, a in arrays.items()}
        outs = {n: nc.dram_tensor("out_" + n, shape, mybir.dt.float32, kind="ExternalOutput").ap() for n, shape in _OUTS}
        aps = {n: dram["in_" + n] for n in _INS}
        aps.update(outs)
        io = {"ap": aps, "consts": consts, "cap": {n: dram["const_" + n] for n in consts}}
        known = build(nc, io, known)
    r = run_bass_kernel_spmd(nc, [arrays], core_ids=[0])
    return tuple(r.results[0]["out_" + n] for n, _ in _OUTS)
```

```python
import math
from contextlib import ExitStack

import numpy as np
import concourse.bass as bass
from concourse import mybir
from concourse.alu_op_type import AluOpType as ALU

P = 128
D = 1024
KC = D // P
L = 2
NG = 2
D_IN = 3840
NH, DQ, DV = 8, 32, 64
HR, DR = 4, 64
NE, DE = 16, 512
KE = DE // P
SLOTS = 64
EPS = 1e-6
C_DAQ, C_DAK, C_DAV = 0, 512, 1024
C_RQ, C_RK, C_RV, C_RG = 1536, 1792, 2048, 2304
C_GQ, C_GFF, C_GFB, C_GI, C_GG = 2560, 2816, 3072, 3328, 3584
LEVELS = (64, 32, 16, 8, 4, 2, 1)
NLV = len(LEVELS)
RING = 6
KH = KC // 2
BLK = 512
N_IN = (D_IN + BLK - 1) // BLK
FAR = 1024.0
LN_LOW = 2.0 ** -60
GRID_W = 64


def host_constants():
    t = np.arange(P)
    c = {}
    c["ident"] = np.eye(P)
    masks = []
    for b in LEVELS:
        pair = (t[:, None] // (2 * b)) == (t[None, :] // (2 * b))
        fwd = pair & (t[:, None] // b % 2 == 0) & (t[None, :] // b % 2 == 1)
        masks += [fwd, fwd.T]
    c["masks"] = np.stack(masks, 1).reshape(P, -1)
    steps = []
    for b in LEVELS:
        fwd, bwd = np.zeros((P, P)), np.zeros((P, P))
        for i in t:
            base = i - i % (2 * b)
            mid, end = base + b, base + 2 * b
            if i >= mid:
                fwd[mid:i + 1, i] = 1
                bwd[mid:i, i] = 1
            else:
                fwd[i + 1:mid, i] = 1
                bwd[i:mid, i] = 1
        steps += [fwd, bwd]
    u, i = t[:, None], t[None, :]
    steps += [u <= i, u >= i]
    steps += [u > i, u < i]
    c["steps"] = np.stack(steps, 1).reshape(P, -1)
    c["dist"] = np.stack([np.maximum(i - u, 0), np.maximum(u - i, 0)], 1).reshape(P, -1)
    c["inpos"] = np.where(u < 64, i + 1, P - i) * np.ones((P, P))
    c["endpos"] = np.stack([P - 1 - t, t], 1)
    c["quarter"] = (t[:, None] // DQ == np.arange(4)[None, :])
    c["pick"] = np.stack([((u % 32 == g) | (u == NG)) * np.ones((P, P)) for g in range(NG)], 1).reshape(P, -1)
    c["pick2"] = (t[:, None] % 32 == np.arange(NG)[None, :]) | (t[:, None] == NG)
    rows = P // GRID_W
    inv = 10000.0 ** (-np.arange(DQ // 4) / (DQ // 4))
    ang = np.concatenate([np.repeat(np.arange(rows), GRID_W)[:, None] * inv, np.tile(np.arange(GRID_W), rows)[:, None] * inv], -1)
    c["cos"] = np.repeat(np.cos(ang), 2, axis=1)
    sn = np.sin(ang)
    c["sin"] = np.stack([-sn, sn], -1).reshape(P, DQ)
    c["slot"] = np.tile(np.arange(SLOTS)[None], (P, 1))
    c["rank4"] = np.tile(np.arange(4, 0, -1)[None], (P, 1))
    c["rank16"] = np.tile(np.arange(NE, 0, -1)[None], (P, 1))
    li = [0.8 - 0.6 * math.exp(-0.3 * l) for l in range(L)]
    c["lami"] = np.tile(np.array([[a, 1.0 - a] for a in li]).reshape(1, -1), (P, 1))
    return {k: np.ascontiguousarray(v, dtype=np.float32) for k, v in c.items()}


class Ledger:

    def __init__(self, known):
        self.totals, self.labels = known or ({}, {})
        self.count, self.found, self.where = {}, {}, "start"

    def made(self, sem, label=None, n=1):
        key = (sem, self.where)
        self.count[key] = self.count.get(key, 0) + n
        if label is not None:
            self.found[label] = (sem, self.where, self.count[key])
        return self.where, self.count[key]

    def value(self, sem, where, n, layer, rounds, turn):
        t = {w: self.totals.get((sem, w), 0) for w in ("start", "layer", "turn", "after")}
        if where == "start":
            return n
        v = n + t["start"]
        if t["layer"] + t["after"]:
            v = layer * (t["layer"] + t["after"]) + v
        if where != "layer":
            v = v + t["layer"]
        if t["turn"]:
            v = (turn if where == "turn" else rounds * TURNS) * t["turn"] + v
        return v


TURNS = NE // 2


class Counts:

    def __init__(self, led, sem):
        self.led, self.sem, self.l, self.rounds, self.t = led, sem, 0, 0, 0
        self.last = None

    def value(self, sem, where, n):
        return self.led.value(sem, where, n, self.l, self.rounds, self.t)

    def of(self, *label):
        if label not in self.led.labels:
            self.led.found.setdefault("missing", set()).add(label)
        return self.sem(self.led.labels.get(label, ("none",))[0])

    def at(self, *label):
        sem, where, n = self.led.labels.get(label, ("none", "start", 1))
        return self.value(sem, where, n)

    def makes(self, *label):
        self.last = (label[0], *self.led.made(label[0], label))
        return self.sem(label[0])

    def last_value(self):
        return self.value(*self.last)

    def claim(self, b):
        where, n = self.led.made(f"bank{b}_claim")
        t = self.led.totals
        for w in ("layer", "turn", "after"):
            t[(f"bank{b}_free", w)] = t.get((f"bank{b}_full", w), 0)
        return self.value(f"bank{b}_free", where, n - 1)

    def fills(self, b, *label):
        self.led.made(f"bank{b}_full", label)
        return self.sem(f"bank{b}_full")

    def freed(self, read, *label):
        sem, where, n = self.led.labels.get(read, ("bank0_full", "start", 1))
        sem = sem.replace("_full", "_free")
        if label:
            self.led.found[label] = (sem, where, n)
        self.last = (sem, where, n)
        return self.sem(sem)

    def bank(self, *read):
        return int(self.led.labels.get(read, ("bank0_full",))[0][4])

    def loads(self, s):
        where, n = self.led.made(f"slot{s}_turn")
        t = self.led.totals
        for w in ("start", "layer", "turn", "after"):
            t[(f"slot{s}_loaded", w)] = 16 * t.get((f"slot{s}_turn", w), 0)
        return self.value(f"slot{s}_loaded", where, 16 * n)


def build(nc, io, known):
    f32 = mybir.dt.float32
    AF = mybir.ActivationFunctionType
    AX = mybir.AxisListType.X
    led = Ledger(known)
    ap = io["ap"]
    v = nc.vector
    with ExitStack() as ctx:
        sems = {}

        def S(name):
            if name not in sems:
                sems[name] = ctx.enter_context(nc.semaphore(name))
            return sems[name]

        def sb(name, *shape):
            return ctx.enter_context(nc.sbuf_tensor(name, [P, *shape], f32))

        ps = ctx.enter_context(nc.psum_tensor("ps", [P, 8, BLK], f32))

        ring = sb("ring", RING, KH, BLK)
        x = sb("x", NG, D)
        proj = sb("proj", NG, D_IN)
        xs = sb("xs", NG, D)
        hnT = sb("hnT", KC, NG * P)
        gateR = sb("gateR", 2, D)
        modT = sb("modT", 4, KC, NG)
        C = {n: sb("c_" + n, a.shape[1]) for n, a in io["consts"].items()}
        condT, silT, sile = sb("condT", NG, KC), sb("silT", KC, 32), sb("sile", NG, KC)
        lbt, oml = sb("lbt", L, 256), sb("oml", 256)
        epsc = sb("epsc", 1)
        nrmT = sb("nrmT", 2, KC)
        wqk, lamp = sb("wqk", 2, DQ), sb("lamp", 4, DQ)
        subln, rnorm, hnorm = sb("subln", DV), sb("rnorm", DR), sb("hnorm", DR)
        rdec, rdecH = sb("rdec", 2 * HR), sb("rdecH", HR)
        ctxk, ctxv = sb("ctxk", BLK), sb("ctxv", BLK)
        s0r, s0h = sb("s0r", HR, DR), sb("s0h", HR, DR)
        wrt, rbias = sb("wrt", KC, NE), sb("rbias", NE)
        lam, lams = sb("lam", 8), sb("lams", 2)
        decT, decin, decend = sb("decT", HR, P), sb("decin", HR, P), sb("decend", HR, 2)
        stat = sb("stat", NG, 64)
        sq, t1, t2, t3, t4 = sb("sq", D), sb("t1", D), sb("t2", BLK), sb("t3", BLK), sb("t4", BLK)
        oT = sq[:, BLK:D].rearrange("p (m t) -> p m t", t=P)
        qw, kT = sb("qw", 4, 4 * P), sb("kT", 4, 2, P)
        qTm = qw[:].rearrange("p j (m t) -> p j m t", m=4)
        wT = qw[:].rearrange("p (hh u) (v t) -> p hh (u v) t", hh=2, t=P).rearrange("p hh (hd part) t -> p hh hd part t", part=2)
        rqT, rkT, rqi = (qw[:, i].rearrange("p (h t) -> p h t", h=HR) for i in range(3))
        hqT, hkT, hqi = rqT, rkT, rqi
        rA = qw[:, 3].rearrange("p (h t) -> p h t", h=HR)
        la = qw[:, 3].rearrange("p (r h d) -> p r h d", r=2, h=HR)
        kf = kT[:].rearrange("p m r t -> p (m r t)")
        rq2, rk2 = (kf[:, i * BLK:(i + 1) * BLK].rearrange("p (h r d) -> p h r d", h=HR, r=2) for i in range(2))
        hq2, hk = rq2, rk2
        eP = sb("eP", 2, 8, 2 * P)
        ef = eP[:].rearrange("p a b c -> p (a b c)")
        A = ef[:, 0:4 * BLK].rearrange("p (z r h t) -> p z r h t", z=2, r=2, h=HR)
        lbin = ef[:, 0:BLK].rearrange("p (l n) -> p l n", l=L)
        gbuf1 = ef[:, 0:NG * D].rearrange("p (g n) -> p g n", g=NG)
        wP = hnT[:].rearrange("p k t -> p (k t)").rearrange("p (hh hd t) -> p hh hd t", hh=2, hd=4)
        rkd = sb("rkd", HR, 2, DR)
        hkd = rkd
        qlv, klv = sb("qlv", 2, HR, P), sb("klv", 2, HR, P)
        ex = sb("ex", 2, HR, P)
        stout = sb("stout", 2, HR, DR)
        gt, seatno = sb("gt", NG, NE), sb("seatno", NG, NE)
        need = sb("need", 8)
        roundsf = sb("roundsf", L + 1)
        roundsi = ctx.enter_context(nc.sbuf_tensor("roundsi", [P, L + 1], mybir.dt.int32))
        rt = sb("rt", 14, NG, NE)
        pf = proj[:].rearrange("p g n -> p (g n)")
        modR = pf[:, 0:4 * D]
        ge, gs, act = (pf[:, i * BLK:(i + 1) * BLK] for i in range(3))
        actT = pf[:, 3 * BLK:4 * BLK].rearrange("p (k s) -> p k s", k=KE)
        xT = pf[:, 4 * BLK:6 * BLK].rearrange("p (k s) -> p k s", k=KC)
        ys = pf[:, 6 * BLK:8 * BLK].rearrange("p (h n) -> p h n", h=2)
        seat, seatG, seatT = (pf[:, 6 * D + i * NG * P:6 * D + (i + 1) * NG * P].rearrange("p (g s) -> p g s", g=NG) for i in range(3))
        rows = xs[:].rearrange("p g (k q) -> p g k q", k=KC)
        gbuf2 = pf[:, 4 * D:6 * D].rearrange("p (g n) -> p g n", g=NG)
        zero = t2

        w_in = ap["w_in"].rearrange("l (p k) n -> p l k n", k=KC)
        w_ada = ap["w_ada"].rearrange("l (p k) n -> p l k n", k=KC)
        w_out = ap["w_out"].rearrange("l (p k) n -> p l k n", k=KC)
        w_gate = ap["w_gate"].rearrange("l e (p k) f -> p (l e) k f", k=KC)
        w_up = ap["w_up"].rearrange("l e (p k) f -> p (l e) k f", k=KC)
        w_down = ap["w_down"].rearrange("l e (p k) d -> p (l e) k d", k=KE)

        block = ctx.enter_context(nc.Block())

        def one(i):
            return bass.ds(i, 1)

        def count_of_rounds(e, i):
            e.sem_inc(S("rounds_seen"), 1)
            return e.value_load(roundsi[0:1, one(i)], min_val=0, max_val=4 * L)

        @block.sync
        def _(sp):
            c = Counts(led, S)
            led.where = "start"
            n_loads = [0]
            for s in range(RING):
                sp.sem_inc(c.makes(f"slot{s}_used"), 1)

            def load(dst_cols, src):
                s = n_loads[0] % RING
                n_loads[0] += 1
                where, n = led.made(f"slot{s}_load")
                t = led.totals
                for w in ("layer", "turn", "after"):
                    t[(f"slot{s}_used", w)] = t.get((f"slot{s}_load", w), 0)
                sp.wait_ge(S(f"slot{s}_used"), c.value(f"slot{s}_used", where, n - 1))
                sp.dma_start(dst_cols(s), src).then_inc(S(f"slot{s}_loaded"), 16)

            with sp.Fori(0, L) as l:
                c.l = l
                sp.wait_ge(S("rounds"), l + 1)
                c.rounds = count_of_rounds(sp, l)
                led.where = "layer"
                for i in range(12):
                    for r in range(2):
                        load(lambda s: ring[:, s:s + 1], w_ada[:, one(l), KH * r:KH * (r + 1), i * BLK:(i + 1) * BLK])
                for i in range(N_IN):
                    n = min(BLK, D_IN - i * BLK)
                    for r in range(2):
                        load(lambda s: ring[:, s:s + 1, :, 0:n], w_in[:, one(l), KH * r:KH * (r + 1), i * BLK:i * BLK + n])
                for i in range(4):
                    for r in range(2):
                        load(lambda s: ring[:, s:s + 1, :, 0:256], w_out[:, one(l), KH * r:KH * (r + 1), i * 256:(i + 1) * 256])
                until = sp.alloc_register("rounds_until")
                with sp.Fori(c.rounds, until) as r:
                    with sp.Fori(0, TURNS) as t:
                        c.t = r * TURNS + t
                        led.where = "turn"
                        for w in (w_gate, w_up):
                            for half in range(2):
                                for e in range(2):
                                    load(lambda s: ring[:, s:s + 1], w[:, one(l * NE + t * 2 + e), KH * half:KH * (half + 1)])
                        for h in range(2):
                            for e in range(2):
                                load(lambda s: ring[:, s:s + 1], w_down[:, one(l * NE + t * 2 + e), :, h * BLK:(h + 1) * BLK])
                    led.where = "rounds"
                    sp.wait_ge(S("rounds"), l + 2)
                    sp.sem_inc(S("rounds_seen"), 1)
                    sp.reg_load(until, roundsi[0:1, one(l + 1)])
                led.where = "after"

        @block.tensor
        def _(pe):
            c = Counts(led, S)
            led.where = "start"
            n_slots, n_tr, owed = [0], [0], []

            def mm(*a, **k):
                ins = nc.tensor.matmul(*a, **k)
                return ins

            def pay(ins):
                if owed:
                    ins.then_inc(S(f"slot{owed.pop(0)}_used"), 1)
                return ins

            def slot():
                s = n_slots[0] % RING
                n_slots[0] += 1
                pe.wait_ge(S(f"slot{s}_loaded"), c.loads(s))
                return s

            def sweep(out, lhs, rhs, n, free_group=False):
                for k in range(n):
                    last = mm(out, lhs(k), rhs(k), start=(k == 0), stop=(k == n - 1), skip_group_check=free_group)
                    if k < n - 1:
                        pay(last)
                return last

            def step_pattern(i, d):
                return C["steps"][:, (2 * i + d) * P:(2 * i + d + 1) * P]

            def bank_of_transposes(label, sources, b=None):
                if b is None:
                    b = n_tr[0] % 2
                    n_tr[0] += 1
                pe.wait_ge(S(f"bank{b}_free"), c.claim(b))
                for i, src in enumerate(sources):
                    last = nc.tensor.transpose(ps[:, b, i * P:(i + 1) * P], src, C["ident"][:])
                    if i < len(sources) - 1:
                        pay(last)
                last.then_inc(c.fills(b, *label), 1)

            def by_feature(stage, rows):
                for g in range(NG):
                    pe.wait_ge(c.of(rows, g), c.at(rows, g))
                    xv = xs[:, g].rearrange("p (q k) -> p k q", k=KC)
                    for h in range(2):
                        bank_of_transposes((stage + "T", g, h), [xv[:, 4 * h + k, :] for k in range(4)])
                for g in range(NG):
                    for h in range(2):
                        pe.wait_ge(c.of(stage + "S", g, h), c.at(stage + "S", g, h))

            for b in range(8):
                pe.sem_inc(c.makes(f"bank{b}_free"), 1)
            pe.wait_ge(c.of("start_dma"), c.at("start_dma"))
            pe.wait_ge(c.of("silT"), c.at("silT"))
            with pe.Fori(0, L) as l:
                c.l = l
                pe.wait_ge(S("rounds"), l + 1)
                c.rounds = count_of_rounds(pe, l)
                led.where = "layer"
                for i in range(12):
                    b = 4 + i % 4
                    pe.wait_ge(S(f"bank{b}_free"), c.claim(b))
                    for r in range(2):
                        s = slot()
                        for j in range(4):
                            last = mm(ps[32 * j:32 * j + 32, b, :], silT[:, KH * r + j, :], ring[:, s, j, :], start=(r == 0), stop=(r == 1))
                            if not (r and j == 3):
                                pay(last)
                        owed.append(s)
                    last.then_inc(c.fills(b, "mod", i), 1)
                pe.wait_ge(c.of("bias"), c.at("bias"))
                pe.wait_ge(S(f"bank{0}_free"), c.claim(0))
                for a in range(4):
                    mv = modR[:, a * D:(a + 1) * D].rearrange("p (q k) -> p k q", k=KC)
                    for k in range(KC):
                        at = (a * KC + k) * NG
                        last = mm(ps[:, 0, at:at + NG], mv[:, k, :], C["pick2"][:], start=True, stop=True)
                        if k < 7:
                            pay(last)
                last.then_inc(c.fills(0, "modT"), 1)

                def spread_gate(a):
                    for g in range(NG):
                        for h in range(2):
                            b = 2 * g + h
                            pe.wait_ge(S(f"bank{b}_free"), c.claim(b))
                            last = mm(ps[:, b, :], C["pick"][:, g * P:(g + 1) * P], gateR[:, a, h * BLK:(h + 1) * BLK], start=True, stop=True)
                            last.then_inc(c.fills(b, "gateP", a, g, h), 1)

                by_feature("hn1", "xn1")
                nb = 0
                for i in range(N_IN):
                    ss = [slot(), slot()]
                    n = min(BLK, D_IN - i * BLK)
                    for g in range(NG):
                        b = 2 + nb % 6
                        nb += 1
                        pe.wait_ge(S(f"bank{b}_free"), c.claim(b))
                        last = sweep(ps[:, b, 0:n], lambda k: hnT[:, k, g * P:(g + 1) * P], lambda k: ring[:, ss[k // KH], k % KH, 0:n], KC)
                        last.then_inc(c.fills(b, "projP", i, g), 1)
                    owed.extend(ss)

                pe.wait_ge(c.of("params"), c.at("params"))
                for g in range(NG):
                    nk = 1 + g
                    pe.wait_ge(c.of("qkn", g), c.at("qkn", g))
                    bank_of_transposes(("daqT", g), [proj[:, g, C_DAQ + m * P:C_DAQ + (m + 1) * P] for m in range(4)])
                    bank_of_transposes(("dakT", g), [proj[:, g, C_DAK + m * P:C_DAK + (m + 1) * P] for m in range(4)])
                    if g:
                        bank_of_transposes(("ctxkT", g), [ctxk[:, m * P:(m + 1) * P] for m in range(4)])
                    pe.wait_ge(c.of("qTm", g), c.at("qTm", g))
                    pe.wait_ge(c.of("kT", g), c.at("kT", g))
                    if g:
                        pe.wait_ge(c.of("kTc", g), c.at("kTc", g))
                    for hh in range(2):
                        for j in range(4):
                            pe.wait_ge(S(f"bank{4 + j}_free"), c.claim(4 + j))
                            for mi in range(2):
                                m = 2 * hh + mi
                                last = mm(ps[:, 4 + j, mi * nk * P:(mi + 1) * nk * P], qTm[:, j, m, :], kT[:, m, 0:nk, :].rearrange("p a t -> p (a t)"), start=True, stop=True)
                            last.then_inc(c.fills(4 + j, "score", g, hh, j), 1)
                    for hh in range(2):
                        pe.wait_ge(c.of("wP", g, hh), c.at("wP", g, hh))
                        for part in range(nk):
                            bank_of_transposes(("wPT", g, hh, part), [wP[:, hh, hd, part * P:(part + 1) * P] for hd in range(4)])
                        if hh == 0:
                            pe.wait_ge(S(f"bank{2}_free"), c.claim(2))
                        for part in range(nk):
                            pe.wait_ge(c.of("wT", g, hh, part), c.at("wT", g, hh, part))
                        for hd in range(4):
                            h = 4 * hh + hd
                            dst = ps[64 * (h % 2):64 * (h % 2) + 64, 2, (h // 2) * P:(h // 2 + 1) * P]
                            for part in range(nk):
                                val = ctxv[:, h * DV:(h + 1) * DV] if part else proj[:, g, C_DAV + h * DV:C_DAV + (h + 1) * DV]
                                last = mm(dst, val, wT[:, hh, hd, part, :], start=(part == 0), stop=(part == nk - 1), skip_group_check=True)
                    last.then_inc(c.fills(2, "daoT", g), 1)
                    pe.wait_ge(c.of("daoTs", g), c.at("daoTs", g))
                    bank_of_transposes(("dao", g), [oT[:, m, :] for m in range(4)], 3)

                    pe.wait_ge(c.of("rk2", g), c.at("rk2", g))
                    bank_of_transposes(("rqT", g), [rq2[:, h].rearrange("p r d -> p (r d)") for h in range(HR)])
                    bank_of_transposes(("rkT", g), [rk2[:, h].rearrange("p r d -> p (r d)") for h in range(HR)])
                    pe.wait_ge(c.of("rqTs", g), c.at("rqTs", g))
                    pe.wait_ge(c.of("rkTs", g), c.at("rkTs", g))
                    pe.wait_ge(S(f"bank{2}_free"), c.claim(2))
                    for h in range(HR):
                        last = mm(ps[:, 2, h * P:(h + 1) * P], rkT[:, h, :], rqT[:, h, :], start=True, stop=True)
                    last.then_inc(c.fills(2, "rS", g), 1)
                    pe.wait_ge(c.of("rA", g), c.at("rA", g))
                    if g:
                        pe.wait_ge(c.of("rqi", g), c.at("rqi", g))
                    pe.wait_ge(S(f"bank{3}_free"), c.claim(3))
                    for h in range(HR):
                        dst = ps[64 * (h % 2):64 * (h % 2) + 64, 3, (h // 2) * P:(h // 2 + 1) * P]
                        last = mm(dst, proj[:, g, C_RV + h * DR:C_RV + (h + 1) * DR], rA[:, h, :], start=True, stop=not g, skip_group_check=True)
                        if g:
                            last = mm(dst, s0r[:, h, :], rqi[:, h, :], start=False, stop=True, skip_group_check=True)
                    last.then_inc(c.fills(3, "roT", g), 1)
                    pe.wait_ge(c.of("roTs", g), c.at("roTs", g))
                    bank_of_transposes(("ro", g), [oT[:, m, :] for m in range(2)], 2)
                    if not g:
                        pe.wait_ge(c.of("rkd", g), c.at("rkd", g))
                        pe.wait_ge(S(f"bank{3}_free"), c.claim(3))
                        for h in range(HR):
                            last = mm(ps[:, 3, h * DR:(h + 1) * DR], rkd[:, h].rearrange("p r d -> p (r d)"), proj[:, g, C_RV + h * DR:C_RV + (h + 1) * DR], start=True, stop=True)
                        last.then_inc(c.fills(3, "rstate", g), 1)

                    pe.wait_ge(c.of("hk", g), c.at("hk", g))
                    pe.wait_ge(c.of("hq2", g), c.at("hq2", g))
                    bank_of_transposes(("hqT", g), [hq2[:, h].rearrange("p r d -> p (r d)") for h in range(HR)])
                    bank_of_transposes(("hkT", g), [hk[:, h].rearrange("p r d -> p (r d)") for h in range(HR)])
                    pe.wait_ge(c.of("la", g), c.at("la", g))
                    def decays(lv):
                        b = 4 + lv % 2
                        pe.wait_ge(S(f"bank{b}_free"), c.claim(b))
                        for h in range(HR):
                            for d in range(2):
                                last = mm(ps[64 * d:64 * d + 64, b, h * P:(h + 1) * P], la[:, d, h, :], C["steps"][:, (2 * lv + d) * P:(2 * lv + d + 1) * P], start=True, stop=True)
                        last.then_inc(c.fills(b, "level", g, lv), 1)
                    decays(0)
                    decays(1)
                    if not g:
                        pe.wait_ge(S(f"bank{6}_free"), c.claim(6))
                        for d in range(2):
                            at = (2 * (NLV + 1) + d) * P
                            last = mm(ps[:, 6, d * 256:(d + 1) * 256], C["steps"][:, at:at + P], la[:, d].rearrange("p h d -> p (h d)"), start=True, stop=True)
                        last.then_inc(c.fills(6, "toend", g), 1)
                    pe.wait_ge(c.of("hqTs", g), c.at("hqTs", g))
                    pe.wait_ge(c.of("hkTs", g), c.at("hkTs", g))
                    def scores(lv):
                        if lv >= 0:
                            pe.wait_ge(c.of("klv", g, lv), c.at("klv", g, lv))
                            pe.wait_ge(c.of("qlv", g, lv), c.at("qlv", g, lv))
                        for r in range(2 if lv >= 0 else 1):
                            pe.wait_ge(S(f"bank{2 + r}_free"), c.claim(2 + r))
                            q = slice(64 * r, 64 * r + 64)
                            for h in range(HR):
                                k_, q_ = (klv[q, lv % 2, h, :], qlv[q, lv % 2, h, :]) if lv >= 0 else (hkT[:, h, :], hqT[:, h, :])
                                last = mm(ps[:, 2 + r, h * P:(h + 1) * P], k_, q_, start=True, stop=True)
                            last.then_inc(c.fills(2 + r, "hS", g, lv, r), 1)

                    def head(h):
                        return ps[64 * (h % 2):64 * (h % 2) + 64, 7, (h // 2) * P:(h // 2 + 1) * P]

                    def values(lv):
                        for r in range(2 if lv >= 0 else 1):
                            pe.wait_ge(c.of("hA", g, lv, r), c.at("hA", g, lv, r))
                            for h in range(HR):
                                end = not g and lv == NLV - 1 and r == 1
                                last = mm(head(h), proj[:, g, C_GI + h * DR:C_GI + (h + 1) * DR], A[:, lv % 2, r, h, :], start=(lv < 0 and h < 2), stop=end, skip_group_check=True)
                        if lv < NLV - 1:
                            last.then_inc(c.makes("hV", g, lv), 1)
                        return last

                    scores(-1)
                    scores(0)
                    decays(2)
                    pe.wait_ge(S(f"bank{7}_free"), c.claim(7))
                    for lv in range(-1, NLV):
                        last = values(lv)
                        if lv + 2 < NLV:
                            scores(lv + 2)
                        if lv + 4 < NLV + g:
                            decays(lv + 4)
                    if g:
                        pe.wait_ge(c.of("hqi", g), c.at("hqi", g))
                        for h in range(HR):
                            last = mm(head(h), s0h[:, h, :], hqi[:, h, :], start=False, stop=True, skip_group_check=True)
                    last.then_inc(c.fills(7, "hoT", g), 1)
                    pe.wait_ge(c.of("hoTs", g), c.at("hoTs", g))
                    bank_of_transposes(("ho", g), [oT[:, m, :] for m in range(2)], 2)
                    if not g:
                        pe.wait_ge(c.of("hkd", g), c.at("hkd", g))
                        pe.wait_ge(S(f"bank{3}_free"), c.claim(3))
                        for h in range(HR):
                            last = mm(ps[:, 3, h * DR:(h + 1) * DR], hkd[:, h].rearrange("p r d -> p (r d)"), proj[:, g, C_GI + h * DR:C_GI + (h + 1) * DR], start=True, stop=True)
                        last.then_inc(c.fills(3, "hstate", g), 1)

                by_feature("mix", "mixed")
                spread_gate(0)
                for n in range(4):
                    ss = [slot(), slot()]
                    for g in range(NG):
                        b = 4 + 2 * (n % 2) + g
                        pe.wait_ge(S(f"bank{b}_free"), c.claim(b))
                        last = sweep(ps[:, b, 0:256], lambda k: hnT[:, k, g * P:(g + 1) * P], lambda k: ring[:, ss[k // KH], k % KH, 0:256], KC)
                        last.then_inc(c.fills(b, "out", n, g), 1)
                    owed.extend(ss)

                by_feature("hn2", "xn2")
                pe.wait_ge(S(f"bank{2}_free"), c.claim(2))
                for g in range(NG):
                    last = sweep(ps[:, 2, g * NE:(g + 1) * NE], lambda k: hnT[:, k, g * P:(g + 1) * P], lambda k: wrt[:, k, :], KC)
                last.then_inc(c.fills(2, "router"), 1)

                for g in range(NG):
                    for h in range(2):
                        bank_of_transposes(("rows", g, h), [hnT[:, 4 * h + k, g * P:(g + 1) * P] for k in range(4)])
                pe.wait_ge(c.of("picks", 0), c.at("picks", 0))
                pe.wait_ge(S("bank2_free"), c.claim(2))
                mm(ps[:, 2, 0:NG * NE], step_pattern(NLV + 1, 1), rt[:, 13].rearrange("p g e -> p (g e)"), start=True, stop=True)
                for d in range(2):
                    last = mm(ps[:, 2, NG * NE:2 * NG * NE], step_pattern(NLV + d, 0), rt[:, 13].rearrange("p g e -> p (g e)"), start=(d == 0), stop=(d == 1))
                last.then_inc(c.fills(2, "ahead"), 1)

                pe.wait_ge(c.of("zeroed"), c.at("zeroed"))
                for b in range(4, 8):
                    pe.wait_ge(S(f"bank{b}_free"), c.claim(b))
                    mm(ps[:, b, :], zero[:, 0:P], zero[:, 0:BLK], start=True, stop=False, skip_group_check=True)
                for g in range(NG):
                    for h in range(2):
                        pe.wait_ge(c.of("rowsS", g, h), c.at("rowsS", g, h))
                pe.wait_ge(S("rounds"), l + 2)
                until = count_of_rounds(pe, l + 1)
                with pe.Fori(c.rounds, until) as r:
                    with pe.Fori(0, TURNS) as t:
                        c.t = r * TURNS + t
                        led.where = "turn"
                        pe.wait_ge(c.of("seat", 0), c.at("seat", 0))
                        for half in range(2):
                            pe.wait_ge(S(f"bank{half}_free"), c.claim(half))
                            for k in range(KH):
                                for g in range(NG):
                                    last = mm(ps[:, half, k * P:(k + 1) * P], rows[:, g, KH * half + k, :], seat[:, g, :], start=(g == 0), stop=(g == 1))
                            last.then_inc(c.fills(half, "xT", half), 1)
                        for i in range(2):
                            pe.wait_ge(S(f"bank{2 + i}_free"), c.claim(2 + i))
                            for half in range(2):
                                pair = [slot(), slot()]
                                pe.wait_ge(c.of("xTs", half), c.at("xTs", half))
                                for k in range(KH):
                                    for e, s in enumerate(pair):
                                        last = mm(ps[64 * e:64 * e + 64, 2 + i, :], xT[:, KH * half + k, 64 * e:64 * e + 64], ring[:, s, k, :], start=(half == 0 and k == 0), stop=(half == 1 and k == KH - 1), skip_group_check=True)
                                        if k == KH - 1 and not (half and e):
                                            last.then_inc(S(f"slot{s}_used"), 1)
                                        elif not (half and e and k == KH - 1):
                                            pay(last)
                            owed.append(pair[1])
                            last.then_inc(c.fills(2 + i, "gu", i), 1)
                        pe.wait_ge(c.of("seatG", 0), c.at("seatG", 0))
                        bank_of_transposes(("seatT",), [seatG[:, g, :] for g in range(NG)], 1)
                        pe.wait_ge(c.of("act"), c.at("act"))
                        bank_of_transposes(("actT",), [act.rearrange("p (q k) -> p k q", k=KE)[:, k, :] for k in range(KE)], 0)
                        pe.wait_ge(c.of("actTs"), c.at("actTs"))
                        for h in range(2):
                            pair = [slot(), slot()]
                            pe.wait_ge(S(f"bank{2 + h}_free"), c.claim(2 + h))
                            for k in range(KE):
                                for e, s in enumerate(pair):
                                    last = mm(ps[64 * e:64 * e + 64, 2 + h, :], actT[:, k, 64 * e:64 * e + 64], ring[:, s, k, :], start=(k == 0), stop=(k == KE - 1), skip_group_check=True)
                                    if k == KE - 1 and not e:
                                        last.then_inc(S(f"slot{s}_used"), 1)
                                    elif k < KE - 1:
                                        pay(last)
                            owed.append(pair[1])
                            last.then_inc(c.fills(2 + h, "yP", h), 1)
                        pe.wait_ge(c.of("seatTs"), c.at("seatTs"))
                        for h in range(2):
                            pe.wait_ge(c.of("ys", h), c.at("ys", h))
                            for g in range(NG):
                                pay(mm(ps[:, 4 + 2 * g + h, :], seatT[:, g, :], ys[:, h, :], start=False, stop=False, skip_group_check=True))
                c.rounds = until
                led.where = "after"
                for b in range(4, 8):
                    last = mm(ps[:, b, :], zero[:, 0:P], zero[:, 0:BLK], start=False, stop=True, skip_group_check=True)
                    last.then_inc(c.fills(b, "y", b - 4), 1)
                spread_gate(1)
            assert not owed

        @block.vector
        def _(dve):
            c = Counts(led, S)
            led.where = "start"
            tt, ts, stt = v.tensor_tensor, v.tensor_scalar, v.scalar_tensor_tensor

            def st(ins, *label):
                ins.then_inc(c.makes(*(label or ("dve_step",))), 1)
                dve.wait_ge(S(c.last[0]), c.last_value())

            def red(out, in_, op=ALU.add):
                return v.tensor_reduce(out=out, in_=in_, axis=AX, op=op)

            def cols(a, g, n, h=HR):
                return proj[:, g, a:a + n].rearrange("p (h d) -> p h d", h=h)

            st(v.memset(epsc[:], EPS))
            st(v.memset(roundsf[:], 0.0))
            st(v.tensor_copy(roundsi[:], roundsf[:]), "rounds")
            st(v.memset(silT[:].rearrange("p k n -> p (k n)"), 0.0))
            led.found[("eps",)] = ("dve_step", "start", 1)
            dve.wait_ge(c.of("start_dma"), c.at("start_dma"))
            dve.wait_ge(c.of("sile"), c.at("sile"))
            st(ts(t1[:, 0:16], sile[:].rearrange("p g k -> p (g k)"), 1.0, None, ALU.add))
            st(v.reciprocal(t1[:, 16:32], t1[:, 0:16]))
            st(tt(silT[:, :, 0:NG].rearrange("p k g -> p g k"), condT[:], t1[:, 16:32].rearrange("p (g k) -> p g k", k=KC), ALU.mult), "silT", 0)
            led.found[("silT",)] = led.found[("silT", 0)]
            st(tt(t1[:, 0:256], lbin[:, 0], lbin[:, 1], ALU.max))
            for l_ in range(L):
                st(tt(lbt[:, l_], lbin[:, l_], t1[:, 0:256], ALU.subtract), "lbd", l_)
            dve.wait_ge(c.of("lbe"), c.at("lbe"))
            st(tt(t1[:, 0:256], lbin[:, 0], lbin[:, 1], ALU.add))
            st(v.reciprocal(t1[:, 256:512], t1[:, 0:256]))
            for l_ in range(L):
                st(tt(lbin[:, l_], lbin[:, l_], t1[:, 256:512], ALU.mult))
            st(tt(t1[:, 0:256], lbin[:, 0], lbin[:, 1], ALU.add))
            st(tt(lbt[:, 0], lbin[:, 0], lbin[:, 0], ALU.subtract))
            st(tt(lbt[:, 1], t1[:, 0:256], lbin[:, 0], ALU.subtract))

            with dve.Fori(0, L) as l:
                c.l = l
                dve.wait_ge(S("rounds"), l + 1)
                c.rounds = count_of_rounds(dve, l)
                led.where = "layer"
                dve.wait_ge(c.of("params"), c.at("params"))
                lb = lbt[:, one(l)]
                st(ts(oml[:], lb.rearrange("p l n -> p (l n)"), -1.0, 1.0, ALU.mult, ALU.add))
                st(v.tensor_copy(lams[:], C["lami"][:, bass.ds(l * 2, 2)]))
                st(tt(t1[:, 0:32], lamp[:, 0], lamp[:, 1], ALU.mult))
                st(tt(t1[:, 32:64], lamp[:, 2], lamp[:, 3], ALU.mult))
                st(red(lam[:, 0:2], t1[:, 0:64].rearrange("p (a b) -> p a b", a=2)), "lamsum", 0)
                dve.wait_ge(c.of("lamexp"), c.at("lamexp"))
                st(tt(lam[:, 4:5], lam[:, 2:3], lam[:, 3:4], ALU.subtract))
                st(tt(lam[:, 5:6], lam[:, 4:5], lams[:, 0:1], ALU.add))
                st(ts(lam[:, 6:7], lam[:, 5:6], -1.0, None, ALU.mult))
                st(ts(subln[:], subln[:], lams[:, 1:2], None, ALU.mult))
                dve.wait_ge(c.of("rdec"), c.at("rdec"))
                st(ts(rdec[:], rdec[:], -1.0, None, ALU.mult))
                st(ts(rdecH[:], rdecH[:], -1.0, None, ALU.mult), "rdecn", 0)
                dve.wait_ge(c.of("decT"), c.at("decT"))
                tb = t1[:, 0:BLK].rearrange("p (h t) -> p h t", h=HR)
                for d, half in enumerate((decT[:], tb)):
                    st(tt(half, half, C["steps"][:, (2 * NLV + d) * P:(2 * NLV + d + 1) * P].rearrange("p (o t) -> p o t", o=1).broadcast_to([P, HR, P]), ALU.mult))
                st(tt(decT[:], decT[:], tb, ALU.add), "decS", 0)

                dve.wait_ge(c.of("modT"), c.at("modT"))
                v.tensor_copy(modT[:].rearrange("p a k g -> p (a k g)"), ps[:, 0, 0:64]).then_inc(c.freed(("modT",)), 1)
                dve.wait_ge(S(c.last[0]), c.last_value())
                for a in range(2):
                    st(stt(out=modT[:, 2 * a + 1], in0=modT[:, 2 * a + 1], scalar=1.0, in1=nrmT[:, a].rearrange("p (k o) -> p k o", o=1).broadcast_to([P, KC, NG]), op0=ALU.add, op1=ALU.mult), "modS", a)

                def normed(stage):
                    for g in range(NG):
                        dve.wait_ge(c.of(stage + "r", g), c.at(stage + "r", g))
                        st(ts(xs[:, g], x[:, g], stat[:, g, 2:3], None, ALU.mult), stage, g)

                def shifted(stage, a):
                    for h in range(2):
                        dve.wait_ge(c.of(stage + "T", 0, h), c.at(stage + "T", 0, h))
                        b = c.bank(stage + "T", 0, h)
                        for k in range(4):
                            kc = 4 * h + k
                            ins = ts(hnT[:, kc, 0:P], ps[:, b, k * P:(k + 1) * P], modT[:, 2 * a + 1, kc, 0:1], modT[:, 2 * a, kc, 0:1], ALU.mult, ALU.add)
                        ins.then_inc(c.freed((stage + "T", 0, h), stage + "S", 0, h), 1)
                        dve.wait_ge(S(c.last[0]), c.last_value())

                normed("xn1")
                shifted("hn1", 0)
                nb = 0
                for i in range(N_IN):
                    n = min(BLK, D_IN - i * BLK)
                    dve.wait_ge(c.of("projP", i, 0), c.at("projP", i, 0))
                    b = 2 + nb % 6
                    nb += 2
                    v.tensor_copy(proj[:, 0, i * BLK:i * BLK + n], ps[:, b, 0:n]).then_inc(c.freed(("projP", i, 0), "projS", i, 0), 1)
                    dve.wait_ge(S(c.last[0]), c.last_value())

                def group_norm(read, b, n, w, g, base, src_label):
                    m = n * 64
                    dve.wait_ge(c.of(src_label + "q", g), c.at(src_label + "q", g))
                    st(red(stat[:, g, 16:16 + n], sq[:, 0:m].rearrange("p (h d) -> p h d", h=n)), src_label + "m", g)
                    dve.wait_ge(c.of(src_label + "r", g), c.at(src_label + "r", g))
                    out = xs[:, g, base:base + m].rearrange("p (h d) -> p h d", h=n)
                    tt(out, ps[:, b, 0:m].rearrange("p (h d) -> p h d", h=n), stat[:, g, 16:16 + n].rearrange("p (h o) -> p h o", o=1).broadcast_to([P, n, 64]), ALU.mult).then_inc(c.freed(read), 1)
                    dve.wait_ge(S(c.last[0]), c.last_value())
                    ins = tt(out, out, w[:].rearrange("p (o d) -> p o d", o=1).broadcast_to([P, n, 64]), ALU.mult)
                    return ins, out

                def swish(src, e_label, g, out, label):
                    dve.wait_ge(c.of(e_label, g), c.at(e_label, g))
                    st(ts(t4[:, 0:256], t4[:, 0:256], 1.0, None, ALU.add))
                    st(v.reciprocal(t4[:, 0:256], t4[:, 0:256]))
                    st(out(t4[:, 0:256].rearrange("p (h d) -> p h d", h=HR)), *label)

                for g in range(NG):
                    nk = 1 + g
                    for i in range(3):
                        dve.wait_ge(c.of("projS", i, g), c.at("projS", i, g))
                    both = proj[:, g, 0:D].rearrange("p (a d) -> p a d", d=DQ)
                    st(tt(sq[:], proj[:, g, 0:D], proj[:, g, 0:D], ALU.mult))
                    st(red(stat[:, g, 32:64], sq[:].rearrange("p (a d) -> p a d", d=DQ)), "qkm", g)
                    dve.wait_ge(c.of("qkr", g), c.at("qkr", g))
                    st(tt(both, both, stat[:, g, 32:64].rearrange("p (a o) -> p a o", o=1).broadcast_to([P, 32, DQ]), ALU.mult))
                    for r in range(2):
                        lab = ("qkn", g) if (not g and r) else ()
                        st(tt(both[:, 2 * NH * r:2 * NH * (r + 1)], both[:, 2 * NH * r:2 * NH * (r + 1)], wqk[:, r].rearrange("p (o d) -> p o d", o=1).broadcast_to([P, 2 * NH, DQ]), ALU.mult), *lab)
                    if g:
                        pairs = both.rearrange("p a (i z) -> p a i z", z=2)
                        cs = C["cos"][:].rearrange("p (o d) -> p o d", o=1).broadcast_to([P, 32, DQ])
                        sn = C["sin"][:].rearrange("p (o i z) -> p o i z", o=1, z=2).broadcast_to([P, 32, DQ // 2, 2])
                        rot = t1[:].rearrange("p (a i z) -> p a i z", i=DQ // 2, z=2)
                        for z in range(2):
                            st(tt(rot[:, :, :, z], pairs[:, :, :, 1 - z], sn[:, :, :, z], ALU.mult))
                        st(tt(both, both, cs, ALU.mult))
                        st(tt(both, both, t1[:].rearrange("p (a d) -> p a d", d=DQ), ALU.add), "qkn", g)
                    dve.wait_ge(c.of("daqT", g), c.at("daqT", g))
                    b = c.bank("daqT", g)
                    for j in range(4):
                        ins = ts(qTm[:, j], ps[:, b].rearrange("p (m t) -> p m t", m=4), C["quarter"][:, j:j + 1], None, ALU.mult)
                    ins.then_inc(c.freed(("daqT", g), "qTm", g), 1)
                    dve.wait_ge(S(c.last[0]), c.last_value())
                    sm = stat[:, g]
                    for hh in range(2):
                        for j in range(4):
                            dve.wait_ge(c.of("score", g, hh, j), c.at("score", g, hh, j))
                        mx = rt[:, 2 * hh, 0, 0:8].rearrange("p (m j) -> p j m", j=4)
                        st(red(mx, ps[:, 4:8, 0:2 * nk * P].rearrange("p j (m t) -> p j m t", m=2), ALU.max))
                        st(ts(rt[:, 2 * hh, 0, 8:16], rt[:, 2 * hh, 0, 0:8], -DQ ** -0.5, None, ALU.mult), "nmax", g, hh)
                    for hh in range(2):
                        dve.wait_ge(c.of("expd", g, hh), c.at("expd", g, hh))
                        rs = rt[:, 2 * hh + 1, 0]
                        st(v.reciprocal(rs[:, 8:16], rs[:, 0:8]))
                        rr = rs[:, 8:16].rearrange("p (a r) -> p r a", r=2)
                        st(ts(rr[:, 1], rr[:, 1], lam[:, 6:7], None, ALU.mult))
                        for hd in range(4):
                            i0 = 2 * hd
                            st(ts(t2[:, 0:nk * P], eP[:, hh, i0, 0:nk * P], rs[:, 8 + i0:9 + i0], None, ALU.mult))
                            lab = ("wP", g, hh) if hd == 3 else ()
                            st(stt(out=wP[:, hh, hd, 0:nk * P], in0=eP[:, hh, i0 + 1, 0:nk * P], scalar=rs[:, 9 + i0:10 + i0], in1=t2[:, 0:nk * P], op0=ALU.mult, op1=ALU.add), *lab)
                    for i in range(3, 5):
                        dve.wait_ge(c.of("projS", i, g), c.at("projS", i, g))
                    st(v.tensor_copy(rq2, cols(C_RQ, g, 256).rearrange("p h (o d) -> p h o d", o=1).broadcast_to([P, HR, 2, DR])))
                    st(ts(rk2, cols(C_RK, g, 256).rearrange("p h (o d) -> p h o d", o=1).broadcast_to([P, HR, 2, DR]), DR ** -0.5, None, ALU.mult), "rk2", g)
                    if not g:
                        dve.wait_ge(c.of("decend"), c.at("decend"))
                        st(tt(rkd[:], rk2, decend[:].rearrange("p h (r o) -> p h r o", o=1).broadcast_to([P, HR, 2, DR]), ALU.mult), "rkd", g)
                    dve.wait_ge(c.of("rkT", g), c.at("rkT", g))
                    b = c.bank("rkT", g)
                    ts(qw[:, 1], ps[:, b], 0.5, None, ALU.mult).then_inc(c.freed(("rkT", g), "rkTs", g), 1)
                    dve.wait_ge(S(c.last[0]), c.last_value())
                    ins, _ = group_norm(("dao", g), 3, NH, subln, g, 0, "dao")
                    st(ins)
                    if g:
                        dve.wait_ge(c.of("rqTs", g), c.at("rqTs", g))
                        dve.wait_ge(c.of("decin"), c.at("decin"))
                        st(tt(rqi, rqT, decin[:], ALU.mult), "rqi", g)
                    dve.wait_ge(c.of("rS", g), c.at("rS", g))
                    tt(rA, ps[:, 2].rearrange("p (h t) -> p h t", h=HR), decT[:], ALU.mult).then_inc(c.freed(("rS", g), "rA", g), 1)
                    dve.wait_ge(S(c.last[0]), c.last_value())
                    ins, out = group_norm(("ro", g), 2, HR, rnorm, g, 512, "ro")
                    st(ins)
                    swish(None, "rge", g, lambda r: tt(t4[:, 256:512].rearrange("p (h d) -> p h d", h=HR), cols(C_RG, g, 256), r, ALU.mult), ())
                    st(tt(out, out, t4[:, 256:512].rearrange("p (h d) -> p h d", h=HR), ALU.mult), "rgdone", g)

                    for i in range(5, N_IN):
                        dve.wait_ge(c.of("projS", i, g), c.at("projS", i, g))
                    if g:
                        dve.wait_ge(c.of("toend", 0), c.at("toend", 0))
                    zz = proj[:, g, C_GFF:C_GFF + BLK]
                    st(ts(t2[:], zz, -80.0, None, ALU.max), "zc", g)
                    dve.wait_ge(c.of("ze", g), c.at("ze", g))
                    st(ts(t3[:], t2[:], 1.0, None, ALU.add))
                    st(v.reciprocal(t3[:], t3[:]))
                    st(tt(t2[:], t2[:], t3[:], ALU.mult))
                    omlv = oml[:].rearrange("p (o h d) -> p o h d", o=1, h=HR).broadcast_to([P, 2, HR, DR])
                    lbv = lb.rearrange("p o (h d) -> p o h d", h=HR).broadcast_to([P, 2, HR, DR])
                    dhd = lambda a: a.rearrange("p (r h d) -> p r h d", r=2, h=HR)
                    st(tt(hk.rearrange("p h r d -> p r h d"), dhd(t2[:]), omlv, ALU.mult), "hk", g)
                    st(tt(dhd(t3[:]), dhd(t3[:]), omlv, ALU.mult))
                    st(tt(dhd(t3[:]), dhd(t3[:]), lbv, ALU.add))
                    st(ts(t3[:], t3[:], 1e-30, None, ALU.max))
                    st(ts(t2[:], t3[:], LN_LOW, 1.0 / LN_LOW, ALU.is_lt, ALU.mult))
                    st(stt(out=t3[:], in0=t2[:], scalar=1.0, in1=t3[:], op0=ALU.max, op1=ALU.mult), "gatef", g)
                    dve.wait_ge(c.of("gln", g), c.at("gln", g))
                    st(stt(out=qw[:, 3], in0=t2[:], scalar=LN_LOW * math.log(LN_LOW), in1=t3[:], op0=ALU.mult, op1=ALU.add), "la", g)
                    swish(None, "gqe", g, lambda r: tt(hq2, cols(C_GQ, g, 256).rearrange("p h (o d) -> p h o d", o=1).broadcast_to([P, HR, 2, DR]), r.rearrange("p h (o d) -> p h o d", o=1).broadcast_to([P, HR, 2, DR]), ALU.mult), ("hq2", g))
                    dve.wait_ge(c.of("hkT", g), c.at("hkT", g))
                    b = c.bank("hkT", g)
                    v.tensor_copy(qw[:, 1], ps[:, b]).then_inc(c.freed(("hkT", g), "hkTs", g), 1)
                    dve.wait_ge(S(c.last[0]), c.last_value())
                    dve.wait_ge(c.of("hqTs", g), c.at("hqTs", g))

                    def masked(lv):
                        if lv >= 1:
                            dve.wait_ge(c.of("hV", g, lv - 2), c.at("hV", g, lv - 2))
                        for r in range(2 if lv >= 0 else 1):
                            m = C["ident"][:] if lv < 0 else C["masks"][:, (2 * lv + r) * P:(2 * lv + r + 1) * P]
                            dve.wait_ge(c.of("hS", g, lv, r), c.at("hS", g, lv, r))
                            src = ps[:, 2 + r].rearrange("p (h t) -> p h t", h=HR)
                            tt(A[:, lv % 2, r], src, m.rearrange("p (o t) -> p o t", o=1).broadcast_to([P, HR, P]), ALU.mult).then_inc(c.freed(("hS", g, lv, r), "hA", g, lv, r), 1)
                            dve.wait_ge(S(c.last[0]), c.last_value())

                    def scaled_queries(lv):
                        dve.wait_ge(c.of("ex", g, lv), c.at("ex", g, lv))
                        st(tt(qlv[:, lv % 2], hqT, ex[:, lv % 2], ALU.mult), "qlv", g, lv)

                    scaled_queries(0)
                    for lv in range(-1, NLV):
                        if 0 <= lv < NLV - 1:
                            scaled_queries(lv + 1)
                        masked(lv)
                    if g:
                        dve.wait_ge(c.of("ex", g, NLV), c.at("ex", g, NLV))
                        st(tt(hqi, hqT, ex[:, NLV % 2], ALU.mult), "hqi", g)
                    else:
                        dve.wait_ge(c.of("exend", g), c.at("exend", g))
                        st(tt(hkd[:].rearrange("p h r d -> p r h d"), hk.rearrange("p h r d -> p r h d"), dhd(t3[:]), ALU.mult), "hkd", g)
                    ins, out = group_norm(("ho", g), 2, HR, hnorm, g, 768, "ho")
                    st(ins)
                    swish(None, "gge", g, lambda r: tt(t4[:, 256:512].rearrange("p (h d) -> p h d", h=HR), cols(C_GG, g, 256), r, ALU.mult), ())
                    st(tt(out, out, t4[:, 256:512].rearrange("p (h d) -> p h d", h=HR), ALU.mult), "mixed", g)

                for g in range(1):
                    for h in range(2):
                        dve.wait_ge(c.of("mixT", g, h), c.at("mixT", g, h))
                        b = c.bank("mixT", g, h)
                        v.tensor_copy(hnT[:, 4 * h:4 * h + 4, g * P:(g + 1) * P], ps[:, b].rearrange("p (k t) -> p k t", k=4)).then_inc(c.freed(("mixT", g, h), "mixS", g, h), 1)
                        dve.wait_ge(S(c.last[0]), c.last_value())
                for n in range(4):
                    for g in range(NG):
                        sl = slice(n * 256, (n + 1) * 256)
                        dve.wait_ge(c.of("gateS", 0, g, n // 2), c.at("gateS", 0, g, n // 2))
                        dve.wait_ge(c.of("out", n, g), c.at("out", n, g))
                        tt(t1[:, 0:256], ps[:, 4 + 2 * (n % 2) + g, 0:256], gbuf1[:, g, sl], ALU.mult).then_inc(c.freed(("out", n, g)), 1)
                        dve.wait_ge(S(c.last[0]), c.last_value())
                        lab = ("x1", g) if n == 3 else ()
                        st(tt(x[:, g, sl], x[:, g, sl], t1[:, 0:256], ALU.add), *lab)
                normed("xn2")
                shifted("hn2", 1)

                st(v.memset(zero[:], 0.0), "zeroed", 0)
                led.found[("zeroed",)] = led.found[("zeroed", 0)]

                G4 = lambda a: a.rearrange("p g (q e) -> p g q e", e=4)
                dve.wait_ge(c.of("rexp"), c.at("rexp"))
                sc, sel = rt[:, 1], rt[:, 2]
                st(ts(rt[:, 3], rt[:, 0], 1.0, None, ALU.add))
                st(v.reciprocal(sc, rt[:, 3]))
                st(tt(sel, sc, rbias[:].rearrange("p (o e) -> p o e", o=1).broadcast_to([P, NG, NE]), ALU.add))
                s4 = sel.rearrange("p g (q a z) -> p g q a z", a=2, z=2)
                hi = rt[:, 3, :, 0:8].rearrange("p g (q a) -> p g q a", a=2)
                lo = rt[:, 4, :, 0:8].rearrange("p g (q a) -> p g q a", a=2)
                st(tt(hi, s4[:, :, :, :, 0], s4[:, :, :, :, 1], ALU.max))
                st(tt(lo, s4[:, :, :, :, 0], s4[:, :, :, :, 1], ALU.min))
                st(tt(rt[:, 5, :, 0:4], hi[:, :, :, 0], hi[:, :, :, 1], ALU.max))
                st(tt(rt[:, 5, :, 4:8], hi[:, :, :, 0], hi[:, :, :, 1], ALU.min))
                st(tt(rt[:, 5, :, 8:12], lo[:, :, :, 0], lo[:, :, :, 1], ALU.max))
                st(tt(rt[:, 5, :, 4:8], rt[:, 5, :, 4:8], rt[:, 5, :, 8:12], ALU.max))
                st(tt(rt[:, 5, :, 0:4], rt[:, 5, :, 0:4], rt[:, 5, :, 4:8], ALU.add))

                def first_best(vals, rank, n, pick, tmp):
                    m = stat[:, 0, 0:NG]
                    bc = lambda a: a.rearrange("p (g o) -> p g o", o=1).broadcast_to([P, NG, n])
                    st(red(m, vals, ALU.max))
                    st(tt(tmp, vals, bc(m), ALU.is_equal))
                    st(tt(tmp, tmp, C[rank][:].rearrange("p (o e) -> p o e", o=1).broadcast_to([P, NG, n]), ALU.mult))
                    st(red(m, tmp, ALU.max))
                    st(tt(pick, tmp, bc(m), ALU.is_equal))

                first_best(rt[:, 5, :, 0:4], "rank4", 4, rt[:, 6, :, 0:4], rt[:, 7, :, 0:4])
                grp = rt[:, 6, :, 0:4].rearrange("p g (q o) -> p g q o", o=1).broadcast_to([P, NG, 4, 4])
                st(ts(rt[:, 8, :, 0:4], rt[:, 6, :, 0:4], 2.0, -2.0, ALU.mult, ALU.add))
                st(tt(G4(rt[:, 9]), G4(sel), grp, ALU.mult))
                st(tt(G4(rt[:, 9]), G4(rt[:, 9]), rt[:, 8, :, 0:4].rearrange("p g (q o) -> p g q o", o=1).broadcast_to([P, NG, 4, 4]), ALU.add))
                first_best(rt[:, 9], "rank16", NE, rt[:, 10], rt[:, 11])
                st(stt(out=rt[:, 9], in0=rt[:, 10], scalar=-1e30, in1=rt[:, 9], op0=ALU.mult, op1=ALU.add))
                first_best(rt[:, 9], "rank16", NE, rt[:, 12], rt[:, 11])
                st(tt(rt[:, 13], rt[:, 10], rt[:, 12], ALU.add), "picks", 0)
                st(tt(rt[:, 10], rt[:, 13], sc, ALU.mult))
                st(red(stat[:, 0, 0:NG], rt[:, 10]))
                st(v.reciprocal(stat[:, 0, 2:4], stat[:, 0, 0:NG]))
                st(tt(gt[:], rt[:, 10], stat[:, 0, 2:4].rearrange("p (g o) -> p g o", o=1).broadcast_to([P, NG, NE]), ALU.mult))
                for g in range(NG):
                    for h in range(2):
                        if (2 * g + h) % 2:
                            dve.wait_ge(c.of("rows", g, h), c.at("rows", g, h))
                            b = c.bank("rows", g, h)
                            v.tensor_copy(xs[:, g, h * BLK:(h + 1) * BLK], ps[:, b]).then_inc(c.freed(("rows", g, h), "rowsS", g, h), 1)
                            dve.wait_ge(S(c.last[0]), c.last_value())
                dve.wait_ge(c.of("ahead"), c.at("ahead"))
                st(ts(rt[:, 9], rt[:, 13], -FAR, FAR, ALU.mult, ALU.add))
                st(tt(seatno[:], rt[:, 9], ps[:, 2, 0:NG * NE].rearrange("p (g e) -> p g e", g=NG), ALU.add))
                total = rt[:, 12]
                v.tensor_copy(total, ps[:, 2, NG * NE:2 * NG * NE].rearrange("p (g e) -> p g e", g=NG)).then_inc(c.freed(("ahead",)), 1)
                dve.wait_ge(S(c.last[0]), c.last_value())
                st(tt(seatno[:, 1], seatno[:, 1], total[:, 0], ALU.add))
                st(tt(rt[:, 11, 0], total[:, 0], total[:, 1], ALU.add))
                st(red(need[:, 0:1], rt[:, 11, 0], ALU.max))
                for i in range(1, NG * P // SLOTS):
                    st(ts(need[:, i:i + 1], need[:, 0:1], float(i * SLOTS), None, ALU.is_gt))
                st(red(need[:, 4:5], need[:, 1:NG * P // SLOTS]))
                st(stt(out=roundsf[:, one(l + 1)], in0=need[:, 4:5], scalar=1.0, in1=roundsf[:, one(l)], op0=ALU.add, op1=ALU.add))
                st(v.tensor_copy(roundsi[:, one(l + 1)], roundsf[:, one(l + 1)]), "rounds")
                until = count_of_rounds(dve, l + 1)
                with dve.Fori(c.rounds, until) as r:
                    with dve.Fori(0, TURNS) as t:
                        c.t = r * TURNS + t
                        led.where = "turn"
                        at = lambda a, g: a[:, g, bass.ds(t * 2, 2)].rearrange("p (e o) -> p e o", o=1).broadcast_to([P, 2, SLOTS])
                        by_seat = lambda a, g: a[:, g].rearrange("p (e s) -> p e s", e=2)
                        for g in range(NG):
                            st(tt(by_seat(seat, g), C["slot"][:].rearrange("p (o s) -> p o s", o=1).broadcast_to([P, 2, SLOTS]), at(seatno, g), ALU.is_equal), "seat", g - 1)
                        for g in range(NG):
                            st(tt(by_seat(seatG, g), by_seat(seat, g), at(gt, g), ALU.mult), "seatG", g - 1)
                        dve.wait_ge(c.of("gexp"), c.at("gexp"))
                        st(ts(ge, ge, 1.0, None, ALU.add))
                        st(v.reciprocal(ge, ge))
                        tt(gs, ps[:, 2], ge, ALU.mult).then_inc(c.freed(("gu", 0)), 1)
                        dve.wait_ge(S(c.last[0]), c.last_value())
                        dve.wait_ge(c.of("gu", 1), c.at("gu", 1))
                        tt(act, ps[:, 3], gs, ALU.mult).then_inc(c.freed(("gu", 1), "act"), 1)
                        dve.wait_ge(S(c.last[0]), c.last_value())
                        dve.wait_ge(c.of("seatT"), c.at("seatT"))
                        v.tensor_copy(seatT, ps[:, 1, 0:NG * P].rearrange("p (g s) -> p g s", g=NG)).then_inc(c.freed(("seatT",), "seatTs"), 1)
                        dve.wait_ge(S(c.last[0]), c.last_value())
                        dve.wait_ge(c.of("yP", 1), c.at("yP", 1))
                        v.tensor_copy(ys[:, 1], ps[:, 3]).then_inc(c.freed(("yP", 1), "ys", 1), 1)
                        dve.wait_ge(S(c.last[0]), c.last_value())
                    led.where = "rounds"
                    ts(seatno[:], seatno[:], -float(SLOTS), None, ALU.add).then_inc(S("later_seats"), 1)
                    dve.wait_ge(S("later_seats"), r + 1)
                c.rounds = until
                led.where = "after"
                for g in range(NG):
                    for h in range(2):
                        sl = slice(h * BLK, (h + 1) * BLK)
                        dve.wait_ge(c.of("gateS", 1, g, h), c.at("gateS", 1, g, h))
                        dve.wait_ge(c.of("y", 2 * g + h), c.at("y", 2 * g + h))
                        tt(t1[:, 0:BLK], ps[:, 4 + 2 * g + h], gbuf2[:, g, sl], ALU.mult).then_inc(c.freed(("y", 2 * g + h)), 1)
                        dve.wait_ge(S(c.last[0]), c.last_value())
                        lab = ("x2", g) if h else ()
                        st(tt(x[:, g, sl], x[:, g, sl], t1[:, 0:BLK], ALU.add), *lab)

        @block.scalar
        def _(acte):
            c = Counts(led, S)
            led.where = "start"

            def st(ins, *label):
                ins.then_inc(c.makes(*(label or ("act_step",))), 1)
                acte.wait_ge(S(c.last[0]), c.last_value())

            act_ = nc.scalar.activation

            def ex_(out, in_, scale=1.0, **k):
                return act_(out, in_, AF.Exp, scale=scale, **k)

            def rstd(g, cols_, n, label):
                a = stat[:, g, cols_]
                st(act_(a, a, AF.Ln, bias=epsc[:, 0:1], scale=1.0 / n))
                st(ex_(a, a, -0.5), *label)

            def evac(read, out, *label, fn=None):
                acte.wait_ge(c.of(*read), c.at(*read))
                b = c.bank(*read)
                src = ps[:, b]
                (nc.scalar.copy(out, src) if fn is None else fn(src)).then_inc(c.freed(read, *label), 1)
                acte.wait_ge(S(c.last[0]), c.last_value())

            for name in ("stored", "bias", "mixed", "x2"):
                acte.sem_inc(c.makes(name), 1)
            acte.wait_ge(c.of("start_dma"), c.at("start_dma"))
            acte.wait_ge(c.of("eps"), c.at("eps"))
            st(ex_(sile[:].rearrange("p g k -> p (g k)"), condT[:].rearrange("p g k -> p (g k)"), -1.0), "sile", 0)
            led.found[("sile",)] = led.found[("sile", 0)]
            acte.wait_ge(c.of("lbd", L - 1), c.at("lbd", L - 1))
            for l_ in range(L):
                st(ex_(lbin[:, l_], lbt[:, l_]), "lbe", l_)
            led.found[("lbe",)] = led.found[("lbe", L - 1)]
            with acte.Fori(0, L) as l:
                c.l = l
                acte.wait_ge(S("rounds"), l + 1)
                c.rounds = count_of_rounds(acte, l)
                led.where = "layer"

                def squares(stage):
                    for g in range(NG):
                        if stage == "xn1":
                            acte.wait_ge(S("x2"), c.value("x2", "layer", 0))
                        else:
                            acte.wait_ge(c.of("x1", g), c.at("x1", g))
                        st(act_(sq[:], x[:, g], AF.Square, accum_out=stat[:, g, 2:3]))
                        rstd(g, slice(2, 3), D, (stage + "r", g))

                acte.wait_ge(S("mixed"), c.value("mixed", "layer", 0))
                row = lambda name: ap[name][one(l)].rearrange("l n -> (l n)")
                rb = lambda name, a, n: ap[name][one(l), a:a + n].broadcast_to([P, n])
                bT = lambda r: r.rearrange("l (p k) -> p (l k)", k=KC)
                loads = [(nrmT[:, 0], bT(ap["norm_mix"][one(l)])), (nrmT[:, 1], bT(ap["norm_ffn"][one(l)]))]
                loads += [(wqk[:, 0], rb("da_qnorm", 0, DQ)), (wqk[:, 1], rb("da_knorm", 0, DQ)),
                          (lamp[:].rearrange("p a d -> p (a d)"), ap["da_lambda"].rearrange("l a d -> l (a d)")[one(l)].broadcast_to([P, 4 * DQ])),
                          (subln[:], rb("da_subln", 0, DV)), (rnorm[:], rb("ret_norm", 0, DR)), (hnorm[:], rb("hg_norm", 0, DR)),
                          (ctxk[:], ap["cache_k"][0].rearrange("l t h r d -> t l (h r d)")[:, one(l)].rearrange("t l n -> t (l n)")),
                          (ctxv[:], ap["cache_v"][0].rearrange("l t h d -> t l (h d)")[:, one(l)].rearrange("t l n -> t (l n)"))]
                dec = ap["ret_decay"].rearrange("l r h -> l (r h)")
                loads += [(rdec[:], dec[one(l)].broadcast_to([P, 2 * HR]))]
                for d in range(2):
                    q = slice(64 * d, 64 * d + 64)
                    loads += [(rdecH[q], dec[one(l), d * HR:(d + 1) * HR].broadcast_to([64, HR])),
                              (s0r[q], ap["state_ret"][0].rearrange("l r h d e -> r d l h e")[d, :, one(l)].rearrange("d l h e -> d (l h) e")),
                              (s0h[q], ap["state_hgrn"][0].rearrange("l r h d e -> r d l h e")[d, :, one(l)].rearrange("d l h e -> d (l h) e"))]
                for dst, src in loads:
                    acte.dma_start(dst, src).then_inc(S("params"), 16)
                led.made("params", ("params",), 16 * len(loads))

                def store(dst, src):
                    acte.dma_start(dst, src).then_inc(S("stored"), 16)
                    led.made("stored", ("stored",), 16)

                acte.wait_ge(c.of("params"), c.at("params"))
                acte.wait_ge(c.of("lamsum", 0), c.at("lamsum", 0))
                st(ex_(lam[:, 2:4], lam[:, 0:2]), "lamexp", 0)
                led.found[("lamexp",)] = led.found[("lamexp", 0)]
                st(ex_(rdec[:], rdec[:]))
                st(ex_(rdecH[:], rdecH[:]), "rdec", 0)
                led.found[("rdec",)] = led.found[("rdec", 0)]
                acte.wait_ge(c.of("rdecn", 0), c.at("rdecn", 0))
                acte.wait_ge(S("x2"), c.value("x2", "layer", 0))
                for d in range(2):
                    for h in range(HR):
                        lab = ("decT", 0) if (d and h == HR - 1) else ()
                        st(ex_(t1[:, h * P:(h + 1) * P] if d else decT[:, h], C["dist"][:, d * P:(d + 1) * P], rdec[:, d * HR + h:d * HR + h + 1]), *lab)
                led.found[("decT",)] = led.found[("decT", 0)]
                for h in range(HR):
                    st(ex_(decin[:, h], C["inpos"][:], rdecH[:, h:h + 1]), "decin", h)
                led.found[("decin",)] = led.found[("decin", HR - 1)]
                for d in range(2):
                    st(ex_(decend[:, :, d], rdec[:, d * HR:(d + 1) * HR], C["endpos"][:, d:d + 1]), "decend", d)
                led.found[("decend",)] = led.found[("decend", 1)]
                squares("xn1")
                acte.wait_ge(S("stored"), c.value("stored", "layer", 0))
                acte.wait_ge(S("bias"), c.value("bias", "layer", 0))
                for i in range(12):
                    vec, h = divmod(i, 2)
                    to = gateR[:, vec // 3] if vec % 3 == 2 else modR[:, (vec - vec // 3) * D:(vec - vec // 3 + 1) * D]
                    evac(("mod", i), to[:, h * BLK:(h + 1) * BLK], "modR", i)
                for i in range(12):
                    acte.wait_ge(c.of("modR", i), c.at("modR", i))
                rows = [(modR[NG:NG + 1, a * D:(a + 1) * D], vec) for a, vec in enumerate((0, 1, 3, 4))] + [(gateR[NG:NG + 1, a], vec) for a, vec in enumerate((2, 5))]
                for dst, vec in rows:
                    acte.dma_start(dst, ap["b_ada"][one(l), vec * D:(vec + 1) * D]).then_inc(S("bias"), 16)
                led.made("bias", ("bias",), 16 * len(rows))


                def shifted(stage, a):
                    acte.wait_ge(c.of("modS", 1), c.at("modS", 1))
                    for h in range(2):
                        acte.wait_ge(c.of(stage + "T", 1, h), c.at(stage + "T", 1, h))
                        b = c.bank(stage + "T", 1, h)
                        for k in range(4):
                            kc = 4 * h + k
                            ins = act_(hnT[:, kc, P:2 * P], ps[:, b, k * P:(k + 1) * P], AF.Identity, bias=modT[:, 2 * a, kc, 1:2], scale=modT[:, 2 * a + 1, kc, 1:2])
                        ins.then_inc(c.freed((stage + "T", 1, h), stage + "S", 1, h), 1)
                        acte.wait_ge(S(c.last[0]), c.last_value())

                shifted("hn1", 0)
                for i in range(N_IN):
                    n = min(BLK, D_IN - i * BLK)
                    evac(("projP", i, 1), None, "projS", i, 1, fn=lambda src: nc.scalar.copy(proj[:, 1, i * BLK:i * BLK + n], src[:, 0:n]))

                def square_of(read, n, label, g):
                    acte.wait_ge(c.of(*read), c.at(*read))
                    b = c.bank(*read)
                    st(act_(sq[:, 0:n], ps[:, b, 0:n], AF.Square), label + "q", g)
                    acte.wait_ge(c.of(label + "m", g), c.at(label + "m", g))
                    rstd(g, slice(16, 16 + n // 64), 64, (label + "r", g))

                for g in range(NG):
                    nk = 1 + g
                    acte.wait_ge(c.of("qkm", g), c.at("qkm", g))
                    rstd(g, slice(32, 64), DQ, ("qkr", g))
                    if not g:
                        acte.wait_ge(c.of("qkn", 0), c.at("qkn", 0))
                        acte.wait_ge(c.of("projS", 2, 0), c.at("projS", 2, 0))
                        store(ap["o_k"][0].rearrange("l t h r d -> t l (h r d)")[:, one(l)].rearrange("t l n -> t (l n)"), proj[:, 0, C_DAK:C_DAK + BLK])
                        store(ap["o_v"][0].rearrange("l t h d -> t l (h d)")[:, one(l)].rearrange("t l n -> t (l n)"), proj[:, 0, C_DAV:C_DAV + BLK])
                    evac(("dakT", g), None, "kT", g, fn=lambda src: nc.scalar.copy(kT[:, :, 0, :], src.rearrange("p (m t) -> p m t", m=4)))
                    if g:
                        evac(("ctxkT", g), None, "kTc", g, fn=lambda src: nc.scalar.copy(kT[:, :, 1, :], src.rearrange("p (m t) -> p m t", m=4)))
                    for hh in range(2):
                        acte.wait_ge(c.of("nmax", g, hh), c.at("nmax", g, hh))
                        for j in range(4):
                            for mi in range(2):
                                i = mi * 4 + j
                                ins = ex_(eP[:, hh, i, 0:nk * P], ps[:, 4 + j, mi * nk * P:(mi + 1) * nk * P], DQ ** -0.5, bias=rt[:, 2 * hh, 0, 8 + i:9 + i], accum_out=rt[:, 2 * hh + 1, 0, i:i + 1])
                            if j < 3:
                                ins.then_inc(c.freed(("score", g, hh, j)), 1)
                                acte.wait_ge(S(c.last[0]), c.last_value())
                            else:
                                ins.then_inc(c.freed(("score", g, hh, j), "expd", g, hh), 1)
                                acte.wait_ge(S(c.last[0]), c.last_value())
                    for hh in range(2):
                        for part in range(nk):
                            evac(("wPT", g, hh, part), None, "wT", g, hh, part, fn=lambda src: nc.scalar.copy(wT[:, hh, :, part, :], src.rearrange("p (m t) -> p m t", m=4)))
                    evac(("daoT", g), sq[:, BLK:D], "daoTs", g)
                    square_of(("dao", g), 512, "dao", g)
                    evac(("rqT", g), qw[:, 0], "rqTs", g)
                    evac(("roT", g), None, "roTs", g, fn=lambda src: nc.scalar.copy(sq[:, BLK:BLK + 256], src[:, 0:256]))
                    square_of(("ro", g), 256, "ro", g)
                    st(ex_(t4[:, 0:256], proj[:, g, C_RG:C_RG + 256], -1.0), "rge", g)
                    if not g:
                        evac(("rstate", g), None, "rstateS", fn=lambda src: nc.scalar.copy(stout[:, 0].rearrange("p h e -> p (h e)"), src[:, 0:256]))
                        for d in range(2):
                            store(ap["o_ret"][0].rearrange("l r h d e -> r d l h e")[d, :, one(l)].rearrange("d l h e -> d (l h) e"), stout[64 * d:64 * d + 64, 0])
                    acte.wait_ge(c.of("zc", g), c.at("zc", g))
                    st(ex_(t2[:], t2[:], -1.0), "ze", g)
                    acte.wait_ge(c.of("gatef", g), c.at("gatef", g))
                    st(act_(t3[:], t3[:], AF.Ln), "gln", g)
                    acte.wait_ge(c.of("rgdone", g), c.at("rgdone", g))
                    st(ex_(t4[:, 0:256], proj[:, g, C_GQ:C_GQ + 256], -1.0), "gqe", g)
                    evac(("hqT", g), qw[:, 0], "hqTs", g)
                    for lv in range(NLV + g):
                        if lv >= 2:
                            acte.wait_ge(c.of("qlv", g, lv - 2), c.at("qlv", g, lv - 2))
                            acte.wait_ge(c.of("klv", g, lv - 2), c.at("klv", g, lv - 2))
                        evac(("level", g, lv), None, "ex", g, lv, fn=lambda src: ex_(ex[:, lv % 2].rearrange("p h t -> p (h t)"), src))
                    if not g:
                        evac(("toend", g), None, "exend", g, fn=lambda src: ex_(t3[:], src))
                    evac(("hoT", g), None, "hoTs", g, fn=lambda src: nc.scalar.copy(sq[:, BLK:BLK + 256], src[:, 0:256]))
                    square_of(("ho", g), 256, "ho", g)
                    st(ex_(t4[:, 0:256], proj[:, g, C_GG:C_GG + 256], -1.0), "gge", g)
                    if not g:
                        evac(("hstate", g), None, "hstateS", fn=lambda src: nc.scalar.copy(stout[:, 1].rearrange("p h e -> p (h e)"), src[:, 0:256]))
                        for d in range(2):
                            store(ap["o_hg"][0].rearrange("l r h d e -> r d l h e")[d, :, one(l)].rearrange("d l h e -> d (l h) e"), stout[64 * d:64 * d + 64, 1])
                for h in range(2):
                    evac(("mixT", 1, h), None, "mixS", 1, h, fn=lambda src: nc.scalar.copy(hnT[:, 4 * h:4 * h + 4, P:2 * P], src.rearrange("p (k t) -> p k t", k=4)))
                for g in range(NG):
                    for h in range(2):
                        evac(("gateP", 0, g, h), gbuf1[:, g, h * BLK:(h + 1) * BLK], "gateS", 0, g, h)
                squares("xn2")
                shifted("hn2", 1)
                evac(("router",), None, "rexp", fn=lambda src: ex_(rt[:, 0].rearrange("p g e -> p (g e)"), src[:, 0:NG * NE], -1.0))
                acte.wait_ge(c.of("stored"), c.at("stored"))
                for g in range(NG):
                    evac(("rows", g, 0), xs[:, g, 0:BLK], "rowsS", g, 0)
                acte.wait_ge(S("rounds"), l + 2)
                until = count_of_rounds(acte, l + 1)
                with acte.Fori(c.rounds, until) as r:
                    with acte.Fori(0, TURNS) as t:
                        c.t = r * TURNS + t
                        led.where = "turn"
                        for half in range(2):
                            evac(("xT", half), None, "xTs", half, fn=lambda src: nc.scalar.copy(xT[:, KH * half:KH * (half + 1), :], src.rearrange("p (k s) -> p k s", k=KH)))
                        acte.wait_ge(c.of("gu", 0), c.at("gu", 0))
                        st(ex_(ge, ps[:, 2], -1.0), "gexp")
                        evac(("actT",), None, "actTs", fn=lambda src: nc.scalar.copy(actT, src.rearrange("p (k s) -> p k s", k=KE)))
                        evac(("yP", 0), ys[:, 0], "ys", 0)
                c.rounds = until
                led.where = "after"
                for g in range(NG):
                    for h in range(2):
                        evac(("gateP", 1, g, h), gbuf2[:, g, h * BLK:(h + 1) * BLK], "gateS", 1, g, h)
            led.where = "end"
            acte.wait_ge(S("x2"), 1 + NG * L)
            acte.dma_start(ap["o_yp"][0], x[:, 0]).then_inc(S("stored"), 16)
            acte.dma_start(ap["o_ys"][0], x[:, 1]).then_inc(S("stored"), 16)
            acte.wait_ge(S("stored"), 1 + L * led.totals.get(("stored", "layer"), 0) + 32)

        @block.gpsimd
        def _(pool):
            c = Counts(led, S)
            led.where = "start"
            g_ = nc.gpsimd
            bc = lambda a: a.rearrange("(o n) -> o n", o=1).broadcast_to([P, a.shape[0]])
            starts = [(x[:, 0], ap["x_prompt"][0]), (x[:, 1], ap["x_sample"][0])]
            starts += [(C[n][:], io["cap"][n]) for n in io["consts"]]
            starts += [(condT[:, 0], ap["c_ctx"].rearrange("(p k) -> p k", k=KC)),
                       (condT[:, 1], ap["c"][0].rearrange("(p k) -> p k", k=KC)),
                       (wrt[:], ap["w_router"].rearrange("(p k) e -> p k e", k=KC)),
                       (rbias[:], bc(ap["router_bias"]))]
            starts += [(lbin[:, l_], bc(ap["hg_lb"][l_])) for l_ in range(L)]
            for dst, src in starts:
                pool.dma_start(dst, src).then_inc(S("start_dma"), 16)
            led.made("start_dma", ("start_dma",), 16 * len(starts))
            with pool.Fori(0, L) as l:
                c.l = l
                pool.wait_ge(S("rounds"), l + 1)
                c.rounds = count_of_rounds(pool, l)
                led.where = "layer"
                def scaled_keys(g):
                    for lv in range(NLV):
                        pool.wait_ge(c.of("hkTs", g), c.at("hkTs", g))
                        pool.wait_ge(c.of("ex", g, lv), c.at("ex", g, lv))
                        if lv >= 2:
                            pool.wait_ge(c.of("hS", g, lv - 2, 1), c.at("hS", g, lv - 2, 1))
                        g_.tensor_tensor(klv[:, lv % 2], hkT, ex[:, lv % 2], ALU.mult).then_inc(c.makes("klv", g, lv), 1)
                        pool.wait_ge(S(c.last[0]), c.last_value())

                scaled_keys(0)
                scaled_keys(1)
                led.where = "after"
    return dict(led.count), dict(led.found)


_INS = ["x_prompt", "x_sample", "cache_k", "cache_v", "state_ret", "state_hgrn", "c", "c_ctx", "w_in", "w_out", "w_ada", "b_ada",
        "norm_mix", "norm_ffn", "da_qnorm", "da_knorm", "da_lambda", "da_subln", "ret_decay", "ret_norm", "hg_lb", "hg_norm",
        "w_router", "router_bias", "w_gate", "w_up", "w_down"]
_OUTS = [("o_yp", (1, P, D)), ("o_ys", (1, P, D)), ("o_k", (1, L, P, NH, 2, DQ)), ("o_v", (1, L, P, NH, DV)),
         ("o_ret", (1, L, 2, HR, DR, DR)), ("o_hg", (1, L, 2, HR, DR, DR))]


def kernel(**inputs):
    import concourse.bacc as bacc
    from concourse.bass_utils import run_bass_kernel_spmd

    arrays = {"in_" + n: np.ascontiguousarray(inputs[n]) for n in _INS}
    consts = host_constants()
    arrays.update({"const_" + n: a for n, a in consts.items()})
    known = None
    for _ in range(3):
        nc = bacc.Bacc("TRN2", target_bir_lowering=False, num_devices=1)
        dram = {n: nc.dram_tensor(n, a.shape, mybir.dt.from_np(a.dtype), kind="ExternalInput").ap() for n, a in arrays.items()}
        outs = {n: nc.dram_tensor("out_" + n, shape, mybir.dt.float32, kind="ExternalOutput").ap() for n, shape in _OUTS}
        aps = {n: dram["in_" + n] for n in _INS}
        aps.update(outs)
        io = {"ap": aps, "consts": consts, "cap": {n: dram["const_" + n] for n in consts}}
        known = build(nc, io, known)
    r = run_bass_kernel_spmd(nc, [arrays], core_ids=[0])
    return tuple(r.results[0]["out_" + n] for n, _ in _OUTS)
```

```python
import math
from contextlib import ExitStack

import numpy as np
import concourse.bass as bass
from concourse import mybir
from concourse.alu_op_type import AluOpType as ALU

P = 128
D = 1024
KC = D // P
L = 2
NG = 2
D_IN = 3840
NH, DQ, DV = 8, 32, 64
HR, DR = 4, 64
NE, DE = 16, 512
KE = DE // P
SLOTS = 64
EPS = 1e-6
C_DAQ, C_DAK, C_DAV = 0, 512, 1024
C_RQ, C_RK, C_RV, C_RG = 1536, 1792, 2048, 2304
C_GQ, C_GFF, C_GFB, C_GI, C_GG = 2560, 2816, 3072, 3328, 3584
LEVELS = (64, 32, 16, 8, 4, 2, 1)
NLV = len(LEVELS)
RING = 6
KH = KC // 2
BLK = 512
N_IN = (D_IN + BLK - 1) // BLK
FAR = 1024.0
N_MOD1 = 2 * D // BLK
IN_ORDER = (0, 4, 5, 6, 7, 1, 2, 3)
LN_LOW = 2.0 ** -60
GRID_W = 64


def host_constants():
    t = np.arange(P)
    c = {}
    c["ident"] = np.eye(P)
    masks = []
    for b in LEVELS:
        pair = (t[:, None] // (2 * b)) == (t[None, :] // (2 * b))
        fwd = pair & (t[:, None] // b % 2 == 0) & (t[None, :] // b % 2 == 1)
        masks += [fwd, fwd.T]
    c["masks"] = np.stack(masks, 1).reshape(P, -1)
    steps = []
    for b in LEVELS:
        fwd, bwd = np.zeros((P, P)), np.zeros((P, P))
        for i in t:
            base = i - i % (2 * b)
            mid, end = base + b, base + 2 * b
            if i >= mid:
                fwd[mid:i + 1, i] = 1
                bwd[mid:i, i] = 1
            else:
                fwd[i + 1:mid, i] = 1
                bwd[i:mid, i] = 1
        steps += [fwd, bwd]
    u, i = t[:, None], t[None, :]
    steps += [u <= i, u >= i]
    steps += [u > i, u < i]
    c["steps"] = np.stack(steps, 1).reshape(P, -1)
    c["dist"] = np.stack([np.maximum(i - u, 0), np.maximum(u - i, 0)], 1).reshape(P, -1)
    c["inpos"] = np.where(u < 64, i + 1, P - i) * np.ones((P, P))
    c["endpos"] = np.stack([P - 1 - t, t], 1)
    c["quarter"] = (t[:, None] // DQ == np.arange(4)[None, :])
    c["pick"] = np.stack([((u % 32 == g) | (u == NG)) * np.ones((P, P)) for g in range(NG)], 1).reshape(P, -1)
    c["pick2"] = (t[:, None] % 32 == np.arange(NG)[None, :]) | (t[:, None] == NG)
    rows = P // GRID_W
    inv = 10000.0 ** (-np.arange(DQ // 4) / (DQ // 4))
    ang = np.concatenate([np.repeat(np.arange(rows), GRID_W)[:, None] * inv, np.tile(np.arange(GRID_W), rows)[:, None] * inv], -1)
    c["cos"] = np.repeat(np.cos(ang), 2, axis=1)
    sn = np.sin(ang)
    c["sin"] = np.stack([-sn, sn], -1).reshape(P, DQ)
    c["slot"] = np.tile(np.arange(SLOTS)[None], (P, 1))
    c["rank4"] = np.tile(np.arange(4, 0, -1)[None], (P, 1))
    c["rank16"] = np.tile(np.arange(NE, 0, -1)[None], (P, 1))
    li = [0.8 - 0.6 * math.exp(-0.3 * l) for l in range(L)]
    c["lami"] = np.tile(np.array([[a, 1.0 - a] for a in li]).reshape(1, -1), (P, 1))
    return {k: np.ascontiguousarray(v, dtype=np.float32) for k, v in c.items()}


class Ledger:

    def __init__(self, known):
        self.totals, self.labels = known or ({}, {})
        self.count, self.found, self.where = {}, {}, "start"

    def made(self, sem, label=None, n=1):
        key = (sem, self.where)
        self.count[key] = self.count.get(key, 0) + n
        if label is not None:
            self.found[label] = (sem, self.where, self.count[key])
        return self.where, self.count[key]

    def value(self, sem, where, n, layer, rounds, turn):
        t = {w: self.totals.get((sem, w), 0) for w in ("start", "layer", "turn", "after")}
        if where == "start":
            return n
        v = n + t["start"]
        if t["layer"] + t["after"]:
            v = layer * (t["layer"] + t["after"]) + v
        if where != "layer":
            v = v + t["layer"]
        if t["turn"]:
            v = (turn if where == "turn" else rounds * TURNS) * t["turn"] + v
        return v


TURNS = NE // 2


class Counts:

    def __init__(self, led, sem):
        self.led, self.sem, self.l, self.rounds, self.t = led, sem, 0, 0, 0
        self.last = None

    def value(self, sem, where, n):
        return self.led.value(sem, where, n, self.l, self.rounds, self.t)

    def of(self, *label):
        if label not in self.led.labels:
            self.led.found.setdefault("missing", set()).add(label)
        return self.sem(self.led.labels.get(label, ("none",))[0])

    def at(self, *label):
        sem, where, n = self.led.labels.get(label, ("none", "start", 1))
        return self.value(sem, where, n)

    def makes(self, *label):
        self.last = (label[0], *self.led.made(label[0], label))
        return self.sem(label[0])

    def last_value(self):
        return self.value(*self.last)

    def claim(self, b):
        where, n = self.led.made(f"bank{b}_claim")
        t = self.led.totals
        for w in ("layer", "turn", "after"):
            t[(f"bank{b}_free", w)] = t.get((f"bank{b}_full", w), 0)
        return self.value(f"bank{b}_free", where, n - 1)

    def fills(self, b, *label):
        self.led.made(f"bank{b}_full", label)
        return self.sem(f"bank{b}_full")

    def freed(self, read, *label):
        sem, where, n = self.led.labels.get(read, ("bank0_full", "start", 1))
        sem = sem.replace("_full", "_free")
        if label:
            self.led.found[label] = (sem, where, n)
        self.last = (sem, where, n)
        return self.sem(sem)

    def bank(self, *read):
        return int(self.led.labels.get(read, ("bank0_full",))[0][4])

    def loads(self, s):
        where, n = self.led.made(f"slot{s}_turn")
        t = self.led.totals
        for w in ("start", "layer", "turn", "after"):
            t[(f"slot{s}_loaded", w)] = 16 * t.get((f"slot{s}_turn", w), 0)
        return self.value(f"slot{s}_loaded", where, 16 * n)


def build(nc, io, known):
    f32 = mybir.dt.float32
    AF = mybir.ActivationFunctionType
    AX = mybir.AxisListType.X
    led = Ledger(known)
    ap = io["ap"]
    v = nc.vector
    with ExitStack() as ctx:
        sems = {}

        def S(name):
            if name not in sems:
                sems[name] = ctx.enter_context(nc.semaphore(name))
            return sems[name]

        def sb(name, *shape):
            return ctx.enter_context(nc.sbuf_tensor(name, [P, *shape], f32))

        ps = ctx.enter_context(nc.psum_tensor("ps", [P, 8, BLK], f32))

        ring = sb("ring", RING, KH, BLK)
        x = sb("x", NG, D)
        proj = sb("proj", NG, D_IN)
        xs = sb("xs", NG, D)
        hnT = sb("hnT", KC, NG * P)
        gateR = sb("gateR", 2, D)
        modT = sb("modT", 4, KC, NG)
        C = {n: sb("c_" + n, a.shape[1]) for n, a in io["consts"].items()}
        condT, silT, sile = sb("condT", NG, KC), sb("silT", KC, 32), sb("sile", NG, KC)
        lbt, oml = sb("lbt", L, 256), sb("oml", 256)
        epsc = sb("epsc", 1)
        nrmT, badaT = sb("nrmT", 2, KC), sb("badaT", 4, KC)
        wqk, lamp = sb("wqk", 2, DQ), sb("lamp", 4, DQ)
        subln, rnorm, hnorm = sb("subln", DV), sb("rnorm", DR), sb("hnorm", DR)
        rdec, rdecH = sb("rdec", 2 * HR), sb("rdecH", HR)
        ctxk, ctxv = sb("ctxk", BLK), sb("ctxv", BLK)
        s0r, s0h = sb("s0r", HR, DR), sb("s0h", HR, DR)
        wrt, rbias = sb("wrt", KC, NE), sb("rbias", NE)
        lam, lams = sb("lam", 8), sb("lams", 2)
        decT, decin, decend = sb("decT", HR, P), sb("decin", HR, P), sb("decend", HR, 2)
        stat = sb("stat", NG, 64)
        sq, t1, t2, t3, t4 = sb("sq", D), sb("t1", D), sb("t2", BLK), sb("t3", BLK), sb("t4", BLK)
        oT = sq[:, BLK:D].rearrange("p (m t) -> p m t", t=P)
        qw, kT = sb("qw", 4, 4 * P), sb("kT", 4, 2, P)
        qTm = qw[:].rearrange("p j (m t) -> p j m t", m=4)
        wT = qw[:].rearrange("p (hh u) (v t) -> p hh (u v) t", hh=2, t=P).rearrange("p hh (hd part) t -> p hh hd part t", part=2)
        rqT, rkT, rqi = (qw[:, i].rearrange("p (h t) -> p h t", h=HR) for i in range(3))
        hqT, hkT, hqi = rqT, rkT, rqi
        rA = qw[:, 3].rearrange("p (h t) -> p h t", h=HR)
        kf = kT[:].rearrange("p m r t -> p (m r t)")
        rq2, rk2 = (kf[:, i * BLK:(i + 1) * BLK].rearrange("p (h r d) -> p h r d", h=HR, r=2) for i in range(2))
        hq2 = rq2
        eP = sb("eP", 2, 8, 2 * P)
        ef = eP[:].rearrange("p a b c -> p (a b c)")
        A = ef[:, 0:4 * BLK].rearrange("p (z r h t) -> p z r h t", z=2, r=2, h=HR)
        lbin = ef[:, 0:BLK].rearrange("p (l n) -> p l n", l=L)
        modR = ef[:, 0:4 * D]
        gbuf1 = ef[:, 0:NG * D].rearrange("p (g n) -> p g n", g=NG)
        wP = hnT[:].rearrange("p k t -> p (k t)").rearrange("p (hh hd t) -> p hh hd t", hh=2, hd=4)
        rkd = sb("rkd", HR, 2, DR)
        hkd = rkd
        qlv, klv = sb("qlv", 2, HR, P), sb("klv", 2, HR, P)
        ex = sb("ex", 2, HR, P)
        stout = sb("stout", 2, HR, DR)
        gt, seatno = sb("gt", NG, NE), sb("seatno", NG, NE)
        need = sb("need", 8)
        roundsf = sb("roundsf", L + 1)
        roundsi = ctx.enter_context(nc.sbuf_tensor("roundsi", [P, L + 1], mybir.dt.int32))
        rt = sb("rt", 14, NG, NE)
        pf = proj[:].rearrange("p g n -> p (g n)")
        ge, gs, act = (pf[:, i * BLK:(i + 1) * BLK] for i in range(3))
        actT = pf[:, 3 * BLK:4 * BLK].rearrange("p (k s) -> p k s", k=KE)
        xT = pf[:, 4 * BLK:6 * BLK].rearrange("p (k s) -> p k s", k=KC)
        ys = pf[:, 6 * BLK:8 * BLK].rearrange("p (h n) -> p h n", h=2)
        seat, seatG, seatT = (pf[:, 6 * D + i * NG * P:6 * D + (i + 1) * NG * P].rearrange("p (g s) -> p g s", g=NG) for i in range(3))
        rows = xs[:].rearrange("p g (k q) -> p g k q", k=KC)
        gbuf2 = pf[:, 4 * D:6 * D].rearrange("p (g n) -> p g n", g=NG)
        hk = [proj[:, g, C_GFF:C_GFF + BLK].rearrange("p (h r d) -> p h r d", h=HR, r=2) for g in range(NG)]
        laf = (t2, t3)
        la = [a[:].rearrange("p (r h d) -> p r h d", r=2, h=HR) for a in laf]
        spare = {"rg": ex[:, 0], "gq": ex[:, 1], "gg": klv[:, 0]}
        spare = {n: a.rearrange("p h (u t) -> p (h u t)", u=2).rearrange("p (g n) -> p g n", g=NG) for n, a in spare.items()}
        zexp = [qlv[:, g].rearrange("p h t -> p (h t)") for g in range(NG)]
        zero = t2

        w_in = ap["w_in"].rearrange("l (p k) n -> p l k n", k=KC)
        w_ada = ap["w_ada"].rearrange("l (p k) n -> p l k n", k=KC)
        w_out = ap["w_out"].rearrange("l (p k) n -> p l k n", k=KC)
        w_gate = ap["w_gate"].rearrange("l e (p k) f -> p (l e) k f", k=KC)
        w_up = ap["w_up"].rearrange("l e (p k) f -> p (l e) k f", k=KC)
        w_down = ap["w_down"].rearrange("l e (p k) d -> p (l e) k d", k=KE)

        block = ctx.enter_context(nc.Block())

        def one(i):
            return bass.ds(i, 1)

        def count_of_rounds(e, i):
            e.sem_inc(S("rounds_seen"), 1)
            return e.value_load(roundsi[0:1, one(i)], min_val=0, max_val=4 * L)

        @block.sync
        def _(sp):
            c = Counts(led, S)
            led.where = "start"
            n_loads = [0]
            for s in range(RING):
                sp.sem_inc(c.makes(f"slot{s}_used"), 1)

            def load(dst_cols, src):
                s = n_loads[0] % RING
                n_loads[0] += 1
                where, n = led.made(f"slot{s}_load")
                t = led.totals
                for w in ("layer", "turn", "after"):
                    t[(f"slot{s}_used", w)] = t.get((f"slot{s}_load", w), 0)
                sp.wait_ge(S(f"slot{s}_used"), c.value(f"slot{s}_used", where, n - 1))
                sp.dma_start(dst_cols(s), src).then_inc(S(f"slot{s}_loaded"), 16)

            with sp.Fori(0, L) as l:
                c.l = l
                sp.wait_ge(S("rounds"), l + 1)
                c.rounds = count_of_rounds(sp, l)
                led.where = "layer"
                def load_ada(i):
                    for r in range(2):
                        load(lambda s: ring[:, s:s + 1], w_ada[:, one(l), KH * r:KH * (r + 1), i * BLK:(i + 1) * BLK])

                for i in range(N_MOD1):
                    load_ada(i)
                for nth, i in enumerate(IN_ORDER):
                    n = min(BLK, D_IN - i * BLK)
                    for r in range(2):
                        load(lambda s: ring[:, s:s + 1, :, 0:n], w_in[:, one(l), KH * r:KH * (r + 1), i * BLK:i * BLK + n])
                    load_ada(N_MOD1 + nth)
                for i in range(4):
                    for r in range(2):
                        load(lambda s: ring[:, s:s + 1, :, 0:256], w_out[:, one(l), KH * r:KH * (r + 1), i * 256:(i + 1) * 256])
                until = sp.alloc_register("rounds_until")
                with sp.Fori(c.rounds, until) as r:
                    with sp.Fori(0, TURNS) as t:
                        c.t = r * TURNS + t
                        led.where = "turn"
                        for w in (w_gate, w_up):
                            for half in range(2):
                                for e in range(2):
                                    load(lambda s: ring[:, s:s + 1], w[:, one(l * NE + t * 2 + e), KH * half:KH * (half + 1)])
                        for h in range(2):
                            for e in range(2):
                                load(lambda s: ring[:, s:s + 1], w_down[:, one(l * NE + t * 2 + e), :, h * BLK:(h + 1) * BLK])
                    led.where = "rounds"
                    sp.wait_ge(S("rounds"), l + 2)
                    sp.sem_inc(S("rounds_seen"), 1)
                    sp.reg_load(until, roundsi[0:1, one(l + 1)])
                led.where = "after"

        @block.tensor
        def _(pe):
            c = Counts(led, S)
            led.where = "start"
            n_slots, n_tr, owed = [0], [0], []

            def mm(*a, **k):
                ins = nc.tensor.matmul(*a, **k)
                return ins

            def pay(ins):
                if owed:
                    ins.then_inc(S(f"slot{owed.pop(0)}_used"), 1)
                return ins

            def slot():
                s = n_slots[0] % RING
                n_slots[0] += 1
                pe.wait_ge(S(f"slot{s}_loaded"), c.loads(s))
                return s

            def sweep(out, lhs, rhs, n, free_group=False):
                for k in range(n):
                    last = mm(out, lhs(k), rhs(k), start=(k == 0), stop=(k == n - 1), skip_group_check=free_group)
                    if k < n - 1:
                        pay(last)
                return last

            def step_pattern(i, d):
                return C["steps"][:, (2 * i + d) * P:(2 * i + d + 1) * P]

            def bank_of_transposes(label, sources, b=None):
                if b is None:
                    b = n_tr[0] % 2
                    n_tr[0] += 1
                pe.wait_ge(S(f"bank{b}_free"), c.claim(b))
                for i, src in enumerate(sources):
                    last = nc.tensor.transpose(ps[:, b, i * P:(i + 1) * P], src, C["ident"][:])
                    if i < len(sources) - 1:
                        pay(last)
                last.then_inc(c.fills(b, *label), 1)

            def by_feature(stage, rows):
                transposed(stage, rows)
                copied(stage)

            def transposed(stage, rows):
                for g in range(NG):
                    pe.wait_ge(c.of(rows, g), c.at(rows, g))
                    xv = xs[:, g].rearrange("p (q k) -> p k q", k=KC)
                    for h in range(2):
                        bank_of_transposes((stage + "T", g, h), [xv[:, 4 * h + k, :] for k in range(4)])

            def copied(stage):
                for g in range(NG):
                    for h in range(2):
                        pe.wait_ge(c.of(stage + "S", g, h), c.at(stage + "S", g, h))

            for b in range(8):
                pe.sem_inc(c.makes(f"bank{b}_free"), 1)
            pe.wait_ge(c.of("silT"), c.at("silT"))
            with pe.Fori(0, L) as l:
                c.l = l
                pe.wait_ge(S("rounds"), l + 1)
                c.rounds = count_of_rounds(pe, l)
                led.where = "layer"
                def modulation(i, b):
                    pe.wait_ge(S(f"bank{b}_free"), c.claim(b))
                    for r in range(2):
                        s = slot()
                        for j in range(4):
                            last = mm(ps[32 * j:32 * j + 32, b, :], silT[:, KH * r + j, :], ring[:, s, j, :], start=(r == 0), stop=(r == 1))
                            if not (r and j == 3):
                                pay(last)
                        owed.append(s)
                    last.then_inc(c.fills(b, "mod", i), 1)

                def modulation_by_feature(norm):
                    pe.wait_ge(c.of("modR", 2 * norm), c.at("modR", 2 * norm))
                    pe.wait_ge(c.of("modR", 2 * norm + 1), c.at("modR", 2 * norm + 1))
                    pe.wait_ge(S(f"bank{0}_free"), c.claim(0))
                    for a in range(2):
                        mv = modR[:, (2 * norm + a) * D:(2 * norm + a + 1) * D].rearrange("p (q k) -> p k q", k=KC)
                        for k in range(KC):
                            at = (a * KC + k) * NG
                            last = mm(ps[:, 0, at:at + NG], mv[:, k, :], C["pick2"][:], start=True, stop=True)
                            if k < 7:
                                pay(last)
                    last.then_inc(c.fills(0, "modT", norm), 1)

                modulation(0, 4)
                modulation(1, 5)
                pe.wait_ge(c.of("begin_dma"), c.at("begin_dma"))
                transposed("hn1", "xn1")
                modulation(2, 6)
                modulation(3, 7)
                modulation_by_feature(0)

                def spread_gate(a):
                    for g in range(NG):
                        for h in range(2):
                            b = 2 * g + h
                            pe.wait_ge(S(f"bank{b}_free"), c.claim(b))
                            last = mm(ps[:, b, :], C["pick"][:, g * P:(g + 1) * P], gateR[:, a, h * BLK:(h + 1) * BLK], start=True, stop=True)
                            last.then_inc(c.fills(b, "gateP", a, g, h), 1)

                pe.wait_ge(c.of("later_dma"), c.at("later_dma"))
                for g in range(NG):
                    pe.wait_ge(c.of(f"hn1S{g}", 1), c.at(f"hn1S{g}", 1))
                nb = 0
                for nth, i in enumerate(IN_ORDER):
                    ss = [slot(), slot()]
                    n = min(BLK, D_IN - i * BLK)
                    for g in range(NG):
                        b = 2 + nb % 6
                        nb += 1
                        pe.wait_ge(S(f"bank{b}_free"), c.claim(b))
                        last = sweep(ps[:, b, 0:n], lambda k: hnT[:, k, g * P:(g + 1) * P], lambda k: ring[:, ss[k // KH], k % KH, 0:n], KC)
                        last.then_inc(c.fills(b, "projP", i, g), 1)
                    owed.extend(ss)
                    modulation(N_MOD1 + nth, nth % 2)
                modulation_by_feature(1)

                pe.wait_ge(c.of("params"), c.at("params"))
                for g in range(NG):
                    nk = 1 + g
                    pe.wait_ge(c.of("qkn", g), c.at("qkn", g))
                    bank_of_transposes(("daqT", g), [proj[:, g, C_DAQ + m * P:C_DAQ + (m + 1) * P] for m in range(4)])
                    bank_of_transposes(("dakT", g), [proj[:, g, C_DAK + m * P:C_DAK + (m + 1) * P] for m in range(4)])
                    if g:
                        bank_of_transposes(("ctxkT", g), [ctxk[:, m * P:(m + 1) * P] for m in range(4)])
                    pe.wait_ge(c.of("qTm", g), c.at("qTm", g))
                    pe.wait_ge(c.of("kT", g), c.at("kT", g))
                    if g:
                        pe.wait_ge(c.of("kTc", g), c.at("kTc", g))
                    for hh in range(2):
                        for j in range(4):
                            pe.wait_ge(S(f"bank{4 + j}_free"), c.claim(4 + j))
                            for mi in range(2):
                                m = 2 * hh + mi
                                last = mm(ps[:, 4 + j, mi * nk * P:(mi + 1) * nk * P], qTm[:, j, m, :], kT[:, m, 0:nk, :].rearrange("p a t -> p (a t)"), start=True, stop=True)
                            last.then_inc(c.fills(4 + j, "score", g, hh, j), 1)
                    for hh in range(2):
                        pe.wait_ge(c.of("wP", g, hh), c.at("wP", g, hh))
                        for part in range(nk):
                            bank_of_transposes(("wPT", g, hh, part), [wP[:, hh, hd, part * P:(part + 1) * P] for hd in range(4)])
                        if hh == 0:
                            pe.wait_ge(S(f"bank{2}_free"), c.claim(2))
                        for part in range(nk):
                            pe.wait_ge(c.of("wT", g, hh, part), c.at("wT", g, hh, part))
                        for hd in range(4):
                            h = 4 * hh + hd
                            dst = ps[64 * (h % 2):64 * (h % 2) + 64, 2, (h // 2) * P:(h // 2 + 1) * P]
                            for part in range(nk):
                                val = ctxv[:, h * DV:(h + 1) * DV] if part else proj[:, g, C_DAV + h * DV:C_DAV + (h + 1) * DV]
                                last = mm(dst, val, wT[:, hh, hd, part, :], start=(part == 0), stop=(part == nk - 1), skip_group_check=True)
                    last.then_inc(c.fills(2, "daoT", g), 1)
                    pe.wait_ge(c.of("daoTs", g), c.at("daoTs", g))
                    bank_of_transposes(("dao", g), [oT[:, m, :] for m in range(4)], 3)

                    pe.wait_ge(c.of("rk2", g), c.at("rk2", g))
                    bank_of_transposes(("rqT", g), [rq2[:, h].rearrange("p r d -> p (r d)") for h in range(HR)])
                    bank_of_transposes(("rkT", g), [rk2[:, h].rearrange("p r d -> p (r d)") for h in range(HR)])
                    pe.wait_ge(c.of("rqTs", g), c.at("rqTs", g))
                    pe.wait_ge(c.of("rkTs", g), c.at("rkTs", g))
                    pe.wait_ge(S(f"bank{2}_free"), c.claim(2))
                    for h in range(HR):
                        last = mm(ps[:, 2, h * P:(h + 1) * P], rkT[:, h, :], rqT[:, h, :], start=True, stop=True)
                    last.then_inc(c.fills(2, "rS", g), 1)
                    pe.wait_ge(c.of("rA", g), c.at("rA", g))
                    if g:
                        pe.wait_ge(c.of("rqi", g), c.at("rqi", g))
                    pe.wait_ge(S(f"bank{3}_free"), c.claim(3))
                    for h in range(HR):
                        dst = ps[64 * (h % 2):64 * (h % 2) + 64, 3, (h // 2) * P:(h // 2 + 1) * P]
                        last = mm(dst, proj[:, g, C_RV + h * DR:C_RV + (h + 1) * DR], rA[:, h, :], start=True, stop=not g, skip_group_check=True)
                        if g:
                            last = mm(dst, s0r[:, h, :], rqi[:, h, :], start=False, stop=True, skip_group_check=True)
                    last.then_inc(c.fills(3, "roT", g), 1)
                    pe.wait_ge(c.of("roTs", g), c.at("roTs", g))
                    bank_of_transposes(("ro", g), [oT[:, m, :] for m in range(2)], 2)
                    if not g:
                        pe.wait_ge(c.of("rkd", g), c.at("rkd", g))
                        pe.wait_ge(S(f"bank{3}_free"), c.claim(3))
                        for h in range(HR):
                            last = mm(ps[:, 3, h * DR:(h + 1) * DR], rkd[:, h].rearrange("p r d -> p (r d)"), proj[:, g, C_RV + h * DR:C_RV + (h + 1) * DR], start=True, stop=True)
                        last.then_inc(c.fills(3, "rstate", g), 1)

                    pe.wait_ge(c.of("hk", g), c.at("hk", g))
                    pe.wait_ge(c.of("hq2", g), c.at("hq2", g))
                    bank_of_transposes(("hqT", g), [hq2[:, h].rearrange("p r d -> p (r d)") for h in range(HR)])
                    bank_of_transposes(("hkT", g), [hk[g][:, h].rearrange("p r d -> p (r d)") for h in range(HR)])
                    pe.wait_ge(c.of("la", g), c.at("la", g))
                    def decays(lv):
                        b = 4 + lv % 2
                        pe.wait_ge(S(f"bank{b}_free"), c.claim(b))
                        for h in range(HR):
                            for d in range(2):
                                last = mm(ps[64 * d:64 * d + 64, b, h * P:(h + 1) * P], la[g][:, d, h, :], C["steps"][:, (2 * lv + d) * P:(2 * lv + d + 1) * P], start=True, stop=True)
                        last.then_inc(c.fills(b, "level", g, lv), 1)
                    decays(0)
                    decays(1)
                    if not g:
                        pe.wait_ge(S(f"bank{6}_free"), c.claim(6))
                        for d in range(2):
                            at = (2 * (NLV + 1) + d) * P
                            last = mm(ps[:, 6, d * 256:(d + 1) * 256], C["steps"][:, at:at + P], la[g][:, d].rearrange("p h d -> p (h d)"), start=True, stop=True)
                        last.then_inc(c.fills(6, "toend", g), 1)
                    pe.wait_ge(c.of("hqTs", g), c.at("hqTs", g))
                    pe.wait_ge(c.of("hkTs", g), c.at("hkTs", g))
                    def scores(lv):
                        if lv >= 0:
                            pe.wait_ge(c.of("klv", g, lv), c.at("klv", g, lv))
                            pe.wait_ge(c.of("qlv", g, lv), c.at("qlv", g, lv))
                        for r in range(2 if lv >= 0 else 1):
                            pe.wait_ge(S(f"bank{2 + r}_free"), c.claim(2 + r))
                            q = slice(64 * r, 64 * r + 64)
                            for h in range(HR):
                                k_, q_ = (klv[q, lv % 2, h, :], qlv[q, lv % 2, h, :]) if lv >= 0 else (hkT[:, h, :], hqT[:, h, :])
                                last = mm(ps[:, 2 + r, h * P:(h + 1) * P], k_, q_, start=True, stop=True)
                            last.then_inc(c.fills(2 + r, "hS", g, lv, r), 1)

                    def head(h):
                        return ps[64 * (h % 2):64 * (h % 2) + 64, 7, (h // 2) * P:(h // 2 + 1) * P]

                    def values(lv):
                        for r in range(2 if lv >= 0 else 1):
                            pe.wait_ge(c.of("hA", g, lv, r), c.at("hA", g, lv, r))
                            for h in range(HR):
                                end = not g and lv == NLV - 1 and r == 1
                                last = mm(head(h), proj[:, g, C_GI + h * DR:C_GI + (h + 1) * DR], A[:, lv % 2, r, h, :], start=(lv < 0 and h < 2), stop=end, skip_group_check=True)
                        if lv < NLV - 1:
                            last.then_inc(c.makes("hV", g, lv), 1)
                        return last

                    scores(-1)
                    scores(0)
                    decays(2)
                    pe.wait_ge(S(f"bank{7}_free"), c.claim(7))
                    for lv in range(-1, NLV):
                        last = values(lv)
                        if lv + 2 < NLV:
                            scores(lv + 2)
                        if lv + 4 < NLV + g:
                            decays(lv + 4)
                    if g:
                        pe.wait_ge(c.of("hqi", g), c.at("hqi", g))
                        for h in range(HR):
                            last = mm(head(h), s0h[:, h, :], hqi[:, h, :], start=False, stop=True, skip_group_check=True)
                    last.then_inc(c.fills(7, "hoT", g), 1)
                    pe.wait_ge(c.of("hoTs", g), c.at("hoTs", g))
                    bank_of_transposes(("ho", g), [oT[:, m, :] for m in range(2)], 2)
                    if not g:
                        pe.wait_ge(c.of("hkd", g), c.at("hkd", g))
                        pe.wait_ge(S(f"bank{3}_free"), c.claim(3))
                        for h in range(HR):
                            last = mm(ps[:, 3, h * DR:(h + 1) * DR], hkd[:, h].rearrange("p r d -> p (r d)"), proj[:, g, C_GI + h * DR:C_GI + (h + 1) * DR], start=True, stop=True)
                        last.then_inc(c.fills(3, "hstate", g), 1)

                by_feature("mix", "mixed")
                pe.wait_ge(c.of("bias"), c.at("bias"))
                spread_gate(0)
                for n in range(4):
                    ss = [slot(), slot()]
                    for g in range(NG):
                        b = 4 + 2 * (n % 2) + g
                        pe.wait_ge(S(f"bank{b}_free"), c.claim(b))
                        last = sweep(ps[:, b, 0:256], lambda k: hnT[:, k, g * P:(g + 1) * P], lambda k: ring[:, ss[k // KH], k % KH, 0:256], KC)
                        last.then_inc(c.fills(b, "out", n, g), 1)
                    owed.extend(ss)

                by_feature("hn2", "xn2")
                pe.wait_ge(S(f"bank{2}_free"), c.claim(2))
                for g in range(NG):
                    last = sweep(ps[:, 2, g * NE:(g + 1) * NE], lambda k: hnT[:, k, g * P:(g + 1) * P], lambda k: wrt[:, k, :], KC)
                last.then_inc(c.fills(2, "router"), 1)

                for g in range(NG):
                    for h in range(2):
                        bank_of_transposes(("rows", g, h), [hnT[:, 4 * h + k, g * P:(g + 1) * P] for k in range(4)])
                pe.wait_ge(c.of("picks", 0), c.at("picks", 0))
                pe.wait_ge(S("bank2_free"), c.claim(2))
                mm(ps[:, 2, 0:NG * NE], step_pattern(NLV + 1, 1), rt[:, 13].rearrange("p g e -> p (g e)"), start=True, stop=True)
                for d in range(2):
                    last = mm(ps[:, 2, NG * NE:2 * NG * NE], step_pattern(NLV + d, 0), rt[:, 13].rearrange("p g e -> p (g e)"), start=(d == 0), stop=(d == 1))
                last.then_inc(c.fills(2, "ahead"), 1)

                pe.wait_ge(c.of("zeroed"), c.at("zeroed"))
                for b in range(4, 8):
                    pe.wait_ge(S(f"bank{b}_free"), c.claim(b))
                    mm(ps[:, b, :], zero[:, 0:P], zero[:, 0:BLK], start=True, stop=False, skip_group_check=True)
                for g in range(NG):
                    for h in range(2):
                        pe.wait_ge(c.of("rowsS", g, h), c.at("rowsS", g, h))
                pe.wait_ge(S("rounds"), l + 2)
                until = count_of_rounds(pe, l + 1)
                with pe.Fori(c.rounds, until) as r:
                    with pe.Fori(0, TURNS) as t:
                        c.t = r * TURNS + t
                        led.where = "turn"
                        pe.wait_ge(c.of("seat", 0), c.at("seat", 0))
                        for half in range(2):
                            pe.wait_ge(S(f"bank{half}_free"), c.claim(half))
                            for k in range(KH):
                                for g in range(NG):
                                    last = mm(ps[:, half, k * P:(k + 1) * P], rows[:, g, KH * half + k, :], seat[:, g, :], start=(g == 0), stop=(g == 1))
                            last.then_inc(c.fills(half, "xT", half), 1)
                        for i in range(2):
                            pe.wait_ge(S(f"bank{2 + i}_free"), c.claim(2 + i))
                            for half in range(2):
                                pair = [slot(), slot()]
                                pe.wait_ge(c.of("xTs", half), c.at("xTs", half))
                                for k in range(KH):
                                    for e, s in enumerate(pair):
                                        last = mm(ps[64 * e:64 * e + 64, 2 + i, :], xT[:, KH * half + k, 64 * e:64 * e + 64], ring[:, s, k, :], start=(half == 0 and k == 0), stop=(half == 1 and k == KH - 1), skip_group_check=True)
                                        if k == KH - 1 and not (half and e):
                                            last.then_inc(S(f"slot{s}_used"), 1)
                                        elif not (half and e and k == KH - 1):
                                            pay(last)
                            owed.append(pair[1])
                            last.then_inc(c.fills(2 + i, "gu", i), 1)
                        pe.wait_ge(c.of("seatG", 0), c.at("seatG", 0))
                        bank_of_transposes(("seatT",), [seatG[:, g, :] for g in range(NG)], 1)
                        pe.wait_ge(c.of("act"), c.at("act"))
                        bank_of_transposes(("actT",), [act.rearrange("p (q k) -> p k q", k=KE)[:, k, :] for k in range(KE)], 0)
                        pe.wait_ge(c.of("actTs"), c.at("actTs"))
                        for h in range(2):
                            pair = [slot(), slot()]
                            pe.wait_ge(S(f"bank{2 + h}_free"), c.claim(2 + h))
                            for k in range(KE):
                                for e, s in enumerate(pair):
                                    last = mm(ps[64 * e:64 * e + 64, 2 + h, :], actT[:, k, 64 * e:64 * e + 64], ring[:, s, k, :], start=(k == 0), stop=(k == KE - 1), skip_group_check=True)
                                    if k == KE - 1 and not e:
                                        last.then_inc(S(f"slot{s}_used"), 1)
                                    elif k < KE - 1:
                                        pay(last)
                            owed.append(pair[1])
                            last.then_inc(c.fills(2 + h, "yP", h), 1)
                        pe.wait_ge(c.of("seatTs"), c.at("seatTs"))
                        for h in range(2):
                            pe.wait_ge(c.of("ys", h), c.at("ys", h))
                            for g in range(NG):
                                pay(mm(ps[:, 4 + 2 * g + h, :], seatT[:, g, :], ys[:, h, :], start=False, stop=False, skip_group_check=True))
                c.rounds = until
                led.where = "after"
                for b in range(4, 8):
                    last = mm(ps[:, b, :], zero[:, 0:P], zero[:, 0:BLK], start=False, stop=True, skip_group_check=True)
                    last.then_inc(c.fills(b, "y", b - 4), 1)
                spread_gate(1)
            assert not owed

        @block.vector
        def _(dve):
            c = Counts(led, S)
            led.where = "start"
            tt, ts, stt = v.tensor_tensor, v.tensor_scalar, v.scalar_tensor_tensor

            def st(ins, *label):
                ins.then_inc(c.makes(*(label or ("dve_step",))), 1)
                dve.wait_ge(S(c.last[0]), c.last_value())

            def red(out, in_, op=ALU.add):
                return v.tensor_reduce(out=out, in_=in_, axis=AX, op=op)

            def cols(a, g, n, h=HR):
                return proj[:, g, a:a + n].rearrange("p (h d) -> p h d", h=h)

            st(v.memset(epsc[:], EPS))
            st(v.memset(roundsf[:], 0.0))
            st(v.tensor_copy(roundsi[:], roundsf[:]), "rounds")
            st(v.memset(silT[:].rearrange("p k n -> p (k n)"), 0.0))
            led.found[("eps",)] = ("dve_step", "start", 1)
            dve.wait_ge(c.of("cond_dma"), c.at("cond_dma"))
            dve.wait_ge(c.of("sile"), c.at("sile"))
            st(ts(t1[:, 0:16], sile[:].rearrange("p g k -> p (g k)"), 1.0, None, ALU.add))
            st(v.reciprocal(t1[:, 16:32], t1[:, 0:16]))
            st(tt(silT[:, :, 0:NG].rearrange("p k g -> p g k"), condT[:], t1[:, 16:32].rearrange("p (g k) -> p g k", k=KC), ALU.mult), "silT", 0)
            led.found[("silT",)] = led.found[("silT", 0)]
            dve.wait_ge(c.of("begin_dma"), c.at("begin_dma"))
            st(tt(t1[:, 0:256], lbin[:, 0], lbin[:, 1], ALU.max))
            for l_ in range(L):
                st(tt(lbt[:, l_], lbin[:, l_], t1[:, 0:256], ALU.subtract), "lbd", l_)
            dve.wait_ge(c.of("lbe"), c.at("lbe"))
            st(tt(t1[:, 0:256], lbin[:, 0], lbin[:, 1], ALU.add))
            st(v.reciprocal(t1[:, 256:512], t1[:, 0:256]))
            for l_ in range(L):
                st(tt(lbin[:, l_], lbin[:, l_], t1[:, 256:512], ALU.mult))
            st(tt(t1[:, 0:256], lbin[:, 0], lbin[:, 1], ALU.add))
            st(tt(lbt[:, 0], lbin[:, 0], lbin[:, 0], ALU.subtract))
            st(tt(lbt[:, 1], t1[:, 0:256], lbin[:, 0], ALU.subtract), "bounds", 0)

            with dve.Fori(0, L) as l:
                c.l = l
                dve.wait_ge(S("rounds"), l + 1)
                c.rounds = count_of_rounds(dve, l)
                led.where = "layer"
                def normed(stage):
                    for g in range(NG):
                        dve.wait_ge(c.of(stage + "r", g), c.at(stage + "r", g))
                        st(ts(xs[:, g], x[:, g], stat[:, g, 2:3], None, ALU.mult), stage, g)

                def modulation_by_feature(norm):
                    dve.wait_ge(c.of("modT", norm), c.at("modT", norm))
                    both = modT[:, 2 * norm:2 * norm + 2]
                    tt(both.rearrange("p a k g -> p (a k) g"), ps[:, 0, 0:2 * KC * NG].rearrange("p (k g) -> p k g", g=NG),
                       badaT[:, 2 * norm:2 * norm + 2].rearrange("p a (k o) -> p (a k) o", o=1).broadcast_to([P, 2 * KC, NG]), ALU.add).then_inc(c.freed(("modT", norm)), 1)
                    dve.wait_ge(S(c.last[0]), c.last_value())
                    st(stt(out=modT[:, 2 * norm + 1], in0=modT[:, 2 * norm + 1], scalar=1.0, in1=nrmT[:, norm].rearrange("p (k o) -> p k o", o=1).broadcast_to([P, KC, NG]), op0=ALU.add, op1=ALU.mult), "modS", norm)

                normed("xn1")
                for h in range(2):
                    dve.wait_ge(c.of("hn1T", 0, h), c.at("hn1T", 0, h))
                    b = c.bank("hn1T", 0, h)
                    v.tensor_copy(hnT[:, KH * h:KH * (h + 1), 0:P], ps[:, b].rearrange("p (k t) -> p k t", k=KH)).then_inc(c.freed(("hn1T", 0, h)), 1)
                    dve.wait_ge(S(c.last[0]), c.last_value())
                dve.wait_ge(c.of("params"), c.at("params"))
                modulation_by_feature(0)
                for k in range(KC):
                    ins = ts(hnT[:, k, 0:P], hnT[:, k, 0:P], modT[:, 1, k, 0:1], modT[:, 0, k, 0:1], ALU.mult, ALU.add)
                    if k % KH == KH - 1:
                        ins.then_inc(c.makes("hn1S0", k // KH), 1)

                dve.wait_ge(c.of("later_dma"), c.at("later_dma"))
                lb = lbt[:, one(l)]
                st(ts(oml[:], lb.rearrange("p l n -> p (l n)"), -1.0, 1.0, ALU.mult, ALU.add))
                st(v.tensor_copy(lams[:], C["lami"][:, bass.ds(l * 2, 2)]))
                st(tt(t1[:, 0:32], lamp[:, 0], lamp[:, 1], ALU.mult))
                st(tt(t1[:, 32:64], lamp[:, 2], lamp[:, 3], ALU.mult))
                st(red(lam[:, 0:2], t1[:, 0:64].rearrange("p (a b) -> p a b", a=2)), "lamsum", 0)
                dve.wait_ge(c.of("lamexp"), c.at("lamexp"))
                st(tt(lam[:, 4:5], lam[:, 2:3], lam[:, 3:4], ALU.subtract))
                st(tt(lam[:, 5:6], lam[:, 4:5], lams[:, 0:1], ALU.add))
                st(ts(lam[:, 6:7], lam[:, 5:6], -1.0, None, ALU.mult))
                st(ts(subln[:], subln[:], lams[:, 1:2], None, ALU.mult))
                dve.wait_ge(c.of("rdec"), c.at("rdec"))
                st(ts(rdec[:], rdec[:], -1.0, None, ALU.mult))
                st(ts(rdecH[:], rdecH[:], -1.0, None, ALU.mult), "rdecn", 0)
                dve.wait_ge(c.of("decT"), c.at("decT"))
                tb = t1[:, 0:BLK].rearrange("p (h t) -> p h t", h=HR)
                for d, half in enumerate((decT[:], tb)):
                    st(tt(half, half, C["steps"][:, (2 * NLV + d) * P:(2 * NLV + d + 1) * P].rearrange("p (o t) -> p o t", o=1).broadcast_to([P, HR, P]), ALU.mult))
                st(tt(decT[:], decT[:], tb, ALU.add), "decS", 0)


                def shifted(stage, a):
                    dve.wait_ge(c.of("modS", a), c.at("modS", a))
                    for h in range(2):
                        dve.wait_ge(c.of(stage + "T", 0, h), c.at(stage + "T", 0, h))
                        b = c.bank(stage + "T", 0, h)
                        for k in range(4):
                            kc = 4 * h + k
                            ins = ts(hnT[:, kc, 0:P], ps[:, b, k * P:(k + 1) * P], modT[:, 2 * a + 1, kc, 0:1], modT[:, 2 * a, kc, 0:1], ALU.mult, ALU.add)
                        ins.then_inc(c.freed((stage + "T", 0, h), stage + "S", 0, h), 1)
                        dve.wait_ge(S(c.last[0]), c.last_value())

                def swish(name, col):
                    for g in range(NG):
                        e = spare[name][:, g]
                        dve.wait_ge(c.of(name, g), c.at(name, g))
                        st(ts(e, e, 1.0, None, ALU.add))
                        st(v.reciprocal(e, e))
                        here = proj[:, g, col:col + 256]
                        st(tt(here, here, e, ALU.mult), name + "S", g)

                def queries_and_keys():
                    for g in range(NG):
                        both = proj[:, g, 0:D].rearrange("p (a d) -> p a d", d=DQ)
                        st(tt(sq[:], proj[:, g, 0:D], proj[:, g, 0:D], ALU.mult))
                        st(red(stat[:, g, 32:64], sq[:].rearrange("p (a d) -> p a d", d=DQ)), "qkm", g)
                        dve.wait_ge(c.of("qkr", g), c.at("qkr", g))
                        st(tt(both, both, stat[:, g, 32:64].rearrange("p (a o) -> p a o", o=1).broadcast_to([P, 32, DQ]), ALU.mult))
                        for r in range(2):
                            lab = ("qkn", g) if (not g and r) else ()
                            st(tt(both[:, 2 * NH * r:2 * NH * (r + 1)], both[:, 2 * NH * r:2 * NH * (r + 1)], wqk[:, r].rearrange("p (o d) -> p o d", o=1).broadcast_to([P, 2 * NH, DQ]), ALU.mult), *lab)
                        if g:
                            pairs = both.rearrange("p a (i z) -> p a i z", z=2)
                            cs = C["cos"][:].rearrange("p (o d) -> p o d", o=1).broadcast_to([P, 32, DQ])
                            sn = C["sin"][:].rearrange("p (o i z) -> p o i z", o=1, z=2).broadcast_to([P, 32, DQ // 2, 2])
                            rot = t1[:].rearrange("p (a i z) -> p a i z", i=DQ // 2, z=2)
                            for z in range(2):
                                st(tt(rot[:, :, :, z], pairs[:, :, :, 1 - z], sn[:, :, :, z], ALU.mult))
                            st(tt(both, both, cs, ALU.mult))
                            st(tt(both, both, t1[:].rearrange("p (a d) -> p a d", d=DQ), ALU.add), "qkn", g)

                def keys_and_decays():
                    for g in range(NG):
                        E, F = zexp[g], laf[g][:]
                        zz = proj[:, g, C_GFF:C_GFF + BLK]
                        st(ts(E, zz, -80.0, None, ALU.max), "zc", g)
                        dve.wait_ge(c.of("ze", g), c.at("ze", g))
                        st(ts(F, E, 1.0, None, ALU.add))
                        st(v.reciprocal(F, F))
                        st(tt(E, E, F, ALU.mult))
                        omlv = oml[:].rearrange("p (o h d) -> p o h d", o=1, h=HR).broadcast_to([P, 2, HR, DR])
                        lbv = lb.rearrange("p o (h d) -> p o h d", h=HR).broadcast_to([P, 2, HR, DR])
                        dhd = lambda a: a.rearrange("p (r h d) -> p r h d", r=2, h=HR)
                        st(tt(hk[g].rearrange("p h r d -> p r h d"), dhd(E), omlv, ALU.mult), "hk", g)
                        st(tt(dhd(F), dhd(F), omlv, ALU.mult))
                        st(tt(dhd(F), dhd(F), lbv, ALU.add))
                        st(ts(F, F, 1e-30, None, ALU.max))
                        st(ts(E, F, LN_LOW, 1.0 / LN_LOW, ALU.is_lt, ALU.mult))
                        st(stt(out=F, in0=E, scalar=1.0, in1=F, op0=ALU.max, op1=ALU.mult), "gatef", g)
                        dve.wait_ge(c.of("gln", g), c.at("gln", g))
                        st(stt(out=F, in0=E, scalar=LN_LOW * math.log(LN_LOW), in1=F, op0=ALU.mult, op1=ALU.add), "la", g)

                def prepare(i):
                    dve.wait_ge(c.of("projS", i, 1), c.at("projS", i, 1))
                    if i == 1:
                        queries_and_keys()
                    if i == 4:
                        swish("rg", C_RG)
                    if i == 5:
                        swish("gq", C_GQ)
                    if i == 6:
                        keys_and_decays()
                    if i == 7:
                        swish("gg", C_GG)

                nb = 0
                for nth, i in enumerate(IN_ORDER):
                    n = min(BLK, D_IN - i * BLK)
                    dve.wait_ge(c.of("projP", i, 0), c.at("projP", i, 0))
                    b = 2 + nb % 6
                    nb += 2
                    v.tensor_copy(proj[:, 0, i * BLK:i * BLK + n], ps[:, b, 0:n]).then_inc(c.freed(("projP", i, 0), "projS", i, 0), 1)
                    dve.wait_ge(S(c.last[0]), c.last_value())
                    prepare(i)
                modulation_by_feature(1)

                def group_norm(read, b, n, w, g, base, src_label):
                    m = n * 64
                    dve.wait_ge(c.of(src_label + "q", g), c.at(src_label + "q", g))
                    st(red(stat[:, g, 16:16 + n], sq[:, 0:m].rearrange("p (h d) -> p h d", h=n)), src_label + "m", g)
                    dve.wait_ge(c.of(src_label + "r", g), c.at(src_label + "r", g))
                    out = xs[:, g, base:base + m].rearrange("p (h d) -> p h d", h=n)
                    tt(out, ps[:, b, 0:m].rearrange("p (h d) -> p h d", h=n), stat[:, g, 16:16 + n].rearrange("p (h o) -> p h o", o=1).broadcast_to([P, n, 64]), ALU.mult).then_inc(c.freed(read), 1)
                    dve.wait_ge(S(c.last[0]), c.last_value())
                    ins = tt(out, out, w[:].rearrange("p (o d) -> p o d", o=1).broadcast_to([P, n, 64]), ALU.mult)
                    return ins, out

                for g in range(NG):
                    nk = 1 + g
                    dve.wait_ge(c.of("daqT", g), c.at("daqT", g))
                    b = c.bank("daqT", g)
                    for j in range(4):
                        ins = ts(qTm[:, j], ps[:, b].rearrange("p (m t) -> p m t", m=4), C["quarter"][:, j:j + 1], None, ALU.mult)
                    ins.then_inc(c.freed(("daqT", g), "qTm", g), 1)
                    dve.wait_ge(S(c.last[0]), c.last_value())
                    sm = stat[:, g]
                    for hh in range(2):
                        for j in range(4):
                            dve.wait_ge(c.of("score", g, hh, j), c.at("score", g, hh, j))
                        mx = rt[:, 2 * hh, 0, 0:8].rearrange("p (m j) -> p j m", j=4)
                        st(red(mx, ps[:, 4:8, 0:2 * nk * P].rearrange("p j (m t) -> p j m t", m=2), ALU.max))
                        st(ts(rt[:, 2 * hh, 0, 8:16], rt[:, 2 * hh, 0, 0:8], -DQ ** -0.5, None, ALU.mult), "nmax", g, hh)
                    for hh in range(2):
                        dve.wait_ge(c.of("expd", g, hh), c.at("expd", g, hh))
                        rs = rt[:, 2 * hh + 1, 0]
                        st(v.reciprocal(rs[:, 8:16], rs[:, 0:8]))
                        rr = rs[:, 8:16].rearrange("p (a r) -> p r a", r=2)
                        st(ts(rr[:, 1], rr[:, 1], lam[:, 6:7], None, ALU.mult))
                        for hd in range(4):
                            i0 = 2 * hd
                            st(ts(t4[:, 0:nk * P], eP[:, hh, i0, 0:nk * P], rs[:, 8 + i0:9 + i0], None, ALU.mult))
                            lab = ("wP", g, hh) if hd == 3 else ()
                            st(stt(out=wP[:, hh, hd, 0:nk * P], in0=eP[:, hh, i0 + 1, 0:nk * P], scalar=rs[:, 9 + i0:10 + i0], in1=t4[:, 0:nk * P], op0=ALU.mult, op1=ALU.add), *lab)
                    st(v.tensor_copy(rq2, cols(C_RQ, g, 256).rearrange("p h (o d) -> p h o d", o=1).broadcast_to([P, HR, 2, DR])))
                    st(ts(rk2, cols(C_RK, g, 256).rearrange("p h (o d) -> p h o d", o=1).broadcast_to([P, HR, 2, DR]), DR ** -0.5, None, ALU.mult), "rk2", g)
                    if not g:
                        dve.wait_ge(c.of("decend"), c.at("decend"))
                        st(tt(rkd[:], rk2, decend[:].rearrange("p h (r o) -> p h r o", o=1).broadcast_to([P, HR, 2, DR]), ALU.mult), "rkd", g)
                    dve.wait_ge(c.of("rkT", g), c.at("rkT", g))
                    b = c.bank("rkT", g)
                    ts(qw[:, 1], ps[:, b], 0.5, None, ALU.mult).then_inc(c.freed(("rkT", g), "rkTs", g), 1)
                    dve.wait_ge(S(c.last[0]), c.last_value())
                    ins, _ = group_norm(("dao", g), 3, NH, subln, g, 0, "dao")
                    st(ins)
                    if g:
                        dve.wait_ge(c.of("rqTs", g), c.at("rqTs", g))
                        dve.wait_ge(c.of("decin"), c.at("decin"))
                        st(tt(rqi, rqT, decin[:], ALU.mult), "rqi", g)
                    dve.wait_ge(c.of("rS", g), c.at("rS", g))
                    tt(rA, ps[:, 2].rearrange("p (h t) -> p h t", h=HR), decT[:], ALU.mult).then_inc(c.freed(("rS", g), "rA", g), 1)
                    dve.wait_ge(S(c.last[0]), c.last_value())
                    ins, out = group_norm(("ro", g), 2, HR, rnorm, g, 512, "ro")
                    st(ins)
                    st(tt(out, out, cols(C_RG, g, 256), ALU.mult))

                    st(v.tensor_copy(hq2, cols(C_GQ, g, 256).rearrange("p h (o d) -> p h o d", o=1).broadcast_to([P, HR, 2, DR])), "hq2", g)
                    dve.wait_ge(c.of("hkT", g), c.at("hkT", g))
                    b = c.bank("hkT", g)
                    v.tensor_copy(qw[:, 1], ps[:, b]).then_inc(c.freed(("hkT", g), "hkTs", g), 1)
                    dve.wait_ge(S(c.last[0]), c.last_value())
                    dve.wait_ge(c.of("hqTs", g), c.at("hqTs", g))

                    def masked(lv):
                        if lv >= 1:
                            dve.wait_ge(c.of("hV", g, lv - 2), c.at("hV", g, lv - 2))
                        for r in range(2 if lv >= 0 else 1):
                            m = C["ident"][:] if lv < 0 else C["masks"][:, (2 * lv + r) * P:(2 * lv + r + 1) * P]
                            dve.wait_ge(c.of("hS", g, lv, r), c.at("hS", g, lv, r))
                            src = ps[:, 2 + r].rearrange("p (h t) -> p h t", h=HR)
                            tt(A[:, lv % 2, r], src, m.rearrange("p (o t) -> p o t", o=1).broadcast_to([P, HR, P]), ALU.mult).then_inc(c.freed(("hS", g, lv, r), "hA", g, lv, r), 1)
                            dve.wait_ge(S(c.last[0]), c.last_value())

                    def scaled_queries(lv):
                        dve.wait_ge(c.of("ex", g, lv), c.at("ex", g, lv))
                        st(tt(qlv[:, lv % 2], hqT, ex[:, lv % 2], ALU.mult), "qlv", g, lv)

                    scaled_queries(0)
                    for lv in range(-1, NLV):
                        if 0 <= lv < NLV - 1:
                            scaled_queries(lv + 1)
                        masked(lv)
                    if g:
                        dve.wait_ge(c.of("ex", g, NLV), c.at("ex", g, NLV))
                        st(tt(hqi, hqT, ex[:, NLV % 2], ALU.mult), "hqi", g)
                    else:
                        dve.wait_ge(c.of("exend", g), c.at("exend", g))
                        st(tt(hkd[:].rearrange("p h r d -> p r h d"), hk[g].rearrange("p h r d -> p r h d"), t4[:].rearrange("p (r h d) -> p r h d", r=2, h=HR), ALU.mult), "hkd", g)
                    ins, out = group_norm(("ho", g), 2, HR, hnorm, g, 768, "ho")
                    st(ins)
                    st(tt(out, out, cols(C_GG, g, 256), ALU.mult), "mixed", g)

                for g in range(1):
                    for h in range(2):
                        dve.wait_ge(c.of("mixT", g, h), c.at("mixT", g, h))
                        b = c.bank("mixT", g, h)
                        v.tensor_copy(hnT[:, 4 * h:4 * h + 4, g * P:(g + 1) * P], ps[:, b].rearrange("p (k t) -> p k t", k=4)).then_inc(c.freed(("mixT", g, h), "mixS", g, h), 1)
                        dve.wait_ge(S(c.last[0]), c.last_value())
                for n in range(4):
                    for g in range(NG):
                        sl = slice(n * 256, (n + 1) * 256)
                        dve.wait_ge(c.of("gateS", 0, g, n // 2), c.at("gateS", 0, g, n // 2))
                        dve.wait_ge(c.of("out", n, g), c.at("out", n, g))
                        tt(t1[:, 0:256], ps[:, 4 + 2 * (n % 2) + g, 0:256], gbuf1[:, g, sl], ALU.mult).then_inc(c.freed(("out", n, g)), 1)
                        dve.wait_ge(S(c.last[0]), c.last_value())
                        lab = ("x1", g) if n == 3 else ()
                        st(tt(x[:, g, sl], x[:, g, sl], t1[:, 0:256], ALU.add), *lab)
                normed("xn2")
                shifted("hn2", 1)

                st(v.memset(zero[:], 0.0), "zeroed", 0)
                led.found[("zeroed",)] = led.found[("zeroed", 0)]

                G4 = lambda a: a.rearrange("p g (q e) -> p g q e", e=4)
                dve.wait_ge(c.of("rexp"), c.at("rexp"))
                sc, sel = rt[:, 1], rt[:, 2]
                st(ts(rt[:, 3], rt[:, 0], 1.0, None, ALU.add))
                st(v.reciprocal(sc, rt[:, 3]))
                st(tt(sel, sc, rbias[:].rearrange("p (o e) -> p o e", o=1).broadcast_to([P, NG, NE]), ALU.add))
                s4 = sel.rearrange("p g (q a z) -> p g q a z", a=2, z=2)
                hi = rt[:, 3, :, 0:8].rearrange("p g (q a) -> p g q a", a=2)
                lo = rt[:, 4, :, 0:8].rearrange("p g (q a) -> p g q a", a=2)
                st(tt(hi, s4[:, :, :, :, 0], s4[:, :, :, :, 1], ALU.max))
                st(tt(lo, s4[:, :, :, :, 0], s4[:, :, :, :, 1], ALU.min))
                st(tt(rt[:, 5, :, 0:4], hi[:, :, :, 0], hi[:, :, :, 1], ALU.max))
                st(tt(rt[:, 5, :, 4:8], hi[:, :, :, 0], hi[:, :, :, 1], ALU.min))
                st(tt(rt[:, 5, :, 8:12], lo[:, :, :, 0], lo[:, :, :, 1], ALU.max))
                st(tt(rt[:, 5, :, 4:8], rt[:, 5, :, 4:8], rt[:, 5, :, 8:12], ALU.max))
                st(tt(rt[:, 5, :, 0:4], rt[:, 5, :, 0:4], rt[:, 5, :, 4:8], ALU.add))

                def first_best(vals, rank, n, pick, tmp):
                    m = stat[:, 0, 0:NG]
                    bc = lambda a: a.rearrange("p (g o) -> p g o", o=1).broadcast_to([P, NG, n])
                    st(red(m, vals, ALU.max))
                    st(tt(tmp, vals, bc(m), ALU.is_equal))
                    st(tt(tmp, tmp, C[rank][:].rearrange("p (o e) -> p o e", o=1).broadcast_to([P, NG, n]), ALU.mult))
                    st(red(m, tmp, ALU.max))
                    st(tt(pick, tmp, bc(m), ALU.is_equal))

                first_best(rt[:, 5, :, 0:4], "rank4", 4, rt[:, 6, :, 0:4], rt[:, 7, :, 0:4])
                grp = rt[:, 6, :, 0:4].rearrange("p g (q o) -> p g q o", o=1).broadcast_to([P, NG, 4, 4])
                st(ts(rt[:, 8, :, 0:4], rt[:, 6, :, 0:4], 2.0, -2.0, ALU.mult, ALU.add))
                st(tt(G4(rt[:, 9]), G4(sel), grp, ALU.mult))
                st(tt(G4(rt[:, 9]), G4(rt[:, 9]), rt[:, 8, :, 0:4].rearrange("p g (q o) -> p g q o", o=1).broadcast_to([P, NG, 4, 4]), ALU.add))
                first_best(rt[:, 9], "rank16", NE, rt[:, 10], rt[:, 11])
                st(stt(out=rt[:, 9], in0=rt[:, 10], scalar=-1e30, in1=rt[:, 9], op0=ALU.mult, op1=ALU.add))
                first_best(rt[:, 9], "rank16", NE, rt[:, 12], rt[:, 11])
                st(tt(rt[:, 13], rt[:, 10], rt[:, 12], ALU.add), "picks", 0)
                st(tt(rt[:, 10], rt[:, 13], sc, ALU.mult))
                st(red(stat[:, 0, 0:NG], rt[:, 10]))
                st(v.reciprocal(stat[:, 0, 2:4], stat[:, 0, 0:NG]))
                st(tt(gt[:], rt[:, 10], stat[:, 0, 2:4].rearrange("p (g o) -> p g o", o=1).broadcast_to([P, NG, NE]), ALU.mult))
                for g in range(NG):
                    for h in range(2):
                        if (2 * g + h) % 2:
                            dve.wait_ge(c.of("rows", g, h), c.at("rows", g, h))
                            b = c.bank("rows", g, h)
                            v.tensor_copy(xs[:, g, h * BLK:(h + 1) * BLK], ps[:, b]).then_inc(c.freed(("rows", g, h), "rowsS", g, h), 1)
                            dve.wait_ge(S(c.last[0]), c.last_value())
                dve.wait_ge(c.of("ahead"), c.at("ahead"))
                st(ts(rt[:, 9], rt[:, 13], -FAR, FAR, ALU.mult, ALU.add))
                st(tt(seatno[:], rt[:, 9], ps[:, 2, 0:NG * NE].rearrange("p (g e) -> p g e", g=NG), ALU.add))
                total = rt[:, 12]
                v.tensor_copy(total, ps[:, 2, NG * NE:2 * NG * NE].rearrange("p (g e) -> p g e", g=NG)).then_inc(c.freed(("ahead",)), 1)
                dve.wait_ge(S(c.last[0]), c.last_value())
                st(tt(seatno[:, 1], seatno[:, 1], total[:, 0], ALU.add))
                st(tt(rt[:, 11, 0], total[:, 0], total[:, 1], ALU.add))
                st(red(need[:, 0:1], rt[:, 11, 0], ALU.max))
                for i in range(1, NG * P // SLOTS):
                    st(ts(need[:, i:i + 1], need[:, 0:1], float(i * SLOTS), None, ALU.is_gt))
                st(red(need[:, 4:5], need[:, 1:NG * P // SLOTS]))
                st(stt(out=roundsf[:, one(l + 1)], in0=need[:, 4:5], scalar=1.0, in1=roundsf[:, one(l)], op0=ALU.add, op1=ALU.add))
                st(v.tensor_copy(roundsi[:, one(l + 1)], roundsf[:, one(l + 1)]), "rounds")
                until = count_of_rounds(dve, l + 1)
                with dve.Fori(c.rounds, until) as r:
                    with dve.Fori(0, TURNS) as t:
                        c.t = r * TURNS + t
                        led.where = "turn"
                        at = lambda a, g: a[:, g, bass.ds(t * 2, 2)].rearrange("p (e o) -> p e o", o=1).broadcast_to([P, 2, SLOTS])
                        by_seat = lambda a, g: a[:, g].rearrange("p (e s) -> p e s", e=2)
                        for g in range(NG):
                            st(tt(by_seat(seat, g), C["slot"][:].rearrange("p (o s) -> p o s", o=1).broadcast_to([P, 2, SLOTS]), at(seatno, g), ALU.is_equal), "seat", g - 1)
                        for g in range(NG):
                            st(tt(by_seat(seatG, g), by_seat(seat, g), at(gt, g), ALU.mult), "seatG", g - 1)
                        dve.wait_ge(c.of("gexp"), c.at("gexp"))
                        st(ts(ge, ge, 1.0, None, ALU.add))
                        st(v.reciprocal(ge, ge))
                        tt(gs, ps[:, 2], ge, ALU.mult).then_inc(c.freed(("gu", 0)), 1)
                        dve.wait_ge(S(c.last[0]), c.last_value())
                        dve.wait_ge(c.of("gu", 1), c.at("gu", 1))
                        tt(act, ps[:, 3], gs, ALU.mult).then_inc(c.freed(("gu", 1), "act"), 1)
                        dve.wait_ge(S(c.last[0]), c.last_value())
                        dve.wait_ge(c.of("seatT"), c.at("seatT"))
                        v.tensor_copy(seatT, ps[:, 1, 0:NG * P].rearrange("p (g s) -> p g s", g=NG)).then_inc(c.freed(("seatT",), "seatTs"), 1)
                        dve.wait_ge(S(c.last[0]), c.last_value())
                        dve.wait_ge(c.of("yP", 1), c.at("yP", 1))
                        v.tensor_copy(ys[:, 1], ps[:, 3]).then_inc(c.freed(("yP", 1), "ys", 1), 1)
                        dve.wait_ge(S(c.last[0]), c.last_value())
                    led.where = "rounds"
                    ts(seatno[:], seatno[:], -float(SLOTS), None, ALU.add).then_inc(S("later_seats"), 1)
                    dve.wait_ge(S("later_seats"), r + 1)
                c.rounds = until
                led.where = "after"
                for g in range(NG):
                    for h in range(2):
                        sl = slice(h * BLK, (h + 1) * BLK)
                        dve.wait_ge(c.of("gateS", 1, g, h), c.at("gateS", 1, g, h))
                        dve.wait_ge(c.of("y", 2 * g + h), c.at("y", 2 * g + h))
                        tt(t1[:, 0:BLK], ps[:, 4 + 2 * g + h], gbuf2[:, g, sl], ALU.mult).then_inc(c.freed(("y", 2 * g + h)), 1)
                        dve.wait_ge(S(c.last[0]), c.last_value())
                        lab = ("x2", g) if h else ()
                        st(tt(x[:, g, sl], x[:, g, sl], t1[:, 0:BLK], ALU.add), *lab)

        @block.scalar
        def _(acte):
            c = Counts(led, S)
            led.where = "start"

            def st(ins, *label):
                ins.then_inc(c.makes(*(label or ("act_step",))), 1)
                acte.wait_ge(S(c.last[0]), c.last_value())

            act_ = nc.scalar.activation

            def ex_(out, in_, scale=1.0, **k):
                return act_(out, in_, AF.Exp, scale=scale, **k)

            def rstd(g, cols_, n, label):
                a = stat[:, g, cols_]
                st(act_(a, a, AF.Ln, bias=epsc[:, 0:1], scale=1.0 / n))
                st(ex_(a, a, -0.5), *label)

            def evac(read, out, *label, fn=None):
                acte.wait_ge(c.of(*read), c.at(*read))
                b = c.bank(*read)
                src = ps[:, b]
                (nc.scalar.copy(out, src) if fn is None else fn(src)).then_inc(c.freed(read, *label), 1)
                acte.wait_ge(S(c.last[0]), c.last_value())

            nc.scalar.preload_act_table_set("natural_log_exp_and_others")
            for name in ("stored", "bias", "mixed", "x2"):
                acte.sem_inc(c.makes(name), 1)
            acte.wait_ge(c.of("cond_dma"), c.at("cond_dma"))
            acte.wait_ge(c.of("eps"), c.at("eps"))
            st(ex_(sile[:].rearrange("p g k -> p (g k)"), condT[:].rearrange("p g k -> p (g k)"), -1.0), "sile", 0)
            led.found[("sile",)] = led.found[("sile", 0)]
            acte.wait_ge(c.of("begin_dma"), c.at("begin_dma"))
            acte.wait_ge(c.of("lbd", L - 1), c.at("lbd", L - 1))
            for l_ in range(L):
                st(ex_(lbin[:, l_], lbt[:, l_]), "lbe", l_)
            led.found[("lbe",)] = led.found[("lbe", L - 1)]
            with acte.Fori(0, L) as l:
                c.l = l
                acte.wait_ge(S("rounds"), l + 1)
                c.rounds = count_of_rounds(acte, l)
                led.where = "layer"

                def squares(stage):
                    for g in range(NG):
                        if stage == "xn1":
                            acte.wait_ge(S("x2"), c.value("x2", "layer", 0))
                        else:
                            acte.wait_ge(c.of("x1", g), c.at("x1", g))
                        st(act_(sq[:], x[:, g], AF.Square, accum_out=stat[:, g, 2:3]))
                        rstd(g, slice(2, 3), D, (stage + "r", g))

                acte.wait_ge(S("mixed"), c.value("mixed", "layer", 0))
                row = lambda name: ap[name][one(l)].rearrange("l n -> (l n)")
                rb = lambda name, a, n: ap[name][one(l), a:a + n].broadcast_to([P, n])
                bT = lambda r: r.rearrange("l (p k) -> p (l k)", k=KC)
                loads = [(nrmT[:, 0], bT(ap["norm_mix"][one(l)])), (nrmT[:, 1], bT(ap["norm_ffn"][one(l)]))]
                loads += [(badaT[:, a], bT(ap["b_ada"][one(l), vec * D:(vec + 1) * D])) for a, vec in enumerate((0, 1, 3, 4))]
                loads += [(wqk[:, 0], rb("da_qnorm", 0, DQ)), (wqk[:, 1], rb("da_knorm", 0, DQ)),
                          (lamp[:].rearrange("p a d -> p (a d)"), ap["da_lambda"].rearrange("l a d -> l (a d)")[one(l)].broadcast_to([P, 4 * DQ])),
                          (subln[:], rb("da_subln", 0, DV)), (rnorm[:], rb("ret_norm", 0, DR)), (hnorm[:], rb("hg_norm", 0, DR)),
                          (ctxk[:], ap["cache_k"][0].rearrange("l t h r d -> t l (h r d)")[:, one(l)].rearrange("t l n -> t (l n)")),
                          (ctxv[:], ap["cache_v"][0].rearrange("l t h d -> t l (h d)")[:, one(l)].rearrange("t l n -> t (l n)"))]
                dec = ap["ret_decay"].rearrange("l r h -> l (r h)")
                loads += [(rdec[:], dec[one(l)].broadcast_to([P, 2 * HR]))]
                for d in range(2):
                    q = slice(64 * d, 64 * d + 64)
                    loads += [(rdecH[q], dec[one(l), d * HR:(d + 1) * HR].broadcast_to([64, HR])),
                              (s0r[q], ap["state_ret"][0].rearrange("l r h d e -> r d l h e")[d, :, one(l)].rearrange("d l h e -> d (l h) e")),
                              (s0h[q], ap["state_hgrn"][0].rearrange("l r h d e -> r d l h e")[d, :, one(l)].rearrange("d l h e -> d (l h) e"))]
                for dst, src in loads:
                    acte.dma_start(dst, src).then_inc(S("params"), 16)
                led.made("params", ("params",), 16 * len(loads))

                def store(dst, src):
                    acte.dma_start(dst, src).then_inc(S("stored"), 16)
                    led.made("stored", ("stored",), 16)

                squares("xn1")
                acte.wait_ge(S("stored"), c.value("stored", "layer", 0))
                acte.wait_ge(S("bias"), c.value("bias", "layer", 0))
                acte.wait_ge(c.of("bounds", 0), c.at("bounds", 0))

                def modulation(i):
                    vec, h = divmod(i, 2)
                    to = gateR[:, vec // 3] if vec % 3 == 2 else modR[:, (vec - vec // 3) * D:(vec - vec // 3 + 1) * D]
                    name = ("gateR", i) if vec % 3 == 2 else ("modR", vec - vec // 3) if h else ("modRh", vec)
                    evac(("mod", i), to[:, h * BLK:(h + 1) * BLK], *name)

                modulation(0)
                modulation(1)
                for h in range(2):
                    evac(("hn1T", 1, h), None, fn=lambda src: nc.scalar.copy(hnT[:, KH * h:KH * (h + 1), P:2 * P], src.rearrange("p (k t) -> p k t", k=KH)))
                modulation(2)
                modulation(3)
                acte.wait_ge(c.of("modS", 0), c.at("modS", 0))
                for k in range(KC):
                    ins = act_(hnT[:, k, P:2 * P], hnT[:, k, P:2 * P], AF.Identity, bias=modT[:, 0, k, 1:2], scale=modT[:, 1, k, 1:2])
                    if k % KH == KH - 1:
                        ins.then_inc(c.makes("hn1S1", k // KH), 1)
                acte.wait_ge(c.of("params"), c.at("params"))
                acte.wait_ge(c.of("later_dma"), c.at("later_dma"))
                acte.wait_ge(c.of("lamsum", 0), c.at("lamsum", 0))
                st(ex_(lam[:, 2:4], lam[:, 0:2]), "lamexp", 0)
                led.found[("lamexp",)] = led.found[("lamexp", 0)]
                st(ex_(rdec[:], rdec[:]))
                st(ex_(rdecH[:], rdecH[:]), "rdec", 0)
                led.found[("rdec",)] = led.found[("rdec", 0)]
                acte.wait_ge(c.of("rdecn", 0), c.at("rdecn", 0))
                acte.wait_ge(S("x2"), c.value("x2", "layer", 0))
                for d in range(2):
                    for h in range(HR):
                        lab = ("decT", 0) if (d and h == HR - 1) else ()
                        st(ex_(t1[:, h * P:(h + 1) * P] if d else decT[:, h], C["dist"][:, d * P:(d + 1) * P], rdec[:, d * HR + h:d * HR + h + 1]), *lab)
                led.found[("decT",)] = led.found[("decT", 0)]
                for h in range(HR):
                    st(ex_(decin[:, h], C["inpos"][:], rdecH[:, h:h + 1]), "decin", h)
                led.found[("decin",)] = led.found[("decin", HR - 1)]
                for d in range(2):
                    st(ex_(decend[:, :, d], rdec[:, d * HR:(d + 1) * HR], C["endpos"][:, d:d + 1]), "decend", d)
                led.found[("decend",)] = led.found[("decend", 1)]

                def shifted(stage, a):
                    acte.wait_ge(c.of("modS", a), c.at("modS", a))
                    for h in range(2):
                        acte.wait_ge(c.of(stage + "T", 1, h), c.at(stage + "T", 1, h))
                        b = c.bank(stage + "T", 1, h)
                        for k in range(4):
                            kc = 4 * h + k
                            ins = act_(hnT[:, kc, P:2 * P], ps[:, b, k * P:(k + 1) * P], AF.Identity, bias=modT[:, 2 * a, kc, 1:2], scale=modT[:, 2 * a + 1, kc, 1:2])
                        ins.then_inc(c.freed((stage + "T", 1, h), stage + "S", 1, h), 1)
                        acte.wait_ge(S(c.last[0]), c.last_value())

                def prepare(i):
                    acte.wait_ge(c.of("projS", i, 0), c.at("projS", i, 0))
                    for g in range(NG):
                        if i == 1:
                            acte.wait_ge(c.of("qkm", g), c.at("qkm", g))
                            rstd(g, slice(32, 64), DQ, ("qkr", g))
                        for name, block_, col in (("rg", 4, C_RG), ("gq", 5, C_GQ), ("gg", 7, C_GG)):
                            if i == block_:
                                st(ex_(spare[name][:, g], proj[:, g, col:col + 256], -1.0), name, g)
                        if i == 6:
                            acte.wait_ge(c.of("zc", g), c.at("zc", g))
                            st(ex_(zexp[g], zexp[g], -1.0), "ze", g)
                            acte.wait_ge(c.of("gatef", g), c.at("gatef", g))
                            st(act_(laf[g][:], laf[g][:], AF.Ln), "gln", g)
                    if i == 2:
                        acte.wait_ge(c.of("qkn", 0), c.at("qkn", 0))
                        acte.wait_ge(c.of("projS", 2, 0), c.at("projS", 2, 0))
                        store(ap["o_k"][0].rearrange("l t h r d -> t l (h r d)")[:, one(l)].rearrange("t l n -> t (l n)"), proj[:, 0, C_DAK:C_DAK + BLK])
                        store(ap["o_v"][0].rearrange("l t h d -> t l (h d)")[:, one(l)].rearrange("t l n -> t (l n)"), proj[:, 0, C_DAV:C_DAV + BLK])

                for nth, i in enumerate(IN_ORDER):
                    n = min(BLK, D_IN - i * BLK)
                    evac(("projP", i, 1), None, "projS", i, 1, fn=lambda src: nc.scalar.copy(proj[:, 1, i * BLK:i * BLK + n], src[:, 0:n]))
                    modulation(N_MOD1 + nth)
                    prepare(i)
                for i in (4, 5, 10, 11):
                    acte.wait_ge(c.of("gateR", i), c.at("gateR", i))
                for a in range(2):
                    vec = 2 + 3 * a
                    acte.dma_start(gateR[NG:NG + 1, a], ap["b_ada"][one(l), vec * D:(vec + 1) * D]).then_inc(S("bias"), 16)
                led.made("bias", ("bias",), 32)

                def square_of(read, n, label, g):
                    acte.wait_ge(c.of(*read), c.at(*read))
                    b = c.bank(*read)
                    st(act_(sq[:, 0:n], ps[:, b, 0:n], AF.Square), label + "q", g)
                    acte.wait_ge(c.of(label + "m", g), c.at(label + "m", g))
                    rstd(g, slice(16, 16 + n // 64), 64, (label + "r", g))

                for g in range(NG):
                    nk = 1 + g
                    evac(("dakT", g), None, "kT", g, fn=lambda src: nc.scalar.copy(kT[:, :, 0, :], src.rearrange("p (m t) -> p m t", m=4)))
                    if g:
                        evac(("ctxkT", g), None, "kTc", g, fn=lambda src: nc.scalar.copy(kT[:, :, 1, :], src.rearrange("p (m t) -> p m t", m=4)))
                    for hh in range(2):
                        acte.wait_ge(c.of("nmax", g, hh), c.at("nmax", g, hh))
                        for j in range(4):
                            for mi in range(2):
                                i = mi * 4 + j
                                ins = ex_(eP[:, hh, i, 0:nk * P], ps[:, 4 + j, mi * nk * P:(mi + 1) * nk * P], DQ ** -0.5, bias=rt[:, 2 * hh, 0, 8 + i:9 + i], accum_out=rt[:, 2 * hh + 1, 0, i:i + 1])
                            if j < 3:
                                ins.then_inc(c.freed(("score", g, hh, j)), 1)
                                acte.wait_ge(S(c.last[0]), c.last_value())
                            else:
                                ins.then_inc(c.freed(("score", g, hh, j), "expd", g, hh), 1)
                                acte.wait_ge(S(c.last[0]), c.last_value())
                    for hh in range(2):
                        for part in range(nk):
                            evac(("wPT", g, hh, part), None, "wT", g, hh, part, fn=lambda src: nc.scalar.copy(wT[:, hh, :, part, :], src.rearrange("p (m t) -> p m t", m=4)))
                    evac(("daoT", g), sq[:, BLK:D], "daoTs", g)
                    square_of(("dao", g), 512, "dao", g)
                    evac(("rqT", g), qw[:, 0], "rqTs", g)
                    evac(("roT", g), None, "roTs", g, fn=lambda src: nc.scalar.copy(sq[:, BLK:BLK + 256], src[:, 0:256]))
                    square_of(("ro", g), 256, "ro", g)
                    if not g:
                        evac(("rstate", g), None, "rstateS", fn=lambda src: nc.scalar.copy(stout[:, 0].rearrange("p h e -> p (h e)"), src[:, 0:256]))
                        for d in range(2):
                            store(ap["o_ret"][0].rearrange("l r h d e -> r d l h e")[d, :, one(l)].rearrange("d l h e -> d (l h) e"), stout[64 * d:64 * d + 64, 0])
                    evac(("hqT", g), qw[:, 0], "hqTs", g)
                    for lv in range(NLV + g):
                        if lv >= 2:
                            acte.wait_ge(c.of("qlv", g, lv - 2), c.at("qlv", g, lv - 2))
                            acte.wait_ge(c.of("klv", g, lv - 2), c.at("klv", g, lv - 2))
                        evac(("level", g, lv), None, "ex", g, lv, fn=lambda src: ex_(ex[:, lv % 2].rearrange("p h t -> p (h t)"), src))
                    if not g:
                        evac(("toend", g), None, "exend", g, fn=lambda src: ex_(t4[:], src))
                    evac(("hoT", g), None, "hoTs", g, fn=lambda src: nc.scalar.copy(sq[:, BLK:BLK + 256], src[:, 0:256]))
                    square_of(("ho", g), 256, "ho", g)
                    if not g:
                        evac(("hstate", g), None, "hstateS", fn=lambda src: nc.scalar.copy(stout[:, 1].rearrange("p h e -> p (h e)"), src[:, 0:256]))
                        for d in range(2):
                            store(ap["o_hg"][0].rearrange("l r h d e -> r d l h e")[d, :, one(l)].rearrange("d l h e -> d (l h) e"), stout[64 * d:64 * d + 64, 1])
                for h in range(2):
                    evac(("mixT", 1, h), None, "mixS", 1, h, fn=lambda src: nc.scalar.copy(hnT[:, 4 * h:4 * h + 4, P:2 * P], src.rearrange("p (k t) -> p k t", k=4)))
                for g in range(NG):
                    for h in range(2):
                        evac(("gateP", 0, g, h), gbuf1[:, g, h * BLK:(h + 1) * BLK], "gateS", 0, g, h)
                squares("xn2")
                shifted("hn2", 1)
                evac(("router",), None, "rexp", fn=lambda src: ex_(rt[:, 0].rearrange("p g e -> p (g e)"), src[:, 0:NG * NE], -1.0))
                acte.wait_ge(c.of("stored"), c.at("stored"))
                for g in range(NG):
                    evac(("rows", g, 0), xs[:, g, 0:BLK], "rowsS", g, 0)
                acte.wait_ge(S("rounds"), l + 2)
                until = count_of_rounds(acte, l + 1)
                with acte.Fori(c.rounds, until) as r:
                    with acte.Fori(0, TURNS) as t:
                        c.t = r * TURNS + t
                        led.where = "turn"
                        for half in range(2):
                            evac(("xT", half), None, "xTs", half, fn=lambda src: nc.scalar.copy(xT[:, KH * half:KH * (half + 1), :], src.rearrange("p (k s) -> p k s", k=KH)))
                        acte.wait_ge(c.of("gu", 0), c.at("gu", 0))
                        st(ex_(ge, ps[:, 2], -1.0), "gexp")
                        evac(("actT",), None, "actTs", fn=lambda src: nc.scalar.copy(actT, src.rearrange("p (k s) -> p k s", k=KE)))
                        evac(("yP", 0), ys[:, 0], "ys", 0)
                c.rounds = until
                led.where = "after"
                for g in range(NG):
                    for h in range(2):
                        evac(("gateP", 1, g, h), gbuf2[:, g, h * BLK:(h + 1) * BLK], "gateS", 1, g, h)
            led.where = "end"
            acte.wait_ge(S("x2"), 1 + NG * L)
            acte.dma_start(ap["o_yp"][0], x[:, 0]).then_inc(S("stored"), 16)
            acte.dma_start(ap["o_ys"][0], x[:, 1]).then_inc(S("stored"), 16)
            acte.wait_ge(S("stored"), 1 + L * led.totals.get(("stored", "layer"), 0) + 32)

        @block.gpsimd
        def _(pool):
            c = Counts(led, S)
            led.where = "start"
            g_ = nc.gpsimd
            bc = lambda a: a.rearrange("(o n) -> o n", o=1).broadcast_to([P, a.shape[0]])
            first = [(condT[:, 0], ap["c_ctx"].rearrange("(p k) -> p k", k=KC)),
                     (condT[:, 1], ap["c"][0].rearrange("(p k) -> p k", k=KC))]
            begin = [(x[:, 0], ap["x_prompt"][0]), (x[:, 1], ap["x_sample"][0])]
            begin += [(C[n][:], io["cap"][n]) for n in ("ident", "pick2")]
            begin += [(lbin[:, l_], bc(ap["hg_lb"][l_])) for l_ in range(L)]
            later = [(C[n][:], io["cap"][n]) for n in io["consts"] if n not in ("ident", "pick2")]
            later += [(wrt[:], ap["w_router"].rearrange("(p k) e -> p k e", k=KC)), (rbias[:], bc(ap["router_bias"]))]
            for name, lot in (("cond_dma", first), ("begin_dma", begin), ("later_dma", later)):
                for dst, src in lot:
                    pool.dma_start(dst, src).then_inc(S(name), 16)
                led.made(name, (name,), 16 * len(lot))
            with pool.Fori(0, L) as l:
                c.l = l
                pool.wait_ge(S("rounds"), l + 1)
                c.rounds = count_of_rounds(pool, l)
                led.where = "layer"
                def scaled_keys(g):
                    for lv in range(NLV):
                        pool.wait_ge(c.of("hkTs", g), c.at("hkTs", g))
                        pool.wait_ge(c.of("ex", g, lv), c.at("ex", g, lv))
                        if lv >= 2:
                            pool.wait_ge(c.of("hS", g, lv - 2, 1), c.at("hS", g, lv - 2, 1))
                        g_.tensor_tensor(klv[:, lv % 2], hkT, ex[:, lv % 2], ALU.mult).then_inc(c.makes("klv", g, lv), 1)
                        pool.wait_ge(S(c.last[0]), c.last_value())

                scaled_keys(0)
                scaled_keys(1)
                led.where = "after"
    return dict(led.count), dict(led.found)


_INS = ["x_prompt", "x_sample", "cache_k", "cache_v", "state_ret", "state_hgrn", "c", "c_ctx", "w_in", "w_out", "w_ada", "b_ada",
        "norm_mix", "norm_ffn", "da_qnorm", "da_knorm", "da_lambda", "da_subln", "ret_decay", "ret_norm", "hg_lb", "hg_norm",
        "w_router", "router_bias", "w_gate", "w_up", "w_down"]
_OUTS = [("o_yp", (1, P, D)), ("o_ys", (1, P, D)), ("o_k", (1, L, P, NH, 2, DQ)), ("o_v", (1, L, P, NH, DV)),
         ("o_ret", (1, L, 2, HR, DR, DR)), ("o_hg", (1, L, 2, HR, DR, DR))]


def kernel(**inputs):
    import concourse.bacc as bacc
    from concourse.bass_utils import run_bass_kernel_spmd

    arrays = {"in_" + n: np.ascontiguousarray(inputs[n]) for n in _INS}
    consts = host_constants()
    arrays.update({"const_" + n: a for n, a in consts.items()})
    known = None
    for _ in range(3):
        nc = bacc.Bacc("TRN2", target_bir_lowering=False, num_devices=1)
        dram = {n: nc.dram_tensor(n, a.shape, mybir.dt.from_np(a.dtype), kind="ExternalInput").ap() for n, a in arrays.items()}
        outs = {n: nc.dram_tensor("out_" + n, shape, mybir.dt.float32, kind="ExternalOutput").ap() for n, shape in _OUTS}
        aps = {n: dram["in_" + n] for n in _INS}
        aps.update(outs)
        io = {"ap": aps, "consts": consts, "cap": {n: dram["const_" + n] for n in consts}}
        known = build(nc, io, known)
    r = run_bass_kernel_spmd(nc, [arrays], core_ids=[0])
    return tuple(r.results[0]["out_" + n] for n, _ in _OUTS)
```
